# Optimizing a Trainium2 kernel written in Bass

```python
import jax, jax.numpy as jnp
from jax import lax
import numpy as np
import math
import jax
import jax.numpy as jnp

D_MODEL = 1024
BATCH = 1
SEQ = 512
DEPTH = 1

HEAD_DIM = 64
ATTN_GROUPS = ((128, 1), (512, 4), (2048, 16))
ATTN_HEADS_PER_GROUP = 4
ATTN_HEADS = ATTN_HEADS_PER_GROUP * len(ATTN_GROUPS)
ATTN_WIDTH = ATTN_HEADS * HEAD_DIM
ATTN_OUT_WIDTH = ATTN_HEADS_PER_GROUP * HEAD_DIM
ATTN_BLOCK = 128
ROPE_THETA = 500000.0
ROPE_DIM = HEAD_DIM // 4
RWKV_HEADS = D_MODEL // HEAD_DIM
RWKV_WIDTH = RWKV_HEADS * HEAD_DIM
DECAY_LORA = 64
ICLR_LORA = 64
GATE_LORA = 128
D_FF = 4 * D_MODEL
NORM_EPS = 1e-6
GN_EPS = 64e-5
NEG_INF = -1e30
SPLITS = (ATTN_WIDTH, ATTN_WIDTH, ATTN_WIDTH,
          RWKV_WIDTH, RWKV_WIDTH, RWKV_WIDTH,
          DECAY_LORA, ICLR_LORA, GATE_LORA,
          D_MODEL, D_MODEL)
ATTN_QKV_WIDTH = 3 * ATTN_WIDTH
SHIFT_WIDTH = 3 * RWKV_WIDTH + DECAY_LORA + ICLR_LORA + GATE_LORA
IN_WIDTH = sum(SPLITS)


def rms_norm(t, gain):
    t32 = t.astype(jnp.float32)
    y = t32 * lax.rsqrt(jnp.mean(t32 * t32, axis=-1, keepdims=True) + NORM_EPS)
    return (y * gain.astype(jnp.float32)).astype(t.dtype)

def partial_rope(t, positions):
    half = ROPE_DIM // 2
    inv = ROPE_THETA ** (-jnp.arange(half, dtype=jnp.float32) * 2.0 / ROPE_DIM)
    ang = positions.astype(jnp.float32)[..., None] * inv
    cos = jnp.cos(ang)[:, :, None, :]
    sin = jnp.sin(ang)[:, :, None, :]
    t32 = t.astype(jnp.float32)
    x1 = t32[..., :half]
    x2 = t32[..., half:ROPE_DIM]
    out = jnp.concatenate([x1 * cos - x2 * sin, x1 * sin + x2 * cos, t32[..., ROPE_DIM:]], axis=-1)
    return out.astype(t.dtype)

def dilated_band_attention(q, k, v, dilation, span):
    B, S, H, Dh = q.shape
    unit = dilation * ATTN_BLOCK
    Sp = -(-S // unit) * unit
    L = Sp // dilation
    nb = L // ATTN_BLOCK

    def to_blocks(t):
        t = jnp.pad(t.astype(jnp.float32), ((0, 0), (0, Sp - S), (0, 0), (0, 0)))
        t = t.reshape(B, L, dilation, H, Dh).transpose(0, 2, 1, 3, 4)
        return t.reshape(B, dilation, nb, ATTN_BLOCK, H, Dh)

    qb, kb, vb = to_blocks(q), to_blocks(k), to_blocks(v)

    def with_prev(t):
        prev = jnp.pad(t[:, :, :-1], ((0, 0), (0, 0), (1, 0), (0, 0), (0, 0), (0, 0)))
        return jnp.concatenate([prev, t], axis=3)

    kw, vw = with_prev(kb), with_prev(vb)
    s = jnp.einsum('bdnqhe,bdnkhe->bdnhqk', qb, kw) * (HEAD_DIM ** -0.5)
    qi = jnp.arange(ATTN_BLOCK)[:, None]
    kj = jnp.arange(2 * ATTN_BLOCK)[None, :]
    lag = qi + ATTN_BLOCK - kj
    band = (lag >= 0) & (lag <= span)
    has_prev = (jnp.arange(nb) > 0)[:, None, None] | (kj >= ATTN_BLOCK)[None]
    mask = band[None] & has_prev
    s = jnp.where(mask[None, None, :, None], s, NEG_INF)
    m = jnp.max(s, axis=-1, keepdims=True)
    p = jnp.exp(s - m)
    l = jnp.sum(p, axis=-1, keepdims=True)
    o = jnp.einsum('bdnhqk,bdnkhe->bdnqhe', p / l, vw)
    lse = jnp.swapaxes((m + jnp.log(l))[..., 0], -1, -2)

    def from_blocks(t):
        t = t.reshape((B, dilation, L) + t.shape[4:])
        t = jnp.swapaxes(t, 1, 2)
        return t.reshape((B, Sp) + t.shape[3:])[:, :S]

    return from_blocks(o), from_blocks(lse)

def dilated_attention_mixer(q, k, v, positions):
    B, S = q.shape[:2]
    q = partial_rope(q, positions)
    k = partial_rope(k, positions)
    outs, lses = [], []
    for g, (window, dilation) in enumerate(ATTN_GROUPS):
        sl = slice(g * ATTN_HEADS_PER_GROUP, (g + 1) * ATTN_HEADS_PER_GROUP)
        o, lse = dilated_band_attention(q[:, :, sl], k[:, :, sl], v[:, :, sl], dilation, window // dilation)
        outs.append(o)
        lses.append(lse)
    o = jnp.stack(outs)
    w = jax.nn.softmax(jnp.stack(lses), axis=0)
    out = jnp.sum(w[..., None] * o, axis=0)
    return out.reshape(B, S, ATTN_OUT_WIDTH).astype(q.dtype)

def token_shift(u, mu):
    prev = jnp.pad(u, ((0, 0), (1, 0), (0, 0)))[:, :-1]
    return u + (prev - u) * mu

def wkv7_scan(r, w, k, v, a, b):
    B, S, H, N = r.shape
    xs = tuple(jnp.moveaxis(t, 1, 0) for t in (r, w, k, v, a, b))

    def step(state, inp):
        r_t, w_t, k_t, v_t, a_t, b_t = inp
        sa = jnp.einsum('bhvk,bhk->bhv', state, a_t)
        state = (state * w_t[:, :, None, :] + sa[..., None] * b_t[:, :, None, :]
                 + v_t[..., None] * k_t[:, :, None, :])
        return state, jnp.einsum('bhvk,bhk->bhv', state, r_t)

    s0 = jnp.zeros((B, H, N, N), jnp.float32)
    _, ys = lax.scan(step, s0, xs)
    return jnp.moveaxis(ys, 0, 1)

def rwkv7_mixer(r, k, v, dw, da, dg, w0, w2, a0, a2, g2, k_k, k_a, r_k, gn_w, gn_b):
    B, S, C = r.shape
    H, N = RWKV_HEADS, HEAD_DIM
    f32 = jnp.float32
    w_log = -jax.nn.softplus(-(w0 + jnp.tanh(dw) @ w2).astype(f32)) - 0.5
    decay = jnp.exp(-jnp.exp(w_log))
    a = jax.nn.sigmoid((a0 + da @ a2).astype(f32))
    g = (jax.nn.sigmoid(dg) @ g2).astype(f32)
    kk = (k * k_k).astype(f32).reshape(B, S, H, N)
    kk = kk / jnp.maximum(jnp.sqrt(jnp.sum(kk * kk, axis=-1, keepdims=True)), 1e-12)
    k = k.astype(f32) * (1.0 + (a - 1.0) * k_a.astype(f32))
    heads = lambda t: t.astype(f32).reshape(B, S, H, N)
    rh, kh, vh, wh, ah = heads(r), heads(k), heads(v), heads(decay), heads(a)
    y = wkv7_scan(rh, wh, kh, vh, -kk, kk * ah)
    mu = jnp.mean(y, axis=-1, keepdims=True)
    var = jnp.mean(jnp.square(y - mu), axis=-1, keepdims=True)
    y = ((y - mu) * lax.rsqrt(var + GN_EPS)).reshape(B, S, C) * gn_w + gn_b
    bonus = jnp.sum(rh * kh * r_k.astype(f32), axis=-1, keepdims=True) * vh
    y = y + bonus.reshape(B, S, C)
    return (y * g).astype(r.dtype)

def first_inputs(seed: int = 0) -> dict:
    key = jax.random.key(seed)
    ks = jax.random.split(key, 32)
    f32 = jnp.float32
    L, D = DEPTH, D_MODEL
    nrm = lambda kk, shape, scale: jax.random.normal(kk, shape, f32) * scale
    x = nrm(ks[0], (BATCH, SEQ, D), 1.0)
    c = nrm(ks[1], (BATCH, D), 1.0)
    offset = jax.random.randint(ks[2], (BATCH, 1), 0, 4096, dtype=jnp.int32)
    positions = offset + jnp.arange(SEQ, dtype=jnp.int32)[None, :]
    return {
        "x": x,
        "c": c,
        "positions": positions,
        "ada_w": nrm(ks[3], (L, D, 6 * D), 0.5 * D ** -0.5),
        "ada_b": nrm(ks[4], (L, 6 * D), 0.02),
        "norm_mix_pre": 1.0 + nrm(ks[5], (L, D), 0.05),
        "norm_mix_post": 1.0 + nrm(ks[6], (L, D), 0.05),
        "norm_ffn_pre": 1.0 + nrm(ks[7], (L, D), 0.05),
        "norm_ffn_post": 1.0 + nrm(ks[8], (L, D), 0.05),
        "w_in": nrm(ks[9], (L, D, IN_WIDTH), D ** -0.5),
        "shift_mu": jax.random.uniform(ks[10], (L, SHIFT_WIDTH), f32),
        "decay_w0": jax.random.uniform(ks[11], (L, RWKV_WIDTH), f32, -6.0, 1.0),
        "decay_w2": nrm(ks[12], (L, DECAY_LORA, RWKV_WIDTH), DECAY_LORA ** -0.5),
        "iclr_a0": nrm(ks[13], (L, RWKV_WIDTH), 0.1),
        "iclr_a2": nrm(ks[14], (L, ICLR_LORA, RWKV_WIDTH), ICLR_LORA ** -0.5),
        "gate_g2": nrm(ks[15], (L, GATE_LORA, RWKV_WIDTH), GATE_LORA ** -0.5),
        "k_k": 0.85 + nrm(ks[16], (L, RWKV_WIDTH), 0.05),
        "k_a": 1.0 + nrm(ks[17], (L, RWKV_WIDTH), 0.05),
        "r_k": nrm(ks[18], (L, RWKV_HEADS, HEAD_DIM), 0.1),
        "gn_w": 1.0 + nrm(ks[19], (L, RWKV_WIDTH), 0.05),
        "gn_b": nrm(ks[20], (L, RWKV_WIDTH), 0.02),
        "w_branch": jnp.concatenate([nrm(ks[21], (L, ATTN_OUT_WIDTH, D), ATTN_OUT_WIDTH ** -0.5),
                                     nrm(ks[22], (L, RWKV_WIDTH, D), RWKV_WIDTH ** -0.5)], axis=1),
        "w_out": nrm(ks[23], (L, D, D), D ** -0.5),
        "w_ff1": nrm(ks[24], (L, D, D_FF), D ** -0.5),
        "w_ff2": nrm(ks[25], (L, D_FF, D), D_FF ** -0.5),
    }

def first_block(x, c, positions, ada_w, ada_b, norm_mix_pre, norm_mix_post, norm_ffn_pre,
              norm_ffn_post, w_in, shift_mu, decay_w0, decay_w2, iclr_a0, iclr_a2, gate_g2,
              k_k, k_a, r_k, gn_w, gn_b, w_branch, w_out, w_ff1, w_ff2):
    B, S, D = x.shape
    for l in range(DEPTH):
        mod = jax.nn.silu(c) @ ada_w[l] + ada_b[l]
        sh1, sc1, gt1, sh2, sc2, gt2 = [m[:, None, :] for m in jnp.split(mod, 6, axis=-1)]

        h = rms_norm(x, norm_mix_pre[l]) * (1.0 + sc1) + sh1
        proj = h @ w_in[l]
        attn_part = proj[..., :ATTN_QKV_WIDTH]
        rwkv_part = token_shift(proj[..., ATTN_QKV_WIDTH:ATTN_QKV_WIDTH + SHIFT_WIDTH], shift_mu[l])
        gate_part = proj[..., ATTN_QKV_WIDTH + SHIFT_WIDTH:]
        q, k, v = [t.reshape(B, S, ATTN_HEADS, HEAD_DIM) for t in jnp.split(attn_part, 3, axis=-1)]
        cuts = np.cumsum([RWKV_WIDTH, RWKV_WIDTH, RWKV_WIDTH, DECAY_LORA, ICLR_LORA])
        r_r, r_k_, r_v, dw, da, dg = jnp.split(rwkv_part, cuts, axis=-1)
        g_attn, g_rwkv = jnp.split(gate_part, 2, axis=-1)

        o_attn = dilated_attention_mixer(q, k, v, positions)
        o_rwkv = rwkv7_mixer(r_r, r_k_, r_v, dw, da, dg, decay_w0[l], decay_w2[l], iclr_a0[l],
                             iclr_a2[l], gate_g2[l], k_k[l], k_a[l], r_k[l], gn_w[l], gn_b[l])
        wb = w_branch[l]
        merged = (jax.nn.sigmoid(g_attn) * (o_attn @ wb[:ATTN_OUT_WIDTH])
                  + jax.nn.sigmoid(g_rwkv) * (o_rwkv @ wb[ATTN_OUT_WIDTH:]))
        mix_out = merged @ w_out[l]
        x = (x + gt1 * rms_norm(mix_out, norm_mix_post[l])).astype(x.dtype)

        h = rms_norm(x, norm_ffn_pre[l]) * (1.0 + sc2) + sh2
        f = jnp.square(jax.nn.relu(h @ w_ff1[l])) @ w_ff2[l]
        x = (x + gt2 * rms_norm(f, norm_ffn_post[l])).astype(x.dtype)
    return x


DEPTH_2 = 2

PLE_DIM = 256
Q_BLOCK = 128
EPS = 1e-6
MLA_HEADS = 8
MLA_Q_RANK = 256
MLA_KV_RANK = 128
MLA_NOPE = 64
MLA_ROPE = 32
MLA_V = 64
ROPE_THETA_2 = 10000.0
DIFF_HEADS = 4
DIFF_QK = 64
DIFF_V = 128
WIN_HEADS = 8
WIN_KV_HEADS = 2
WIN_GROUP = WIN_HEADS // WIN_KV_HEADS
WIN_HEAD_DIM = 64
WINDOW = 128
N_ALIBI = DIFF_HEADS + WIN_HEADS
N_BRANCH = 3
BRANCH_WIDTH = 512
D_FF_2 = 2816
CONV_WIDTH = 3
IN_SPLITS = (MLA_Q_RANK, MLA_KV_RANK, MLA_ROPE,
             2 * DIFF_HEADS * DIFF_QK, 2 * DIFF_HEADS * DIFF_QK, DIFF_HEADS * DIFF_V,
             WIN_HEADS * WIN_HEAD_DIM, WIN_KV_HEADS * WIN_HEAD_DIM, WIN_KV_HEADS * WIN_HEAD_DIM,
             N_BRANCH * D_MODEL)
IN_COLS = sum(IN_SPLITS)


def rms_norm_2(x, g):
    xf = x.astype(jnp.float32)
    y = xf * lax.rsqrt(jnp.mean(xf * xf, axis=-1, keepdims=True) + EPS)
    return (y * g.astype(jnp.float32)).astype(x.dtype)

def rope(x, positions):
    half = x.shape[-1] // 2
    freqs = ROPE_THETA_2 ** (-jnp.arange(half, dtype=jnp.float32) / half)
    ang = positions.astype(jnp.float32)[:, :, None, None] * freqs
    cos, sin = jnp.cos(ang), jnp.sin(ang)
    xf = x.astype(jnp.float32)
    x1, x2 = xf[..., :half], xf[..., half:]
    return jnp.concatenate([x1 * cos - x2 * sin, x2 * cos + x1 * sin], axis=-1).astype(x.dtype)

def alibi_slopes():
    return 2.0 ** (-8.0 * jnp.arange(1, N_ALIBI + 1, dtype=jnp.float32) / N_ALIBI)

def to_blocks(t):
    b, s = t.shape[:2]
    return jnp.moveaxis(t.reshape((b, s // Q_BLOCK, Q_BLOCK) + t.shape[2:]), 1, 0)

def from_blocks(t):
    t = jnp.moveaxis(t, 0, 1)
    return t.reshape((t.shape[0], t.shape[1] * t.shape[2]) + t.shape[3:])

def mla_attention(q, k, v):
    scale = (MLA_NOPE + MLA_ROPE) ** -0.5

    def block(qb):
        s = jnp.einsum('bqhd,bkhd->bhqk', qb, k, preferred_element_type=jnp.float32) * scale
        p = jax.nn.softmax(s, axis=-1).astype(v.dtype)
        return jnp.einsum('bhqk,bkhd->bqhd', p, v)

    return from_blocks(lax.map(block, to_blocks(q)))

def diff_attention(q, k, v, positions, lam, slopes):
    scale = DIFF_QK ** -0.5
    pos_f = positions.astype(jnp.float32)

    def block(args):
        qb, pb = args
        s = jnp.einsum('bqmhd,bkmhd->bmhqk', qb, k, preferred_element_type=jnp.float32) * scale
        dist = jnp.abs(pb[:, :, None] - pos_f[:, None, :])
        s = s - slopes[None, None, :, None, None] * dist[:, None, None]
        p = jax.nn.softmax(s, axis=-1)
        a = p[:, 0] - lam * p[:, 1]
        return jnp.einsum('bhqk,bkhd->bqhd', a.astype(v.dtype), v)

    return from_blocks(lax.map(block, (to_blocks(q), to_blocks(pos_f))))

def window_attention(q, k, v, positions, sink, slopes):
    b, s_len = q.shape[:2]
    nb = s_len // Q_BLOCK
    span = Q_BLOCK + 2 * WINDOW
    scale = WIN_HEAD_DIM ** -0.5
    pad = ((0, 0), (WINDOW, WINDOW), (0, 0), (0, 0))
    kp, vp = jnp.pad(k, pad), jnp.pad(v, pad)
    pos_f = positions.astype(jnp.float32)
    posp = jnp.pad(pos_f, ((0, 0), (WINDOW, WINDOW)))
    q_local = jnp.arange(Q_BLOCK)
    k_local = jnp.arange(span)
    band = jnp.abs(k_local[None, :] - WINDOW - q_local[:, None]) <= WINDOW
    qg = q.reshape(b, s_len, WIN_KV_HEADS, WIN_GROUP, WIN_HEAD_DIM)
    slope_hg = slopes.reshape(WIN_KV_HEADS, WIN_GROUP)[None, :, :, None, None]
    sink_hg = sink.astype(jnp.float32).reshape(WIN_KV_HEADS, WIN_GROUP)[None, :, :, None, None]

    def block(args):
        n, qb, pb = args
        start = n * Q_BLOCK
        kb = lax.dynamic_slice_in_dim(kp, start, span, axis=1)
        vb = lax.dynamic_slice_in_dim(vp, start, span, axis=1)
        pk = lax.dynamic_slice_in_dim(posp, start, span, axis=1)
        key_idx = start - WINDOW + k_local
        valid = band & ((key_idx >= 0) & (key_idx < s_len))[None, :]
        s = jnp.einsum('bqhgd,bkhd->bhgqk', qb, kb, preferred_element_type=jnp.float32) * scale
        dist = jnp.abs(pb[:, :, None] - pk[:, None, :])
        s = s - slope_hg * dist[:, None, None]
        s = jnp.where(valid, s, -jnp.inf)
        m = jnp.maximum(jnp.max(s, axis=-1, keepdims=True), sink_hg)
        e = jnp.exp(s - m)
        p = e / (jnp.sum(e, axis=-1, keepdims=True) + jnp.exp(sink_hg - m))
        return jnp.einsum('bhgqk,bkhd->bqhgd', p.astype(v.dtype), vb)

    out = from_blocks(lax.map(block, (jnp.arange(nb), to_blocks(qg), to_blocks(pos_f))))
    return out.reshape(b, s_len, WIN_HEADS * WIN_HEAD_DIM)

def depthwise_conv(a, w, bias):
    out = lax.conv_general_dilated(
        a, w[:, None, :].astype(a.dtype), window_strides=(1,),
        padding=((CONV_WIDTH // 2, CONV_WIDTH // 2),),
        dimension_numbers=('NWC', 'WIO', 'NWC'), feature_group_count=a.shape[-1])
    return out + bias.astype(a.dtype)

def hybrid_layer(x, pe, positions, layer_idx, g_mix, w_in, g_q_lora, w_uq, g_kv_lora, w_ukv,
                 g_mla_q, g_mla_k, g_diff_q, g_diff_k, lam_q1, lam_k1, lam_q2, lam_k2, g_diff_out,
                 g_win_q, g_win_k, win_sink, w_branch, w_out, g_ffn, w_ffn_gate, w_ffn_up,
                 conv_w, conv_b, w_ffn_down, w_ple_proj, g_ple, g_ple_in, w_ple_gate):
    b, s, _ = x.shape
    slopes = alibi_slopes()
    h = rms_norm_2(x, g_mix)
    proj = h @ w_in
    offs = np.cumsum(IN_SPLITS)[:-1].tolist()
    c_q, c_kv, k_r, d_q, d_k, d_v, s_q, s_k, s_v, gate_logits = jnp.split(proj, offs, axis=-1)

    q = (rms_norm_2(c_q, g_q_lora) @ w_uq).reshape(b, s, MLA_HEADS, MLA_NOPE + MLA_ROPE)
    kv = (rms_norm_2(c_kv, g_kv_lora) @ w_ukv).reshape(b, s, MLA_HEADS, MLA_NOPE + MLA_V)
    k_nope, v_mla = kv[..., :MLA_NOPE], kv[..., MLA_NOPE:]
    k_rope = jnp.broadcast_to(k_r[:, :, None, :], (b, s, MLA_HEADS, MLA_ROPE))
    k = rms_norm_2(jnp.concatenate([k_nope, k_rope], axis=-1), g_mla_k)
    q = rms_norm_2(q, g_mla_q)
    q = jnp.concatenate([q[..., :MLA_NOPE], rope(q[..., MLA_NOPE:], positions)], axis=-1)
    k = jnp.concatenate([k[..., :MLA_NOPE], rope(k[..., MLA_NOPE:], positions)], axis=-1)
    o_mla = mla_attention(q, k, v_mla).reshape(b, s, BRANCH_WIDTH)

    dq = rms_norm_2(d_q.reshape(b, s, 2, DIFF_HEADS, DIFF_QK), g_diff_q)
    dk = rms_norm_2(d_k.reshape(b, s, 2, DIFF_HEADS, DIFF_QK), g_diff_k)
    dv = d_v.reshape(b, s, DIFF_HEADS, DIFF_V)
    lam_init = 0.8 - 0.6 * math.exp(-0.3 * layer_idx)
    lam = (jnp.exp(jnp.sum(lam_q1.astype(jnp.float32) * lam_k1.astype(jnp.float32)))
           - jnp.exp(jnp.sum(lam_q2.astype(jnp.float32) * lam_k2.astype(jnp.float32))) + lam_init)
    od = diff_attention(dq, dk, dv, positions, lam, slopes[WIN_HEADS:])
    o_diff = (rms_norm_2(od, g_diff_out) * (1.0 - lam_init)).reshape(b, s, BRANCH_WIDTH)

    wq = rms_norm_2(s_q.reshape(b, s, WIN_HEADS, WIN_HEAD_DIM), g_win_q)
    wk = rms_norm_2(s_k.reshape(b, s, WIN_KV_HEADS, WIN_HEAD_DIM), g_win_k)
    wv = s_v.reshape(b, s, WIN_KV_HEADS, WIN_HEAD_DIM)
    o_win = window_attention(wq, wk, wv, positions, win_sink, slopes[:WIN_HEADS])

    gates = jax.nn.sigmoid(gate_logits.reshape(b, s, N_BRANCH, D_MODEL))
    merged = (gates[:, :, 0] * (o_mla @ w_branch[0])
              + gates[:, :, 1] * (o_diff @ w_branch[1])
              + gates[:, :, 2] * (o_win @ w_branch[2]))
    x = x + merged @ w_out

    h = rms_norm_2(x, g_ffn)
    a = depthwise_conv(h @ w_ffn_gate, conv_w, conv_b)
    x = x + (jax.nn.gelu(a) * (h @ w_ffn_up)) @ w_ffn_down

    e = rms_norm_2(pe @ w_ple_proj, g_ple)
    g = jax.nn.sigmoid(rms_norm_2(x, g_ple_in) @ w_ple_gate)
    return x + g * e

def second_inputs(seed: int = 0) -> dict:
    key = jax.random.key(seed)
    ks = iter(jax.random.split(key, 40))

    def dense(shape, fan_in):
        return jax.random.normal(next(ks), shape, jnp.float32) * fan_in ** -0.5

    def gain(n):
        return 1.0 + 0.05 * jax.random.normal(next(ks), (DEPTH_2, n), jnp.float32)

    def small(shape, scale):
        return scale * jax.random.normal(next(ks), shape, jnp.float32)

    x = jax.random.normal(next(ks), (BATCH, SEQ, D_MODEL), jnp.float32)
    p = jax.random.normal(next(ks), (DEPTH_2, BATCH, SEQ, PLE_DIM), jnp.float32)
    offset = jax.random.randint(next(ks), (BATCH, 1), 0, 1024, dtype=jnp.int32)
    positions = offset + jnp.arange(SEQ, dtype=jnp.int32)[None, :]
    return {
        'x': x,
        'p': p,
        'positions': positions,
        'g_mix': gain(D_MODEL),
        'w_in': dense((DEPTH_2, D_MODEL, IN_COLS), D_MODEL),
        'g_q_lora': gain(MLA_Q_RANK),
        'w_uq': dense((DEPTH_2, MLA_Q_RANK, MLA_HEADS * (MLA_NOPE + MLA_ROPE)), MLA_Q_RANK),
        'g_kv_lora': gain(MLA_KV_RANK),
        'w_ukv': dense((DEPTH_2, MLA_KV_RANK, MLA_HEADS * (MLA_NOPE + MLA_V)), MLA_KV_RANK),
        'g_mla_q': gain(MLA_NOPE + MLA_ROPE),
        'g_mla_k': gain(MLA_NOPE + MLA_ROPE),
        'g_diff_q': gain(DIFF_QK),
        'g_diff_k': gain(DIFF_QK),
        'lam_q1': small((DEPTH_2, DIFF_QK), 0.1),
        'lam_k1': small((DEPTH_2, DIFF_QK), 0.1),
        'lam_q2': small((DEPTH_2, DIFF_QK), 0.1),
        'lam_k2': small((DEPTH_2, DIFF_QK), 0.1),
        'g_diff_out': gain(DIFF_V),
        'g_win_q': gain(WIN_HEAD_DIM),
        'g_win_k': gain(WIN_HEAD_DIM),
        'win_sink': small((DEPTH_2, WIN_HEADS), 1.0),
        'w_branch': dense((DEPTH_2, N_BRANCH, BRANCH_WIDTH, D_MODEL), BRANCH_WIDTH),
        'w_out': dense((DEPTH_2, D_MODEL, D_MODEL), D_MODEL),
        'g_ffn': gain(D_MODEL),
        'w_ffn_gate': dense((DEPTH_2, D_MODEL, D_FF_2), D_MODEL),
        'w_ffn_up': dense((DEPTH_2, D_MODEL, D_FF_2), D_MODEL),
        'conv_w': dense((DEPTH_2, CONV_WIDTH, D_FF_2), CONV_WIDTH),
        'conv_b': small((DEPTH_2, D_FF_2), 0.02),
        'w_ffn_down': dense((DEPTH_2, D_FF_2, D_MODEL), D_FF_2),
        'w_ple_proj': dense((DEPTH_2, PLE_DIM, D_MODEL), PLE_DIM),
        'g_ple': gain(D_MODEL),
        'g_ple_in': gain(D_MODEL),
        'w_ple_gate': dense((DEPTH_2, D_MODEL, D_MODEL), D_MODEL),
    }

def second_block(x, p, positions, g_mix, w_in, g_q_lora, w_uq, g_kv_lora, w_ukv, g_mla_q, g_mla_k,
              g_diff_q, g_diff_k, lam_q1, lam_k1, lam_q2, lam_k2, g_diff_out, g_win_q, g_win_k,
              win_sink, w_branch, w_out, g_ffn, w_ffn_gate, w_ffn_up, conv_w, conv_b, w_ffn_down,
              w_ple_proj, g_ple, g_ple_in, w_ple_gate):
    for i in range(DEPTH_2):
        x = hybrid_layer(
            x, p[i], positions, i, g_mix[i], w_in[i], g_q_lora[i], w_uq[i], g_kv_lora[i], w_ukv[i],
            g_mla_q[i], g_mla_k[i], g_diff_q[i], g_diff_k[i], lam_q1[i], lam_k1[i], lam_q2[i],
            lam_k2[i], g_diff_out[i], g_win_q[i], g_win_k[i], win_sink[i], w_branch[i], w_out[i],
            g_ffn[i], w_ffn_gate[i], w_ffn_up[i], conv_w[i], conv_b[i], w_ffn_down[i],
            w_ple_proj[i], g_ple[i], g_ple_in[i], w_ple_gate[i])
    return x


def setup_inputs(seed=0):
    out = dict(first_inputs(seed))
    for name, value in second_inputs(seed + 1).items():
        if name != "x":
            out[name + "_2"] = value
    return out


def reference(
    x, c, positions, ada_w, ada_b, norm_mix_pre, norm_mix_post, norm_ffn_pre, norm_ffn_post,
    w_in, shift_mu, decay_w0, decay_w2, iclr_a0, iclr_a2, gate_g2, k_k, k_a, r_k, gn_w, gn_b,
    w_branch, w_out, w_ff1, w_ff2, p_2, positions_2, g_mix_2, w_in_2, g_q_lora_2, w_uq_2,
    g_kv_lora_2, w_ukv_2, g_mla_q_2, g_mla_k_2, g_diff_q_2, g_diff_k_2, lam_q1_2, lam_k1_2,
    lam_q2_2, lam_k2_2, g_diff_out_2, g_win_q_2, g_win_k_2, win_sink_2, w_branch_2, w_out_2,
    g_ffn_2, w_ffn_gate_2, w_ffn_up_2, conv_w_2, conv_b_2, w_ffn_down_2, w_ple_proj_2, g_ple_2,
    g_ple_in_2, w_ple_gate_2,
):
    x = first_block(
        x, c, positions, ada_w, ada_b, norm_mix_pre, norm_mix_post, norm_ffn_pre, norm_ffn_post,
        w_in, shift_mu, decay_w0, decay_w2, iclr_a0, iclr_a2, gate_g2, k_k, k_a, r_k, gn_w,
        gn_b, w_branch, w_out, w_ff1, w_ff2,
    )
    return second_block(
        x, p_2, positions_2, g_mix_2, w_in_2, g_q_lora_2, w_uq_2, g_kv_lora_2, w_ukv_2,
        g_mla_q_2, g_mla_k_2, g_diff_q_2, g_diff_k_2, lam_q1_2, lam_k1_2, lam_q2_2, lam_k2_2,
        g_diff_out_2, g_win_q_2, g_win_k_2, win_sink_2, w_branch_2, w_out_2, g_ffn_2,
        w_ffn_gate_2, w_ffn_up_2, conv_w_2, conv_b_2, w_ffn_down_2, w_ple_proj_2, g_ple_2,
        g_ple_in_2, w_ple_gate_2,
    )


_drawn_inputs = setup_inputs


def setup_inputs(seed=0):
    import zlib

    import numpy as np

    out = dict(_drawn_inputs(seed))
    spreads = {}
    factors = {'norm_ffn_pre': 3.283,
     'iclr_a0': 5.085,
     'gn_w': 3.936,
     'gn_b': 5.45,
     'g_q_lora_2': 8.0,
     'g_kv_lora_2': 6.906,
     'g_mla_q_2': 8.0,
     'g_mla_k_2': 8.0,
     'g_diff_q_2': 4.142,
     'g_diff_k_2': 4.327,
     'lam_q1_2': 3.19,
     'lam_q2_2': 8.0,
     'lam_k2_2': 4.911,
     'g_win_q_2': 8.0,
     'g_win_k_2': 8.0,
     'conv_b_2': 4.649,
     'g_ple_in_2': 5.987}
    for name, (base, spread) in spreads.items():
        noise = np.random.default_rng([zlib.crc32(name.encode()), seed]).standard_normal(out[name].shape)
        drawn = base * np.exp(spread * noise) if base else spread * noise
        out[name] = jnp.asarray(drawn.astype(out[name].dtype))
    for name, factor in factors.items():
        out[name] = (out[name] * factor).astype(out[name].dtype)
    return out
```

```python
from contextlib import ExitStack

import numpy as np

import concourse.bass as bass
from concourse import mybir

F32 = mybir.dt.float32
F32R = mybir.dt.float32r
I32 = mybir.dt.int32
ALU = mybir.AluOpType
ACT = mybir.ActivationFunctionType
AX = mybir.AxisListType.X

P = 128
T = 512
NQ = T // P
D = 1024
KD = D // P
TILES = 8
RAW = 2
SPLIT = 2
BANKS = 4
ARENA = 45

AH, HD = 12, 64
AW = AH * HD
GH = 4
FF1 = 4096
LORA = 64
EPS = 1e-6
GN_EPS = 64e-5
DECAY = float(np.exp(-0.5))
LAYERS = 2
MH, NOPE, ROPE, MV = 8, 64, 32, 64
MQ = NOPE + ROPE
QR, KVR = 256, 128
DH, DV = 4, 128
WH, WKV = 8, 2
BW = 512
FF2 = 2816
PLE = 256
NEG = -1e30
SLOPES = [2.0 ** (-8.0 * (n + 1) / (DH + WH)) for n in range(DH + WH)]
LAM0 = [0.8 - 0.6 * float(np.exp(-0.3 * n)) for n in range(LAYERS)]


def tile_of(name, layer, row, col, rows=P, cols=P, at_row=0, at_col=0):
    return (name, layer, row, rows, col, cols, at_row, at_col)


def weight_plan():
    plan = []

    def mat(tag, name, layer, col, k=KD, row=0):
        for t in range(k):
            plan.append((tag, [tile_of(name, layer, row + t * P, col)]))

    def pad():
        while len(plan) % TILES:
            plan.append(("pad", []))

    for n in range(2 * KD):
        mat("ada", "ada_w", 0, n * P)
    for n in range(2 * AW // P):
        mat("qk", "w_in", 0, n * P)
    for t in range(KD):
        for n in range(4):
            plan.append(("v4", [tile_of("w_in", 0, t * P, 2 * AW + n * P)]))
    for t in range(KD):
        for n in range(4, 6):
            plan.append(("v2", [tile_of("w_in", 0, t * P, 2 * AW + n * P)]))
    for n in range(2 * KD, 6 * KD):
        mat("ada", "ada_w", 0, n * P)
    r0 = 3 * AW
    mat("lora", "w_in", 0, r0 + 3 * D)
    mat("lora", "w_in", 0, r0 + 3 * D + P)
    for j in range(KD):
        for part in range(3):
            mat("rkv", "w_in", 0, r0 + part * D + j * P)
        plan.append(("w2", [tile_of("decay_w2", 0, 0, j * P, rows=LORA)]))
        plan.append(("a2", [tile_of("iclr_a2", 0, 0, j * P, rows=LORA, at_row=LORA)]))
        plan.append(("g2", [tile_of("gate_g2", 0, 0, j * P)]))
    g0 = r0 + 3 * D + 2 * P
    for n in range(KD):
        mat("gate", "w_in", 0, g0 + n * P)
        mat("gate", "w_in", 0, g0 + D + n * P)
        mat("branch", "w_branch", 0, n * P, k=2)
        mat("branch", "w_branch", 0, n * P, row=2 * P)
    for n in range(KD):
        mat("out", "w_out", 0, n * P)
    G1 = 4

    def up1(g):
        for n in range(G1):
            mat("up1", "w_ff1", 0, (g * G1 + n) * P)

    def down1(g):
        for n in range(KD):
            mat("down1", "w_ff2", 0, n * P, k=G1, row=g * G1 * P)

    up1(0)
    for g in range(FF1 // P // G1 - 1):
        up1(g + 1)
        down1(g)
    down1(FF1 // P // G1 - 1)

    for l in range(LAYERS):
        assert len(plan) % TILES == 0
        for n in range(3):
            mat("c", "w_in_2", l, n * P)
        for t in range(KD):
            plan.append(("kr", [tile_of("w_in_2", l, t * P, QR + KVR, cols=ROPE, at_col=NOPE)]))
        for half in range(2):
            for h in range(4 * half, 4 * half + 4):
                for t in range(2):
                    plan.append(("uq", [tile_of("w_uq_2", l, t * P, h * MQ, cols=MQ)]))
                plan.append(("uk", [tile_of("w_ukv_2", l, 0, h * P, cols=NOPE)]))
            for hp in range(2 * half, 2 * half + 2):
                plan.append(("uv", [tile_of("w_ukv_2", l, 0, (2 * hp + i) * P + NOPE, cols=MV, at_col=i * MV)
                                    for i in range(2)]))
            pad() if half else None
        c0 = QR + KVR + ROPE
        gates = c0 + 3 * 512 + 512 + 256

        def branch(b):
            for n in range(KD):
                for t in range(BW // P):
                    plan.append(("branch2", [("w_branch_2", (l, b), t * P, P, n * P, P, 0, 0)]))
                mat("gate2", "w_in_2", l, gates + b * D + n * P)

        branch(0)
        for n in range(8):
            mat("dqk", "w_in_2", l, c0 + n * P)
        for t in range(KD):
            for n in range(4):
                plan.append(("dv", [tile_of("w_in_2", l, t * P, c0 + 1024 + n * P)]))
        branch(1)
        for n in range(4):
            mat("sqk", "w_in_2", l, c0 + 1536 + n * P)
        for kv in range(WKV):
            for t in range(KD):
                plan.append(("sqk", [tile_of("w_in_2", l, t * P, c0 + 2048 + kv * HD, cols=HD, at_col=i * HD)
                                     for i in range(2)]))
        mat("sv", "w_in_2", l, c0 + 1536 + 640)
        branch(2)
        for n in range(KD):
            mat("out2", "w_out_2", l, n * P)

        def up2(g):
            for n in range(2):
                mat("gate_up", "w_ffn_gate_2", l, (2 * g + n) * P)
                mat("gate_up", "w_ffn_up_2", l, (2 * g + n) * P)

        def down2(g):
            for n in range(KD):
                mat("down2", "w_ffn_down_2", l, n * P, k=2, row=2 * g * P)

        up2(0)
        for g in range(FF2 // P // 2 - 1):
            up2(g + 1)
            down2(g)
        down2(FF2 // P // 2 - 1)
        for n in range(KD):
            mat("ple", "w_ple_proj_2", l, n * P, k=2)
        for n in range(KD):
            mat("pgate", "w_ple_gate_2", l, n * P)
    while len(plan) % (RAW * TILES):
        plan.append(("pad", []))
    return plan


def param_columns():
    at, n = {}, 0
    for name, cols in [("c", 8), ("ada_b", 48), ("norm_mix_pre", 8), ("norm_mix_post", 8), ("norm_ffn_pre", 8),
                       ("norm_ffn_post", 8), ("shift_mu", 26), ("decay_w0", 8), ("iclr_a0", 8), ("k_k", 8),
                       ("k_a", 8), ("r_k", 8), ("gn_w", 8), ("gn_b", 8)]:
        at[name] = n
        n += cols
    for name, cols in [("g_mix_2", 8), ("g_q_lora_2", 2), ("g_kv_lora_2", 1), ("g_mla_q_2", 1), ("g_mla_k_2", 1),
                       ("g_diff_q_2", 1), ("g_diff_k_2", 1), ("lam_q1_2", 1), ("lam_k1_2", 1), ("lam_q2_2", 1),
                       ("lam_k2_2", 1), ("g_diff_out_2", 1), ("g_win_q_2", 1), ("g_win_k_2", 1), ("win_sink_2", 8),
                       ("g_ffn_2", 8), ("conv_w_2", 66), ("conv_b_2", 22), ("g_ple_2", 8), ("g_ple_in_2", 8)]:
        for l in range(LAYERS):
            at[name, l] = n
            n += cols
    return at, n


C_IDENT, C_ONES, C_PAIR, C_MASK4, C_LOW1, C_LOW1T, C_LEVEL = 0, 128, 256, 384, 896, 1024, 1152
C_PERM1, C_PERM2 = 1152 + 6 * 128, 1152 + 7 * 128
C_INV = 1152 + 8 * 128
C_END = C_INV + 8
M_NEAR, M_MOD4, M_MOD16, M_BAND, M_END = 0, 256, 768, 1280, 1664


def constants():
    c = np.zeros((P, C_END), np.float32)
    i = np.arange(P)
    row, col = i[:, None], i[None, :]
    c[:, C_IDENT:C_IDENT + P] = row == col
    c[:, C_ONES:C_ONES + P] = 1.0
    c[:, C_PAIR:C_PAIR + P] = row // HD == col // HD
    c[:, C_MASK4:C_MASK4 + 512] = np.concatenate([col > row, col >= row] * 2, 1)
    low1 = (row // 2 == col // 2) & (row > col)
    c[:, C_LOW1:C_LOW1 + P] = low1
    c[:, C_LOW1T:C_LOW1T + P] = low1.T
    for k in range(1, 7):
        h = 1 << k
        m = (row // (2 * h) == col // (2 * h)) & (row // h % 2 == 1) & (col // h % 2 == 0)
        c[:, C_LEVEL + (k - 1) * P:C_LEVEL + k * P] = m
    for m in range(P):
        if m % HD < 8:
            c[m + 8, C_PERM1 + m] = -1.0
        elif m % HD < 16:
            c[m - 8, C_PERM1 + m] = 1.0
        if 64 <= m < 80:
            c[m + 16, C_PERM2 + m] = -1.0
        elif 80 <= m < 96:
            c[m - 16, C_PERM2 + m] = 1.0
    f1 = 500000.0 ** (-np.arange(8) * 2.0 / 16)
    f2 = 10000.0 ** (-np.arange(16) / 16.0)
    for m in range(P):
        if m % HD < 16:
            c[m, C_INV] = f1[m % 8]
        if 64 <= m < 96:
            c[m, C_INV + 1] = f2[m % 16]
    c[:, C_INV + 2] = EPS
    c[:, C_INV + 3] = GN_EPS
    m = np.zeros((P, M_END), np.float32)
    off = lambda keep: np.where(keep, 0.0, NEG).astype(np.float32)
    m[:, M_NEAR:M_NEAR + 256] = np.concatenate([off(col >= row), off(col <= row)], 1)
    for at, d in ((M_MOD4, 4), (M_MOD16, 16)):
        same = (row - col) % d == 0
        m[:, at:at + 512] = np.concatenate([off(same)] * 3 + [off(same & (col <= row))], 1)
    m[:, M_BAND:M_END] = np.concatenate([off(col >= row), off(row + col >= 0), off(col <= row)], 1)
    return c, m


class Signals:

    def __init__(self, nc, ctx):
        self.nc, self.ctx, self.of = nc, ctx, {}

    def __getitem__(self, name):
        if name not in self.of:
            self.of[name] = self.ctx.enter_context(self.nc.semaphore(name))
        return self.of[name]


class Counts:

    def __init__(self, eng, sem, step):
        self.eng, self.sem, self.last = eng, sem, step
        self.raised, self.seen = {}, {}
        self.turn = None

    def value(self, name, count):
        per = self.turn[1].get(name, 0) if self.turn else 0
        return count + self.turn[0] * per if per else count

    def up(self, name):
        self.raised[name] = self.raised.get(name, 0) + 1
        self.last = name
        return 1

    def own(self):
        return self.value(self.last, self.raised[self.last])

    def due(self, name, n=1):
        self.seen[name] = self.seen.get(name, 0) + n
        return self.value(name, self.seen[name])

    def loop(self, n, **per):
        return Turns(self, n, per)


class Turns:

    def __init__(self, counts, n, per):
        self.counts, self.n, self.per = counts, n, per

    def __enter__(self):
        self.fori = self.counts.eng.Fori(0, self.n)
        self.counts.turn = (self.fori.__enter__(), self.per)
        self.start = (dict(self.counts.raised), dict(self.counts.seen))

    def __exit__(self, *exc):
        self.fori.__exit__(*exc)
        self.counts.turn = None
        if exc[0]:
            return
        for now, was in zip((self.counts.raised, self.counts.seen), self.start):
            for name in now:
                d = now[name] - was.get(name, 0)
                assert d == self.per.get(name, 0), (name, d)
                now[name] += (self.n - 1) * d


def heads_of_first_block(i, h):
    return [(h, max(i - 1, 0), M_NEAR + 256 - (min(i, 1) + 1) * P),
            (GH + h, 0, M_MOD4 + (3 - i) * P),
            (2 * GH + h, 0, M_MOD16 + (3 - i) * P)]


class Buffers:

    def __init__(self, nc, ctx, ncols, cols):
        def sb(name, shape, dt=F32):
            return ctx.enter_context(nc.sbuf_tensor(name, shape, dt))

        self.cols = cols
        self.raw = sb("raw", [P, RAW, TILES * P])
        self.w_hi = sb("w_hi", [P, SPLIT, TILES * P], F32R)
        self.w_lo = sb("w_lo", [P, SPLIT, TILES * P], F32R)
        self.x = sb("x", [P, KD, T])
        self.h_hi, self.h_lo = sb("h_hi", [P, KD, T], F32R), sb("h_lo", [P, KD, T], F32R)
        self.o_hi, self.o_lo = sb("o_hi", [P, KD, T], F32R), sb("o_lo", [P, KD, T], F32R)
        self.s_hi, self.s_lo = sb("s_hi", [P, 4, T], F32R), sb("s_lo", [P, 4, T], F32R)
        self.c_pair = sb("c_pair", [P, KD, 2], F32R)
        self.const = sb("const", [P, C_END])
        self.par = sb("par", [P, ncols])
        self.mark = sb("mark", [P, 2])
        self.mod = sb("mod", [P, 6 * KD])
        self.col = sb("col", [P, 192])
        self.posi = sb("posi", [P, NQ], I32)
        self.arena = sb("arena", [P, ARENA * T])
        self.posrow_i = self.arena[:, 44 * T:45 * T].bitcast(I32)
        self.psum = {"a": ctx.enter_context(nc.psum_tensor("psum_a", [P, BANKS, T], F32)),
                     "d": ctx.enter_context(nc.psum_tensor("psum_d", [P, BANKS, T], F32))}
        c = self.const
        self.ident, self.ones = c[:, C_IDENT:C_IDENT + P], c[:, C_ONES:C_ONES + P]
        self.pair = c[:, C_PAIR:C_PAIR + P]
        self.eps, self.gn_eps = c[:, C_INV + 2:C_INV + 3], c[:, C_INV + 3:C_INV + 4]
        ar, art = self.ar, self.art
        self.A_Q, self.A_K = art(0, 6), art(6, 6)
        self.A_V = ar(12, 6).rearrange("p (q n) -> p q n", q=NQ)
        self.A_O = ar(18, 2)[:, 0:NQ * 256].rearrange("p (q n) -> p q n", q=NQ)
        self.A_S, self.A_E, self.A_P = (ar(a, 5).rearrange("p (s n) -> p s n", s=2) for a in (20, 25, 30))
        self.MASKS = ar(35, width=M_BAND)
        self.A_C, self.A_SN, self.A_T = ar(38), ar(39), art(40, 4)
        self.N0 = Norm(self, 18)
        self.R_U = ar(0, width=2 * 513).rearrange("p (s n) -> p s n", s=2)
        self.R_PB = self.arena[:, 1028:1028 + 4 * 129].rearrange("p (c n) -> p c n", c=NQ)
        (self.R_R, self.R_K, self.R_V, self.R_T, self.R_SW, self.R_AA, self.R_CUM, self.R_KK) = (
            ar(4 + n) for n in range(8))
        self.R_AR = ar(12, 2).rearrange("p (c a t) -> p c a t", c=NQ, a=2)
        self.R_BH, self.R_KP, self.R_KH, self.R_BV = (ar(14 + n) for n in range(4))
        self.R_VN, self.R_BN, self.R_KN = (ar(18 + n).rearrange("p (c n) -> p c n", c=NQ) for n in range(3))
        self.R_LM = ar(21, 8).rearrange("p (u m t) -> p u m t", u=8, m=4)
        self.R_Z, self.R_TN, self.R_TT = (ar(a, 2).rearrange("p (u t) -> p u t", u=8) for a in (29, 31, 33))
        self.R_WU = ar(35, width=1024).rearrange("p (s n) -> p s n", s=8)
        self.R_Y, self.R_YC, self.R_O, self.R_G = ar(37), ar(38), ar(39), ar(40)
        self.G_SG, self.G_M = art(0, 4), art(4, 8)
        self.Y8, self.N1 = art(12, 8), Norm(self, 20)
        self.F_R, self.F_T = art(29, 4), ar(33)

        self.L_M, self.L_Q, self.L_K = art(0, 8), art(8, 4), art(12, 4)
        self.L_V, self.L_O = (ar(a, 4).rearrange("p (q n) -> p q n", q=NQ) for a in (16, 20))
        self.L_C, self.L_S, self.L_E, self.L_P = art(8, 3), art(24, 2), art(26, 4), art(30, 2)
        self.L_SG = art(24, 2)
        self.NH = Norm(self, 24)
        self.L_D = ar(32, 4).rearrange("p (q n) -> p q n", q=NQ)
        self.L_DW = ar(36, 3).rearrange("p (q n) -> p q n", q=NQ)
        self.L_COS, self.L_SIN, self.L_KR, self.L_PE, self.L_POS = ar(39), ar(40), ar(41), art(42, 2), ar(44)
        self.F_G = ar(0, width=2 * 514).rearrange("p (s n) -> p s n", s=2)
        self.F_SG = art(8, 2)
        self.L_DW_TMP = art(32, 4)
        self.F_U, self.F_C, self.F_A, self.F_F = art(3, 2), ar(5), ar(6), ar(7)

    def ar(self, at, n=1, width=None):
        w = width if width is not None else n * T
        return self.arena[:, at * T:at * T + w]

    def art(self, at, n):
        return self.ar(at, n).rearrange("p (n t) -> p n t", n=n)

    def pc(self, name, k=0, l=None):
        at = (self.cols[name] if l is None else self.cols[name, l]) + k
        return self.par[:, at:at + 1]

    def pcs(self, name, n, l=None):
        at = self.cols[name] if l is None else self.cols[name, l]
        return self.par[:, at:at + n]


class Norm:

    def __init__(self, b, base):
        self.sq, self.acc = b.art(base, 2), b.ar(base + 2)
        self.std, self.inv = b.ar(base + 3), b.ar(base + 4)
        self.tmp = b.art(base + 5, 4)


class Tile:

    def __init__(self, ring, n, ps, full, free):
        self.ring, self.n, self.ps, self.full, self.free = ring, n, ps, full, free


class Pe(Counts):

    def __init__(self, eng, sem, b, plan):
        super().__init__(eng, sem, "pe_step")
        self.b, self.plan, self.at, self.old_block = b, plan, 0, False
        self.opened = {"a": 0, "d": 0}

    def tile(self, ring):
        n = self.opened[ring]
        self.opened[ring] += 1
        return Tile(ring, n, self.b.psum[ring][:, n % BANKS], self.sem["full_" + ring], self.sem["free_" + ring])

    def emptied(self, tile):
        return self.value("full_" + tile.ring, tile.n + 1)

    def taken(self, tile):
        return self.value("full_" + tile.ring, tile.n + 1 + BANKS)

    def new_block(self):
        return self.at % TILES == 0

    def take(self, tag, n=1):
        t = self.at
        assert all(self.plan[t + i][0] == tag for i in range(n)), (tag, self.plan[t][0], t)
        assert t // TILES == (t + n - 1) // TILES
        if t % TILES == 0:
            self.old_block = t > 0
        s, c0 = (t // TILES) % SPLIT, (t % TILES) * P
        self.at = t + n
        return self.b.w_hi[:, s, c0:c0 + n * P], self.b.w_lo[:, s, c0:c0 + n * P]

    def done_with_block(self):
        was, self.old_block = self.old_block, False
        return was

    def skip_turns(self, turns, at, opened):
        self.at += (turns - 1) * (self.at - at)
        for ring, n in opened.items():
            self.opened[ring] += (turns - 1) * (self.opened[ring] - n)


def pe_product(pe, dst, tag, hi, lo, k, ready):
    for t in range(k):
        if ready:
            pe.eng.wait_ge(pe.sem[ready], pe.due(ready))
        if pe.new_block():
            pe.eng.wait_ge(pe.sem["w_ready"], pe.due("w_ready"))
        wh, wl = pe.take(tag)
        m = pe.eng.matmul(dst, wh, hi(t), start=t == 0, stop=False)
        if pe.done_with_block():
            m.then_inc(pe.sem["w_used"], pe.up("w_used"))
        pe.eng.matmul(dst, wh, lo(t), start=False, stop=False)
        m = pe.eng.matmul(dst, wl, hi(t), start=False, stop=t == k - 1)
    return m


def pe_features(pe, ring, tag, act, k=KD, ready=None):
    tl = pe.tile(ring)
    pe.eng.wait_ge(tl.free, pe.emptied(tl))
    pe_product(pe, tl.ps, tag, *act, k, ready).then_inc(tl.full, pe.up("full_" + ring))
    return tl


def pe_tokens(pe, ring, tag, n, act, k=KD):
    tiles = [pe.tile(ring) for _ in range(NQ)]
    pe.eng.wait_ge(tiles[-1].free, pe.emptied(tiles[-1]))
    for t in range(k):
        if pe.new_block():
            pe.eng.wait_ge(pe.sem["w_ready"], pe.due("w_ready"))
        wh, wl = pe.take(tag, n)
        for q in range(NQ):
            d = tiles[q].ps[:, 0:n * P]
            ah, al = (a(t)[:, q * P:(q + 1) * P] for a in act)
            m = pe.eng.matmul(d, ah, wh, start=t == 0, stop=False)
            if pe.done_with_block():
                m.then_inc(pe.sem["w_used"], pe.up("w_used"))
            pe.eng.matmul(d, al, wh, start=False, stop=False)
            m = pe.eng.matmul(d, ah, wl, start=False, stop=t == k - 1)
            if t == k - 1:
                m.then_inc(tiles[q].full, pe.up("full_" + ring))
    return tiles[-1]


def pe_plain(pe, ring, lhsT, rhs):
    tl = pe.tile(ring)
    pe.eng.wait_ge(tl.free, pe.emptied(tl))
    pe.eng.matmul(tl.ps[0:lhsT.shape[1], 0:rhs.shape[1]], lhsT, rhs, start=True, stop=True)\
        .then_inc(tl.full, pe.up("full_" + ring))
    return tl


def pe_norm(pe, N):
    pe.eng.wait_ge(pe.sem["sum_ready"], pe.due("sum_ready"))
    pe_plain(pe, "a", pe.b.ones, N.acc)


def pe_turned(pe, srcs):
    tl = pe.tile("a")
    pe.eng.wait_ge(tl.free, pe.emptied(tl))
    for q, s in enumerate(srcs):
        m = pe.eng.transpose(tl.ps[:, q * P:(q + 1) * P], s, pe.b.ident)
    m.then_inc(tl.full, pe.up("full_a"))
    return tl


def pe_attention(pe, units, extra=None):
    n_units, turned, tl = len(units), {}, None
    for s in range(n_units + 3):
        if s < n_units:
            for lhsT, rhs in units[s].scores:
                pe_plain(pe, "d", lhsT, rhs)
        if extra:
            extra(s)
        if 0 <= s - 2 < n_units and units[s - 2].v:
            u = units[s - 2]
            pe.eng.wait_ge(pe.sem[u.ready], pe.due(u.ready))
            if u.ready == "p_ready":
                pe.seen["e_done"] += 2
            blocks = [u.e[:, k * P:(k + 1) * P] for k in range(len(u.v))]
            for k in range(0, len(blocks), 4):
                turned[s - 2] = pe_turned(pe, blocks[k:k + 4])
        if 0 <= s - 3 < n_units and units[s - 3].v:
            u = units[s - 3]
            pe.eng.wait_ge(turned[s - 3].free, pe.taken(turned[s - 3]))
            tl = pe.tile("d")
            pe.eng.wait_ge(tl.free, pe.emptied(tl))
            for k, v in enumerate(u.v):
                m = pe.eng.matmul(tl.ps[:, 0:u.width], u.pt[:, k * P:(k + 1) * P], v, start=k == 0,
                                  stop=k == len(u.v) - 1)
            m.then_inc(tl.full, pe.up("full_d"))
    return tl


class Unit:

    def __init__(self, scores, v, width, s, e, pt, o, ready="e_done", masks=None, dist=None, slope=0.0, sink=None,
                 neg_lam=None):
        self.scores, self.v, self.width, self.s, self.e, self.pt, self.o = scores, v, width, s, e, pt, o
        self.ready, self.masks, self.dist, self.slope, self.sink, self.neg_lam = ready, masks, dist, slope, sink, neg_lam


def units_1(b):
    units = []
    for n in range(GH * NQ):
        h, i = n // NQ, n % NQ
        scores, v, masks = [], [], []
        for head, k0, m0 in heads_of_first_block(i, h):
            p0, t = head % 2 * HD, head // 2
            scores.append((b.A_Q[p0:p0 + HD, t, i * P:(i + 1) * P], b.A_K[p0:p0 + HD, t, k0 * P:(i + 1) * P]))
            masks.append(b.MASKS[:, m0:m0 + (i + 1 - k0) * P])
            v += [b.A_V[:, kt, head * HD:(head + 1) * HD] for kt in range(k0, i + 1)]
        w = len(v) * P
        units.append(Unit(scores, v, HD, b.A_S[:, n % 2, 0:w], b.A_E[:, n % 2, 0:w], b.A_P[:, n % 2, 0:w],
                          masks=masks, o=b.A_O[:, i, h * HD:(h + 1) * HD]))
    return units


def units_mla(b, half):
    units = []
    for h in range(4):
        for i in range(NQ):
            n, head = len(units), 4 * half + h
            units.append(Unit([(b.L_Q[0:MQ, h, i * P:(i + 1) * P], b.L_K[0:MQ, h])],
                              [b.L_V[:, kt, head * MV:(head + 1) * MV] for kt in range(NQ)], MV,
                              b.L_S[:, n % 2], b.L_E[:, n % 4], b.L_P[:, n % 2],
                              o=b.L_O[:, i, head * MV:(head + 1) * MV]))
    return units


def units_diff(b, neg_lam):
    units = []
    for h in range(DH):
        for i in range(NQ):
            for m in range(2):
                n, t, r = len(units), 2 * m + h // 2, slice(h % 2 * HD, h % 2 * HD + HD)
                units.append(Unit([(b.L_Q[r, t, i * P:(i + 1) * P], b.L_K[r, t])],
                                  [b.L_V[:, kt, h * DV:(h + 1) * DV] for kt in range(NQ)] if m else [], DV,
                                  b.L_S[:, n % 2], b.L_E[:, n % 4], b.L_P[:, n // 2 % 2], ready="p_ready",
                                  dist=b.L_D[:, i], slope=SLOPES[WH + h], neg_lam=neg_lam,
                                  o=b.L_O[:, i, h * DV:(h + 1) * DV]))
    return units


def units_win(b, l):
    units = []
    for h in range(WH):
        for i in range(NQ):
            n, kv, r = len(units), h // (WH // WKV), slice(h % 2 * HD, h % 2 * HD + HD)
            k0, k1 = max(i - 1, 0), min(i + 2, NQ)
            w, d0 = (k1 - k0) * P, (k0 - i + 1) * P
            units.append(Unit([(b.L_Q[r, h // 2, i * P:(i + 1) * P], b.L_K[r, kv, k0 * P:k1 * P])],
                              [b.L_V[:, kt, kv * HD:(kv + 1) * HD] for kt in range(k0, k1)], HD,
                              b.L_S[:, n % 2, 0:w], b.L_E[:, n % 4, 0:w], b.L_P[:, n % 2, 0:w],
                              dist=b.L_DW[:, i, d0:d0 + w], slope=SLOPES[h], sink=b.pc("win_sink_2", h, l),
                              o=b.L_O[:, i, h * HD:(h + 1) * HD]))
    return units


def mla_heads(b, l):
    r, out = slice(0, MQ), []
    for n in range(4):
        out += [(b.L_Q[:, n], b.col[:, 140:141], r), (b.L_K[:, n], b.pc("g_mla_k_2", 0, l), r)]
    return out


def diff_heads(b, l):
    r = slice(0, P)
    return [(b.L_Q[:, n], b.col[:, 141:142], r) for n in range(4)] + \
        [(b.L_K[:, n], b.pc("g_diff_k_2", 0, l), r) for n in range(4)]


def win_heads(b, l):
    r = slice(0, P)
    return [(b.L_Q[:, n], b.col[:, 142:143], r) for n in range(4)] + \
        [(b.L_K[:, n], b.pc("g_win_k_2", 0, l), r) for n in range(2)]


def of(hi, lo, at=0):
    return (lambda t: hi[:, at + t, :]), (lambda t: lo[:, at + t, :])


def pe_ada(pe, n):
    b, tl = pe.b, pe.tile("d")
    pe.eng.wait_ge(tl.free, pe.emptied(tl))
    for k in range(n):
        d = tl.ps[:, 2 * k:2 * k + 2]
        for t in range(KD):
            if pe.new_block():
                pe.eng.wait_ge(pe.sem["w_ready"], pe.due("w_ready"))
            wh, wl = pe.take("ada")
            m = pe.eng.matmul(d, wh, b.c_pair[:, t, :], start=t == 0, stop=False)
            if pe.done_with_block():
                m.then_inc(pe.sem["w_used"], pe.up("w_used"))
            m = pe.eng.matmul(d, wl, b.c_pair[:, t, :], start=False, stop=t == KD - 1)
    m.then_inc(tl.full, pe.up("full_d"))


def pe_skip_pad(pe):
    while pe.at < len(pe.plan) and pe.plan[pe.at][0] == "pad":
        if pe.new_block():
            pe.eng.wait_ge(pe.sem["w_ready"], pe.due("w_ready"))
        pe.take("pad")


def pe_rwkv(pe, j):
    b, eng = pe.b, pe.eng
    rows = [slice(0, HD), slice(HD, P)]
    h = of(b.h_hi, b.h_lo)
    for _ in range(3):
        pe_features(pe, "a", "rkv", h)
    pe_features(pe, "a", "w2", of(b.s_hi, b.s_lo), 1)
    pe_features(pe, "a", "a2", of(b.s_hi, b.s_lo), 1)
    pe_features(pe, "d", "g2", of(b.s_hi, b.s_lo, 1), 1)
    pe.eng.wait_ge(pe.sem["kk_sq"], pe.due("kk_sq"))
    pe_plain(pe, "a", b.pair, b.R_KK)
    pe.eng.wait_ge(pe.sem["rk_ready"], pe.due("rk_ready"))
    pe_plain(pe, "d", b.pair, b.R_T)
    for src in (b.R_V, b.R_BH, b.R_KH):
        tn = pe_turned(pe, [src[:, c * P:(c + 1) * P] for c in range(NQ)])
    for u in range(8):
        c, r = u % NQ, rows[u // NQ]
        tl = pe.tile("d")
        pe.eng.wait_ge(tl.free, pe.emptied(tl))
        eng.matmul(tl.ps[:, 0:2 * P], b.R_BH[r, c * P:(c + 1) * P], b.R_AR[r, c], start=True, stop=True)
        eng.matmul(tl.ps[:, 2 * P:], b.R_KH[r, c * P:(c + 1) * P], b.R_AR[r, c], start=True, stop=True)\
            .then_inc(tl.full, pe.up("full_" + tl.ring))
    for g in range(2):
        tl = pe.tile("d")
        pe.eng.wait_ge(tl.free, pe.emptied(tl))
        for i in range(4):
            u = 4 * g + i
            c, r = u % NQ, rows[u // NQ]
            m = eng.matmul(tl.ps[:, i * P:(i + 1) * P], b.R_AR[r, c, 0], b.R_BH[r, c * P:(c + 1) * P],
                           start=True, stop=True)
        m.then_inc(tl.full, pe.up("full_" + tl.ring))

    def four(g, lhsT, rhs):
        tl = pe.tile("d")
        pe.eng.wait_ge(tl.free, pe.emptied(tl))
        for i in range(4):
            u = 4 * g + i
            m = eng.matmul(tl.ps[:, i * P:(i + 1) * P], lhsT[:, u], rhs[:, u], start=True, stop=True)
        m.then_inc(tl.full, pe.up("full_" + tl.ring))
        return tl

    pe.eng.wait_ge(pe.sem["t_ready"], pe.due("t_ready"))
    LT = b.R_LM[:, :, 0]
    for k in range(1, 7):
        z = [four(g, LT, b.R_TN) for g in range(2)]
        done = []
        for g in range(2):
            pe.eng.wait_ge(z[g].free, pe.taken(z[g]))
            if k < 6:
                done.append(four(g, b.R_TT, b.R_Z))
            done.append(four(g, b.R_Z, b.R_TT))
        pe.eng.wait_ge(done[-1].free, pe.taken(done[-1]))
    pe.eng.wait_ge(tn.free, pe.taken(tn))
    W, U = b.R_WU[:, 0], b.R_WU[:, 1]
    for c in range(NQ):
        state = b.R_WU[:, 2 + c % 2]
        heads = [(rows[i], NQ * i + c) for i in range(2)]
        if c:
            pe.eng.wait_ge(new.free, pe.taken(new))
        tl = pe.tile("a")
        pe.eng.wait_ge(tl.free, pe.emptied(tl))
        if c:
            eng.matmul(tl.ps[:, 0:P], b.R_AR[:, c, 0], state, start=True, stop=False)
        for r, u in heads:
            m = eng.matmul(tl.ps[:, r], b.R_LM[:, u, 2], b.R_VN[:, c, r], start=c == 0, stop=c == 0 or r is rows[1])
        m.then_inc(tl.full, pe.up("full_" + tl.ring))
        pe.eng.wait_ge(tl.free, pe.taken(tl))
        tl = pe.tile("a")
        pe.eng.wait_ge(tl.free, pe.emptied(tl))
        for r, u in heads:
            m = eng.matmul(tl.ps[:, r], b.R_TT[:, u], W[:, r], start=True, stop=True)
        m.then_inc(tl.full, pe.up("full_" + tl.ring))
        pe.eng.wait_ge(tl.free, pe.taken(tl))
        if c < NQ - 1:
            new = pe.tile("d")
            pe.eng.wait_ge(new.free, pe.emptied(new))
            eng.matmul(new.ps[:, 0:P], b.R_BN[:, c], U, start=True, stop=False)
            eng.matmul(new.ps[:, 0:P], b.R_KN[:, c], b.R_VN[:, c], start=False, stop=True)\
                .then_inc(new.full, pe.up("full_" + new.ring))
        tl = pe.tile("d")
        pe.eng.wait_ge(tl.free, pe.emptied(tl))
        if c:
            eng.matmul(tl.ps[:, 0:P], state, b.R_AR[:, c, 1], start=True, stop=False)
        for r, u in heads:
            eng.matmul(tl.ps[r, 0:P], U[:, r], b.R_LM[:, u, 1], start=c == 0, stop=False)
            m = eng.matmul(tl.ps[r, 0:P], b.R_VN[:, c, r], b.R_LM[:, u, 3], start=False, stop=True)
        m.then_inc(tl.full, pe.up("full_" + tl.ring))
    pe.eng.wait_ge(tl.free, pe.taken(tl))
    pe_plain(pe, "d", b.pair, b.R_Y)
    pe.eng.wait_ge(pe.sem["yc_sq"], pe.due("yc_sq"))
    pe_plain(pe, "a", b.pair, b.R_KK)


def pe_head_norms(pe, heads, lhsT, rope=False):
    b, N = pe.b, pe.b.NH
    for n, (_, _, rows) in enumerate(heads):
        pe.eng.wait_ge(pe.sem["head_sq"], pe.due("head_sq"))
        pe_plain(pe, "a", lhsT[rows], N.sq[rows, n % 2])
    if rope:
        pe.eng.wait_ge(pe.sem["head_normed"], pe.due("head_normed", len(heads)))
        for t, _, rows in heads:
            pe_plain(pe, "d", b.const[rows, C_PERM2:C_PERM2 + MQ], t[rows])
    pe.eng.wait_ge(pe.sem["heads_ready"], pe.due("heads_ready"))


def pe_branch(pe):
    b = pe.b
    for n in range(KD):
        pe_features(pe, "d", "branch2", of(b.o_hi, b.o_lo), BW // P, ready="act_lo" if n == 0 else None)
        pe_features(pe, "a", "gate2", of(b.h_hi, b.h_lo))


def pe_turn_out(pe):
    pe.eng.wait_ge(pe.sem["o_done"], pe.due("o_done"))
    for f in range(4):
        pe_turned(pe, [pe.b.L_O[:, q, f * P:(f + 1) * P] for q in range(NQ)])


def pe_layer(pe, l):
    b = pe.b
    H = of(b.h_hi, b.h_lo)
    pe.eng.wait_ge(pe.sem["lam_parts"], pe.due("lam_parts"))
    pe_plain(pe, "a", b.ones[0:HD], b.col[0:HD, 152:154])
    pe_norm(pe, b.N1)
    for n in range(3):
        pe_features(pe, "a", "c", H, ready="act_lo" if n == 0 else None)
    pe_features(pe, "a", "kr", H)
    pe_norm(pe, b.N1)
    pe_norm(pe, b.N1)
    pe.eng.wait_ge(pe.sem["act_lo"], pe.due("act_lo", 3))
    for half in range(2):
        for n in range(4):
            pe_features(pe, "a", "uq", of(b.s_hi, b.s_lo), 2)
            pe_features(pe, "a", "uk", of(b.s_hi, b.s_lo, 2), 1)
        v = pe_tokens(pe, "a", "uv", 2, of(b.s_hi, b.s_lo, 2), 1)
        pe_head_norms(pe, mla_heads(b, l), b.ones, rope=True)
        pe.eng.wait_ge(v.free, pe.taken(v))
        last = pe_attention(pe, units_mla(b, half))
    pe_skip_pad(pe)
    pe_turn_out(pe)
    pe_branch(pe)
    for n in range(8):
        pe_features(pe, "a", "dqk", H)
    v = pe_tokens(pe, "a", "dv", 4, H)
    pe_head_norms(pe, diff_heads(b, l), b.pair)
    pe.eng.wait_ge(v.free, pe.taken(v))
    pe_attention(pe, units_diff(b, None))
    pe_turn_out(pe)
    pe_branch(pe)
    for n in range(6):
        pe_features(pe, "a", "sqk", H)
    v = pe_tokens(pe, "a", "sv", 1, H)
    pe_head_norms(pe, win_heads(b, l), b.pair)
    pe.eng.wait_ge(v.free, pe.taken(v))
    pe_attention(pe, units_win(b, l))
    pe_turn_out(pe)
    pe_branch(pe)
    for n in range(KD):
        pe_features(pe, "d", "out2", H, ready="act_lo" if n == 0 else None)
    pe_norm(pe, b.N1)

    def up(ready=None):
        for n in range(4):
            pe_features(pe, "a", "gate_up", H, ready=ready if n == 0 else None)

    def down(half):
        pe.eng.wait_ge(pe.sem["hid_lo"], pe.due("hid_lo", 2))
        for n in range(KD):
            pe_features(pe, "d", "down2", of(b.o_hi, b.o_lo, 2 * half), 2)

    up("act_lo")
    turns = (FF2 // P // 2 - 1) // 2
    at, opened = pe.at, dict(pe.opened)
    with pe.loop(turns, w_ready=12, w_used=12, full_a=8, full_d=16, hid_lo=4):
        for half in range(2):
            up()
            down(half)
    pe.skip_turns(turns, at, opened)
    down(0)
    pe.eng.wait_ge(pe.sem["act_lo"], pe.due("act_lo", 2))
    for n in range(KD):
        pe_features(pe, "d", "ple", of(b.s_hi, b.s_lo), 2)
    pe_norm(pe, b.N1)
    pe_norm(pe, b.N1)
    for n in range(KD):
        pe_features(pe, "a", "pgate", H, ready="act_lo" if n == 0 else None)


def pe_program(eng, sig, b, plan):
    pe = Pe(eng, sig, b, plan)
    H, O = of(b.h_hi, b.h_lo), of(b.o_hi, b.o_lo)
    pe.eng.wait_ge(pe.sem["loaded"], pe.due("loaded", NLOAD * 16))
    pe.eng.wait_ge(pe.sem["c_ready"], pe.due("c_ready"))
    pe_ada(pe, 2 * KD)
    pe_norm(pe, b.N0)
    raws = [pe_features(pe, "a", "qk", H, ready="act_lo" if n == 0 else None) for n in range(12)]
    for n in range(12):
        pe.eng.wait_ge(raws[n].free, pe.taken(raws[n]))
        tl = pe_plain(pe, "d", b.const[:, C_PERM1:C_PERM1 + P], (b.A_Q if n < 6 else b.A_K)[:, n % 6])
    pe_tokens(pe, "a", "v4", 4, H)
    v = pe_tokens(pe, "a", "v2", 2, H)
    pe.eng.wait_ge(pe.sem["qk_ready"], pe.due("qk_ready"))
    pe.eng.wait_ge(v.free, pe.taken(v))
    last = pe_attention(pe, units_1(b), extra=lambda s: pe_ada(pe, 2) if s < 16 else None)
    pe.eng.wait_ge(last.free, pe.taken(last))
    for f in range(2):
        pe_turned(pe, [b.A_O[:, q, f * P:(f + 1) * P] for q in range(NQ)])
    for n in range(2):
        pe_features(pe, "a", "lora", H)
    pe.eng.wait_ge(pe.sem["act_lo"], pe.due("act_lo", 4))
    for j in range(KD):
        pe_rwkv(pe, j)
    pe.eng.wait_ge(pe.sem["act_lo"], pe.due("act_lo", KD))
    for n in range(KD):
        for part in range(2):
            pe_features(pe, "a", "gate", H)
        pe_features(pe, "d", "branch", of(b.s_hi, b.s_lo, 2), 2)
        pe_features(pe, "d", "branch", O)
    for n in range(KD):
        pe_features(pe, "d", "out", H, ready="act_lo" if n == 0 else None)
    pe_norm(pe, b.N1)
    pe_norm(pe, b.N1)

    def up(ready=None):
        for n in range(4):
            pe_features(pe, "a", "up1", H, ready=ready if n == 0 else None)

    def down(half):
        pe.eng.wait_ge(pe.sem["hid_lo"], pe.due("hid_lo", 4))
        for n in range(KD):
            pe_features(pe, "d", "down1", of(b.o_hi, b.o_lo, 4 * half), 4)

    up("act_lo")
    turns = (FF1 // P // 4 - 2) // 2
    at, opened = pe.at, dict(pe.opened)
    with pe.loop(turns, w_ready=16, w_used=16, full_a=8, full_d=16, hid_lo=8):
        for half in range(2):
            up()
            down(half)
    pe.skip_turns(turns, at, opened)
    up()
    down(0)
    down(1)
    pe_norm(pe, b.N1)
    for l in range(LAYERS):
        pe_layer(pe, l)
    pe_skip_pad(pe)


class Act(Counts):
    def __init__(self, eng, sem, b):
        super().__init__(eng, sem, "act_step")
        self.b, self.n, self.counts = b, 0, {}

    def bank(self):
        self.n += 1
        return self.b.psum["a"][:, (self.n - 1) % BANKS]


def act_norm(a, N, k, src, width, dst=None, bias=None, src_ready=None):
    base = a.counts.get("sq_used", 0)
    for t in range(k):
        if src_ready:
            a.eng.wait_ge(a.sem[src_ready], a.due(src_ready))
        if base + max(1, t - 2) > 0 and t >= 2:
            a.eng.wait_ge(a.sem["sq_used"], base + max(1, t - 2))
        a.eng.wait_ge(a.sem[a.last], a.own())
        a.eng.activation(N.sq[:, t % 2], src(t), ACT.Square).then_inc(a.sem["sq"], a.up("sq"))
    a.counts["sq_used"] = base + max(0, k - 2)
    a.eng.wait_ge(a.sem["full_a"], a.due("full_a"))
    a.eng.activation(N.std, a.bank(), ACT.Sqrt, bias=a.b.eps, scale=1.0 / width)\
        .then_inc(a.sem["free_a"], a.up("free_a"))
    a.eng.wait_ge(a.sem[a.last], a.own())
    a.eng.sem_inc(a.sem["std"], a.up("std"))
    if dst:
        for t in range(k):
            a.eng.wait_ge(a.sem["scaled"], a.due("scaled"))
            if bias is None:
                a.eng.activation(dst(t), N.tmp[:, t % 4], ACT.Copy).then_inc(a.sem["act_hi"], a.up("act_hi"))
            else:
                a.eng.activation(dst(t), N.tmp[:, t % 4], ACT.Identity, bias=bias(t))\
                    .then_inc(a.sem["act_hi"], a.up("act_hi"))


def act_rwkv(a, j):
    b, n = a.b, 2 + 3 * j
    for part in range(3):
        if n + part - 1 > 0:
            a.eng.wait_ge(a.sem["shifted"], a.value("shifted", n + part - 1))
        a.eng.wait_ge(a.sem["full_a"], a.due("full_a"))
        a.eng.wait_ge(a.sem[a.last], a.own())
        a.eng.activation(b.R_U[:, (n + part) % 2, 1:], a.bank(), ACT.Copy).then_inc(a.sem["free_a"], a.up("free_a"))
        a.eng.wait_ge(a.sem[a.last], a.own())
        a.eng.sem_inc(a.sem["u_ready"], a.up("u_ready"))
    a.eng.wait_ge(a.sem["full_a"], a.due("full_a"))
    a.eng.wait_ge(a.sem[a.last], a.own())
    a.eng.activation(b.R_SW, a.bank(), ACT.Sigmoid, bias=b.pc("decay_w0", j))\
        .then_inc(a.sem["free_a"], a.up("free_a"))
    a.eng.wait_ge(a.sem["full_a"], a.due("full_a"))
    a.eng.wait_ge(a.sem[a.last], a.own())
    a.eng.activation(b.R_AA, a.bank(), ACT.Sigmoid, bias=b.pc("iclr_a0", j)).then_inc(a.sem["free_a"], a.up("free_a"))
    a.eng.wait_ge(a.sem[a.last], a.own())
    a.eng.sem_inc(a.sem["wa_ready"], a.up("wa_ready"))
    if n + 2 > 0:
        a.eng.wait_ge(a.sem["shifted"], a.value("shifted", n + 2))
    a.eng.wait_ge(a.sem[a.last], a.own())
    a.eng.activation(b.R_KK, b.R_K, ACT.Square, scale=b.pc("k_k", j)).then_inc(a.sem["kk_sq"], a.up("kk_sq"))
    a.eng.wait_ge(a.sem["cum_ready"], a.due("cum_ready"))
    plus, minus = b.col[:, 160:164], b.col[:, 164:168]
    for c in range(NQ):
        a.eng.wait_ge(a.sem[a.last], a.own())
        a.eng.activation(b.R_PB[:, c, 1:], b.R_CUM[:, c * P:(c + 1) * P], ACT.Exp, bias=plus[:, c:c + 1], scale=-DECAY)\
            .then_inc(a.sem["act_step"], a.up("act_step"))
    a.eng.wait_ge(a.sem[a.last], a.own())
    a.eng.activation(b.R_PB[:, :, 0], plus, ACT.Exp).then_inc(a.sem["act_step"], a.up("act_step"))
    a.eng.wait_ge(a.sem[a.last], a.own())
    a.eng.activation(b.col[:, 168:172], minus, ACT.Exp).then_inc(a.sem["act_step"], a.up("act_step"))
    for c in range(NQ):
        a.eng.wait_ge(a.sem[a.last], a.own())
        a.eng.activation(b.R_CUM[:, c * P:(c + 1) * P], b.R_CUM[:, c * P:(c + 1) * P], ACT.Exp, bias=minus[:, c:c + 1], scale=DECAY)\
            .then_inc(a.sem["decays" if c == NQ - 1 else "act_step"], a.up("decays" if c == NQ - 1 else "act_step"))
    a.eng.wait_ge(a.sem["full_a"], a.due("full_a"))
    a.eng.wait_ge(a.sem[a.last], a.own())
    a.eng.activation(b.R_SW, a.bank(), ACT.Sqrt).then_inc(a.sem["free_a"], a.up("free_a"))
    a.eng.wait_ge(a.sem[a.last], a.own())
    a.eng.sem_inc(a.sem["kk_std"], a.up("kk_std"))
    for dst in (b.R_VN, b.R_BN, b.R_KN):
        a.eng.wait_ge(a.sem["full_a"], a.due("full_a"))
        a.eng.wait_ge(a.sem[a.last], a.own())
        a.eng.activation(dst, a.bank().rearrange("p (c n) -> p c n", c=NQ), ACT.Copy)\
            .then_inc(a.sem["free_a"], a.up("free_a"))
    for c in range(NQ):
        for s in range(2):
            a.eng.wait_ge(a.sem["full_a"], a.due("full_a"))
            a.eng.wait_ge(a.sem[a.last], a.own())
            a.eng.activation(b.R_WU[:, s], a.bank()[:, 0:P], ACT.Copy).then_inc(a.sem["free_a"], a.up("free_a"))
    a.eng.wait_ge(a.sem["centered"], a.due("centered"))
    a.eng.wait_ge(a.sem[a.last], a.own())
    a.eng.activation(b.R_KK, b.R_YC, ACT.Square).then_inc(a.sem["yc_sq"], a.up("yc_sq"))
    a.eng.wait_ge(a.sem["full_a"], a.due("full_a"))
    a.eng.wait_ge(a.sem[a.last], a.own())
    a.eng.activation(b.R_SW, a.bank(), ACT.Sqrt, bias=b.gn_eps, scale=1.0 / HD)\
        .then_inc(a.sem["free_a"], a.up("free_a"))
    a.eng.wait_ge(a.sem[a.last], a.own())
    a.eng.sem_inc(a.sem["gn_std"], a.up("gn_std"))
    a.eng.wait_ge(a.sem["mixed"], a.due("mixed"))
    a.eng.wait_ge(a.sem[a.last], a.own())
    a.eng.activation(b.o_hi[:, j], b.R_O, ACT.Copy).then_inc(a.sem["act_hi"], a.up("act_hi"))


def act_attention(a, units):
    n_units = len(units)
    for s in range(n_units + 3):
        if 0 <= s - 1 < n_units:
            u = units[s - 1]
            a.eng.wait_ge(a.sem["s_ready"], a.due("s_ready"))
            if u.sink is not None:
                a.eng.wait_ge(a.sem[a.last], a.own())
                a.eng.activation(u.sunk, u.sink, ACT.Exp, bias=u.neg).then_inc(a.sem["act_step"], a.up("act_step"))
            a.eng.wait_ge(a.sem[a.last], a.own())
            a.eng.activation(u.e, u.s, ACT.Exp, bias=u.neg, accum_out=u.sum).then_inc(a.sem["e_done"], a.up("e_done"))
        if 0 <= s - 2 < n_units and units[s - 2].v:
            u = units[s - 2]
            for b0 in range(0, len(u.v), 4):
                w = min(4, len(u.v) - b0) * P
                a.eng.wait_ge(a.sem["full_a"], a.due("full_a"))
                a.eng.wait_ge(a.sem[a.last], a.own())
                a.eng.activation(u.pt[:, b0 * P:b0 * P + w], a.bank()[:, 0:w], ACT.Copy)\
                    .then_inc(a.sem["free_a"], a.up("free_a"))


def act_head_norms(a, heads, lhs_width):
    b, N = a.b, a.b.NH
    base = a.counts.get("head_normed", 0)
    for n in range(len(heads) + 1):
        if n < len(heads):
            t, _, rows = heads[n]
            a.eng.wait_ge(a.sem[a.last], a.own())
            a.eng.activation(N.sq[rows, n % 2], t[rows], ACT.Square).then_inc(a.sem["head_sq"], a.up("head_sq"))
        if n:
            _, _, rows = heads[n - 1]
            if base + n - 2 > 0:
                a.eng.wait_ge(a.sem["head_normed"], a.value("head_normed", base + n - 2))
            a.eng.wait_ge(a.sem["full_a"], a.due("full_a"))
            a.eng.wait_ge(a.sem[a.last], a.own())
            a.eng.activation((N.std if (n - 1) % 2 else N.acc)[rows], a.bank()[rows], ACT.Sqrt, bias=b.eps[rows], scale=1.0 / lhs_width)\
                .then_inc(a.sem["free_a"], a.up("free_a"))
            a.eng.wait_ge(a.sem[a.last], a.own())
            a.eng.sem_inc(a.sem["head_std"], a.up("head_std"))
    a.counts["head_normed"] = base + len(heads)


def act_turned(a, gain=None):
    b = a.b
    for f in range(4):
        a.eng.wait_ge(a.sem["full_a"], a.due("full_a"))
        a.eng.activation(b.L_E[:, f], a.bank(), ACT.Identity, scale=1.0 if gain is None else gain)\
            .then_inc(a.sem["free_a"], a.up("free_a"))
        a.eng.wait_ge(a.sem[a.last], a.own())
        a.eng.sem_inc(a.sem["o_plain"], a.up("o_plain"))
        a.eng.wait_ge(a.sem[a.last], a.own())
        a.eng.activation(b.o_hi[:, f], b.L_E[:, f], ACT.Copy).then_inc(a.sem["act_hi"], a.up("act_hi"))


def act_gates(a, slots):
    base = a.counts["merged"]
    for n in range(KD):
        if base + n - 1 > 0:
            a.eng.wait_ge(a.sem["merged"], a.value("merged", base + n - 1))
        a.eng.wait_ge(a.sem["full_a"], a.due("full_a"))
        a.eng.wait_ge(a.sem[a.last], a.own())
        a.eng.activation(slots[:, n % 2], a.bank(), ACT.Sigmoid).then_inc(a.sem["free_a"], a.up("free_a"))
        a.eng.wait_ge(a.sem[a.last], a.own())
        a.eng.sem_inc(a.sem["gate_ready"], a.up("gate_ready"))
    a.counts["merged"] = base + KD
    if base + KD > 0:
        a.eng.wait_ge(a.sem["merged"], a.value("merged", base + KD))


def act_setup(a, ins):
    b = a.b
    a.eng.wait_ge(a.sem["x_ready"], a.due("x_ready", KD))
    a.counts["x_seen"] = 1
    a.eng.dma_start(b.L_KR.bitcast(I32), ins["pos_rows_2"]).then_inc(a.sem["positions"], 16)
    for dst in (b.L_SIN, b.L_COS):
        a.eng.wait_ge(a.sem["angle"], a.due("angle"))
        a.eng.wait_ge(a.sem[a.last], a.own())
        a.eng.activation(dst, b.L_DW_TMP[:, 3], ACT.Sin).then_inc(a.sem["sine"], a.up("sine"))


def act_layer(a, l, ins):
    b, N = a.b, a.b.N1
    h, _ = of(b.h_hi, b.h_lo)
    a.eng.wait_ge(a.sem["full_a"], a.due("full_a"))
    a.eng.wait_ge(a.sem[a.last], a.own())
    a.eng.activation(b.col[:, 154:156], a.bank()[:, 0:2], ACT.Exp).then_inc(a.sem["free_a"], a.up("free_a"))
    a.eng.wait_ge(a.sem[a.last], a.own())
    a.eng.sem_inc(a.sem["lam_exp"], a.up("lam_exp"))
    act_norm(a, N, KD, lambda t: b.x[:, t], D, h, src_ready=None if a.counts["x_seen"] else "x_ready")
    a.counts["x_seen"] = 0
    a.eng.dma_start(b.L_PE[:, :, :], ins["pe"][l].rearrange("(k p) t -> p k t", p=P)).then_inc(a.sem["pe_loaded"], 16)
    for n in range(3):
        a.eng.wait_ge(a.sem["full_a"], a.due("full_a"))
        a.eng.wait_ge(a.sem[a.last], a.own())
        a.eng.activation(b.L_C[:, n], a.bank(), ACT.Copy).then_inc(a.sem["free_a"], a.up("free_a"))
    a.eng.wait_ge(a.sem["full_a"], a.due("full_a"))
    a.eng.wait_ge(a.sem[a.last], a.own())
    a.eng.activation(b.L_KR, a.bank(), ACT.Copy).then_inc(a.sem["free_a"], a.up("free_a"))
    s_hi, _ = of(b.s_hi, b.s_lo)
    act_norm(a, N, 2, lambda t: b.L_C[:, t], QR, s_hi)
    act_norm(a, N, 1, lambda t: b.L_C[:, 2], KVR, of(b.s_hi, b.s_lo, 2)[0])
    for half in range(2):
        for n in range(4):
            a.eng.wait_ge(a.sem["full_a"], a.due("full_a"))
            a.eng.wait_ge(a.sem[a.last], a.own())
            a.eng.activation(b.L_Q[:, n], a.bank(), ACT.Copy).then_inc(a.sem["free_a"], a.up("free_a"))
            a.eng.wait_ge(a.sem["full_a"], a.due("full_a"))
            a.eng.wait_ge(a.sem[a.last], a.own())
            a.eng.activation(b.L_K[0:NOPE, n], a.bank()[0:NOPE], ACT.Copy).then_inc(a.sem["free_a"], a.up("free_a"))
            a.eng.wait_ge(a.sem[a.last], a.own())
            a.eng.activation(b.L_K[NOPE:MQ, n], b.L_KR[NOPE:MQ], ACT.Copy)\
                .then_inc(a.sem["act_step"], a.up("act_step"))
        for q in range(NQ):
            a.eng.wait_ge(a.sem["full_a"], a.due("full_a"))
            a.eng.wait_ge(a.sem[a.last], a.own())
            a.eng.activation(b.L_V[:, q, half * 256:half * 256 + 256], a.bank()[:, 0:256], ACT.Copy)\
                .then_inc(a.sem["free_a"], a.up("free_a"))
        act_head_norms(a, mla_heads(b, l), MQ)
        act_attention(a, columns(units_mla(b, half), b))
    act_turned(a)
    act_gates(a, b.L_SG)
    for dst, n in ((b.L_Q, 4), (b.L_K, 4)):
        for t in range(n):
            a.eng.wait_ge(a.sem["full_a"], a.due("full_a"))
            a.eng.wait_ge(a.sem[a.last], a.own())
            a.eng.activation(dst[:, t], a.bank(), ACT.Copy).then_inc(a.sem["free_a"], a.up("free_a"))
    for q in range(NQ):
        a.eng.wait_ge(a.sem["full_a"], a.due("full_a"))
        a.eng.wait_ge(a.sem[a.last], a.own())
        a.eng.activation(b.L_V[:, q], a.bank(), ACT.Copy).then_inc(a.sem["free_a"], a.up("free_a"))
    act_head_norms(a, diff_heads(b, l), HD)
    act_attention(a, columns(units_diff(b, None), b))
    a.eng.wait_ge(a.sem["out_squares"], a.due("out_squares"))
    a.eng.wait_ge(a.sem[a.last], a.own())
    a.eng.activation(b.col[:, 100:116], b.col[:, 100:116], ACT.Sqrt, bias=b.eps, scale=1.0 / DV)\
        .then_inc(a.sem["act_step"], a.up("act_step"))
    a.eng.wait_ge(a.sem[a.last], a.own())
    a.eng.sem_inc(a.sem["out_std"], a.up("out_std"))
    act_turned(a, b.col[:, 143:144])
    act_gates(a, b.L_SG)
    for dst, n in ((b.L_Q, 4), (b.L_K, 2)):
        for t in range(n):
            a.eng.wait_ge(a.sem["full_a"], a.due("full_a"))
            a.eng.wait_ge(a.sem[a.last], a.own())
            a.eng.activation(dst[:, t], a.bank(), ACT.Copy).then_inc(a.sem["free_a"], a.up("free_a"))
    for q in range(NQ):
        a.eng.wait_ge(a.sem["full_a"], a.due("full_a"))
        a.eng.wait_ge(a.sem[a.last], a.own())
        a.eng.activation(b.L_V[:, q, 0:P], a.bank()[:, 0:P], ACT.Copy).then_inc(a.sem["free_a"], a.up("free_a"))
    act_head_norms(a, win_heads(b, l), HD)
    act_attention(a, columns(units_win(b, l), b))
    act_turned(a)
    act_gates(a, b.L_SG)
    for n in range(KD):
        a.eng.wait_ge(a.sem[a.last], a.own())
        a.eng.activation(b.h_hi[:, n], b.L_M[:, n], ACT.Copy).then_inc(a.sem["act_hi"], a.up("act_hi"))
    act_norm(a, N, KD, lambda t: b.x[:, t], D, h, src_ready="x_ready")
    a.eng.wait_ge(a.sem["mlp_clear"], a.due("mlp_clear"))
    for n in range(FF2 // P):
        a.eng.wait_ge(a.sem["full_a"], a.due("full_a"))
        a.eng.wait_ge(a.sem[a.last], a.own())
        a.eng.activation(b.F_G[:, n % 2, 1:T + 1], a.bank(), ACT.Copy).then_inc(a.sem["free_a"], a.up("free_a"))
        a.eng.wait_ge(a.sem["full_a"], a.due("full_a"))
        a.eng.wait_ge(a.sem[a.last], a.own())
        a.eng.activation(b.F_U[:, n % 2], a.bank(), ACT.Copy).then_inc(a.sem["free_a"], a.up("free_a"))
        a.eng.wait_ge(a.sem[a.last], a.own())
        a.eng.sem_inc(a.sem["gu_ready"], a.up("gu_ready"))
        a.eng.wait_ge(a.sem["conv"], a.due("conv"))
        a.eng.wait_ge(a.sem[a.last], a.own())
        a.eng.activation(b.F_A, b.F_C, ACT.Gelu_apprx_tanh, bias=b.pc("conv_b_2", n, l))\
            .then_inc(a.sem["gelu"], a.up("gelu"))
        a.eng.wait_ge(a.sem["f_ready"], a.due("f_ready"))
        a.eng.wait_ge(a.sem[a.last], a.own())
        a.eng.activation(b.o_hi[:, n % 4], b.F_F, ACT.Copy).then_inc(a.sem["act_hi"], a.up("act_hi"))
    if 16 * (l + 1) > 0:
        a.eng.wait_ge(a.sem["pe_loaded"], a.value("pe_loaded", 16 * (l + 1)))
    for t in range(2):
        a.eng.wait_ge(a.sem[a.last], a.own())
        a.eng.activation(b.s_hi[:, t], b.L_PE[:, t], ACT.Copy).then_inc(a.sem["act_hi"], a.up("act_hi"))
    act_norm(a, N, KD, lambda t: b.Y8[:, t], D, src_ready="y_ready")
    act_norm(a, N, KD, lambda t: b.x[:, t], D, h, src_ready="x_ready")
    act_gates(a, b.F_SG)


def act_program(eng, sig, b, ins):
    a = Act(eng, sig, b)
    eng.sem_inc(sig["free_a"], BANKS)
    a.raised["free_a"] = BANKS
    for dst, src in ((b.par[:, :], ins["params"]), (b.posrow_i, ins["pos_rows"]), (b.posi[:, :], ins["pos_cols"]),
                     (b.const[:, :], ins["const"]), (b.MASKS, ins["masks"][:, 0:M_BAND]),
                     (b.x[:, :, :], ins["x"].rearrange("(k p) t -> p k t", p=P))):
        eng.dma_start(dst, src).then_inc(sig["loaded"], 16)
    a.eng.wait_ge(a.sem["loaded"], a.due("loaded", NLOAD * 16))
    a.eng.activation(b.col[:, 0:8], b.pcs("c", KD), ACT.Sigmoid).then_inc(a.sem["sigmoid_c"], a.up("sigmoid_c"))
    for dst in (b.A_SN, b.A_C):
        a.eng.wait_ge(a.sem["angle"], a.due("angle"))
        a.eng.wait_ge(a.sem[a.last], a.own())
        a.eng.activation(dst, b.A_T[:, 3], ACT.Sin).then_inc(a.sem["sine"], a.up("sine"))
    h, hl = of(b.h_hi, b.h_lo)
    act_norm(a, b.N0, KD, lambda t: b.x[:, t], D, h, bias=lambda t: b.mod[:, t:t + 1])
    for n in range(12):
        a.eng.wait_ge(a.sem["full_a"], a.due("full_a"))
        a.eng.wait_ge(a.sem[a.last], a.own())
        a.eng.activation((b.A_Q if n < 6 else b.A_K)[:, n % 6], a.bank(), ACT.Copy, scale=HD ** -0.5 if n < 6 else 1.0)\
            .then_inc(a.sem["free_a"], a.up("free_a"))
    for w0, w in ((0, 512), (512, 256)):
        for q in range(NQ):
            a.eng.wait_ge(a.sem["full_a"], a.due("full_a"))
            a.eng.wait_ge(a.sem[a.last], a.own())
            a.eng.activation(b.A_V[:, q, w0:w0 + w], a.bank()[:, 0:w], ACT.Copy)\
                .then_inc(a.sem["free_a"], a.up("free_a"))
    us = columns(units_1(b), b)
    act_attention(a, us)
    for f in range(2):
        a.eng.wait_ge(a.sem["full_a"], a.due("full_a"))
        a.eng.wait_ge(a.sem[a.last], a.own())
        a.eng.activation(b.A_T[:, f], a.bank(), ACT.Copy).then_inc(a.sem["free_a"], a.up("free_a"))
        a.eng.wait_ge(a.sem[a.last], a.own())
        a.eng.sem_inc(a.sem["o_plain"], a.up("o_plain"))
        a.eng.wait_ge(a.sem[a.last], a.own())
        a.eng.activation(b.s_hi[:, 2 + f], b.A_T[:, f], ACT.Copy).then_inc(a.sem["act_hi"], a.up("act_hi"))
    for n in range(2):
        if n == 0:
            a.eng.wait_ge(a.sem["rwkv_clear"], a.due("rwkv_clear"))
        a.eng.wait_ge(a.sem["full_a"], a.due("full_a"))
        a.eng.wait_ge(a.sem[a.last], a.own())
        a.eng.activation(b.R_U[:, n, 1:], a.bank(), ACT.Copy).then_inc(a.sem["free_a"], a.up("free_a"))
        a.eng.wait_ge(a.sem[a.last], a.own())
        a.eng.sem_inc(a.sem["u_ready"], a.up("u_ready"))
    if 1 > 0:
        a.eng.wait_ge(a.sem["shifted"], a.value("shifted", 1))
    a.eng.wait_ge(a.sem[a.last], a.own())
    a.eng.activation(b.R_K[0:LORA], b.R_K[0:LORA], ACT.Tanh).then_inc(a.sem["act_step"], a.up("act_step"))
    a.eng.wait_ge(a.sem[a.last], a.own())
    a.eng.sem_inc(a.sem["lora_act"], a.up("lora_act"))
    a.eng.wait_ge(a.sem[a.last], a.own())
    a.eng.activation(b.s_hi[:, 0], b.R_K, ACT.Copy).then_inc(a.sem["act_hi"], a.up("act_hi"))
    if 2 > 0:
        a.eng.wait_ge(a.sem["shifted"], a.value("shifted", 2))
    a.eng.wait_ge(a.sem[a.last], a.own())
    a.eng.activation(b.R_V, b.R_V, ACT.Sigmoid).then_inc(a.sem["act_step"], a.up("act_step"))
    a.eng.wait_ge(a.sem[a.last], a.own())
    a.eng.sem_inc(a.sem["lora_act"], a.up("lora_act"))
    a.eng.wait_ge(a.sem[a.last], a.own())
    a.eng.activation(b.s_hi[:, 1], b.R_V, ACT.Copy).then_inc(a.sem["act_hi"], a.up("act_hi"))
    for j in range(KD):
        act_rwkv(a, j)
    a.eng.wait_ge(a.sem["mix_clear"], a.due("mix_clear"))
    for n in range(KD):
        if n - 1 > 0:
            a.eng.wait_ge(a.sem["merged"], a.value("merged", n - 1))
        for part in range(2):
            a.eng.wait_ge(a.sem["full_a"], a.due("full_a"))
            a.eng.wait_ge(a.sem[a.last], a.own())
            a.eng.activation(b.G_SG[:, 2 * (n % 2) + part], a.bank(), ACT.Sigmoid)\
                .then_inc(a.sem["free_a"], a.up("free_a"))
        a.eng.wait_ge(a.sem[a.last], a.own())
        a.eng.sem_inc(a.sem["gate_ready"], a.up("gate_ready"))
    for n in range(KD):
        if n == 0:
            a.eng.wait_ge(a.sem["merged"], a.due("merged", KD))
        a.eng.wait_ge(a.sem[a.last], a.own())
        a.eng.activation(b.h_hi[:, n], b.G_M[:, n], ACT.Copy).then_inc(a.sem["act_hi"], a.up("act_hi"))
    act_norm(a, b.N1, KD, lambda t: b.Y8[:, t], D, src_ready="y_ready")
    act_norm(a, b.N1, KD, lambda t: b.x[:, t], D, h, bias=lambda t: b.mod[:, 24 + t:25 + t], src_ready="x_ready")
    for n in range(FF1 // P):
        if n - 3 > 0:
            a.eng.wait_ge(a.sem["hid_lo"], a.value("hid_lo", n - 3))
        a.eng.wait_ge(a.sem["full_a"], a.due("full_a"))
        a.eng.wait_ge(a.sem[a.last], a.own())
        a.eng.activation(b.F_R[:, n % 4], a.bank(), ACT.Relu).then_inc(a.sem["free_a"], a.up("free_a"))
        a.eng.wait_ge(a.sem[a.last], a.own())
        a.eng.activation(b.o_hi[:, n % 8], b.F_R[:, n % 4], ACT.Square).then_inc(a.sem["hid_hi"], a.up("hid_hi"))
    a.counts["hid_lo"] = FF1 // P
    act_norm(a, b.N1, KD, lambda t: b.Y8[:, t], D, src_ready="y_ready")
    act_setup(a, ins)
    a.counts["merged"] = KD
    for l in range(LAYERS):
        act_layer(a, l, ins)


def columns(units, b):
    for n, u in enumerate(units):
        c = 32 + 2 * (n % 32)
        u.top, u.neg, u.sum = b.col[:, 120 + n % 4:121 + n % 4], b.col[:, c:c + 1], b.col[:, c + 1:c + 2]
        u.inv, u.sunk = b.col[:, 124 + n % 4:125 + n % 4], b.col[:, 128 + n % 8:129 + n % 8]
    return units


class Dve(Counts):
    def __init__(self, eng, sem, b):
        super().__init__(eng, sem, "dve_step")
        self.b, self.n, self.counts = b, 0, {}

    def bank(self):
        self.n += 1
        return self.b.psum["d"][:, (self.n - 1) % BANKS]

    def each(self, mask, n):
        return mask.unsqueeze(1).to_broadcast([P, n, mask.shape[1]])


def dve_norm(v, N, k):
    for t in range(k):
        v.eng.wait_ge(v.sem["sq"], v.due("sq"))
        name = "sum_ready" if t == k - 1 else "sq_used"
        if k == 1:
            v.eng.tensor_copy(N.acc, N.sq[:, 0]).then_inc(v.sem[name], v.up(name))
        elif t:
            v.eng.wait_ge(v.sem[v.last], v.own())
            v.eng.tensor_tensor(N.acc, N.sq[:, 0] if t == 1 else N.acc, N.sq[:, t % 2], ALU.add)\
                .then_inc(v.sem[name], v.up(name))
    v.eng.wait_ge(v.sem["std"], v.due("std"))
    v.eng.reciprocal(N.inv, N.std).then_inc(v.sem["dve_step"], v.up("dve_step"))


def dve_norm_split(v, N, k, src, gain, hi, lo, bias=None):
    dve_norm(v, N, k)
    for t in range(k + 1):
        v.eng.wait_ge(v.sem[v.last], v.own())
        if t < k:
            v.eng.scalar_tensor_tensor(N.tmp[:, t % 4], src(t), gain(t), N.inv, ALU.mult, ALU.mult)\
                .then_inc(v.sem["scaled"], v.up("scaled"))
        if t:
            v.eng.wait_ge(v.sem["act_hi"], v.due("act_hi"))
            y, high = N.tmp[:, (t - 1) % 4], hi(t - 1).bitcast(F32)
            if bias:
                v.eng.scalar_tensor_tensor(lo(t - 1), y, bias(t - 1), high, ALU.add, ALU.subtract)\
                    .then_inc(v.sem["act_lo"], v.up("act_lo"))
            else:
                v.eng.tensor_tensor(lo(t - 1), y, high, ALU.subtract).then_inc(v.sem["act_lo"], v.up("act_lo"))


def dve_norm_add(v, N, gain, last=None):
    b = v.b
    dve_norm(v, N, KD)
    for t in range(KD):
        v.eng.wait_ge(v.sem[v.last], v.own())
        v.eng.scalar_tensor_tensor(N.tmp[:, t % 4], b.Y8[:, t], gain(t), N.inv, ALU.mult, ALU.mult)\
            .then_inc(v.sem["dve_step"], v.up("dve_step"))
        v.eng.wait_ge(v.sem[v.last], v.own())
        name = last if last and t == KD - 1 else "x_ready"
        v.eng.tensor_tensor(b.x[:, t], b.x[:, t], N.tmp[:, t % 4], ALU.add).then_inc(v.sem[name], v.up(name))


def dve_angles(v, pos, inv, quarter, tmp):
    two_pi = 2 * np.pi
    c1 = 6.28125
    c2 = float(np.float32(np.floor((two_pi - c1) * 2 ** 21) / 2 ** 21))
    c3 = float(np.float32(two_pi - c1 - c2))
    ang, n, r = tmp[:, 0], tmp[:, 1], tmp[:, 2]
    v.eng.wait_ge(v.sem[v.last], v.own())
    v.eng.tensor_scalar(ang, pos, inv, None, ALU.mult).then_inc(v.sem["dve_step"], v.up("dve_step"))
    v.eng.wait_ge(v.sem[v.last], v.own())
    v.eng.tensor_scalar(n, ang, float(1 / two_pi), 0.25 * quarter, ALU.mult, ALU.add)\
        .then_inc(v.sem["dve_step"], v.up("dve_step"))
    v.eng.wait_ge(v.sem[v.last], v.own())
    v.eng.tensor_scalar(n, n, 12582912.0, None, ALU.add).then_inc(v.sem["dve_step"], v.up("dve_step"))
    v.eng.wait_ge(v.sem[v.last], v.own())
    v.eng.tensor_scalar(n, n, 12582912.0, None, ALU.subtract).then_inc(v.sem["dve_step"], v.up("dve_step"))
    v.eng.wait_ge(v.sem[v.last], v.own())
    v.eng.scalar_tensor_tensor(r, n, -c1, ang, ALU.mult, ALU.add).then_inc(v.sem["dve_step"], v.up("dve_step"))
    v.eng.wait_ge(v.sem[v.last], v.own())
    v.eng.scalar_tensor_tensor(r, n, -c2, r, ALU.mult, ALU.add).then_inc(v.sem["dve_step"], v.up("dve_step"))
    v.eng.wait_ge(v.sem[v.last], v.own())
    v.eng.scalar_tensor_tensor(r, n, -c3, r, ALU.mult, ALU.add).then_inc(v.sem["dve_step"], v.up("dve_step"))
    if quarter:
        v.eng.wait_ge(v.sem[v.last], v.own())
        v.eng.tensor_scalar(r, r, float(np.pi / 2), None, ALU.add).then_inc(v.sem["dve_step"], v.up("dve_step"))
    v.eng.wait_ge(v.sem[v.last], v.own())
    v.eng.tensor_scalar(tmp[:, 3], r, 3.1415925, -3.1415925, ALU.min, ALU.max).then_inc(v.sem["angle"], v.up("angle"))
    v.eng.wait_ge(v.sem["sine"], v.due("sine"))


def dve_ada(v, n, at):
    b = v.b
    v.eng.wait_ge(v.sem["full_d"], v.due("full_d"))
    ps = v.bank()
    mr = b.col[:, 100:100 + 2 * n] if n <= 8 else b.A_T[:, 0, 0:2 * n]
    v.eng.wait_ge(v.sem[v.last], v.own())
    v.eng.tensor_copy(mr, ps[:, 0:2 * n]).then_inc(v.sem["free_d"], v.up("free_d"))
    pairs = mr.rearrange("p (n two) -> p n two", two=2)
    m = b.mod[:, at:at + n]
    v.eng.wait_ge(v.sem[v.last], v.own())
    v.eng.tensor_tensor(m, pairs[:, :, 0], pairs[:, :, 1], ALU.add).then_inc(v.sem["dve_step"], v.up("dve_step"))
    c0 = b.cols["ada_b"] + at
    v.eng.wait_ge(v.sem[v.last], v.own())
    v.eng.tensor_tensor(m, m, b.par[:, c0:c0 + n], ALU.add).then_inc(v.sem["dve_step"], v.up("dve_step"))


def dve_rwkv(v, j):
    b = v.b
    n = 2 + 3 * j
    for part, dst in enumerate((b.R_R, b.R_K, b.R_V)):
        dve_shift(v, n + part, dst, 8 * part + j)
    v.eng.wait_ge(v.sem["full_d"], v.due("full_d"))
    v.eng.wait_ge(v.sem[v.last], v.own())
    v.eng.tensor_copy(b.R_G, v.bank()).then_inc(v.sem["free_d"], v.up("free_d"))
    v.eng.wait_ge(v.sem["wa_ready"], v.due("wa_ready"))
    for c in range(NQ):
        s = slice(c * P, (c + 1) * P)
        v.eng.wait_ge(v.sem[v.last], v.own())
        v.eng.tensor_tensor_scan(b.R_CUM[:, s], b.ones, b.R_SW[:, s], 0.0, ALU.mult, ALU.add)\
            .then_inc(v.sem["dve_step"], v.up("dve_step"))
    mids = b.R_CUM.rearrange("p (c n) -> p c n", c=NQ)[:, :, P // 2 - 1]
    v.eng.wait_ge(v.sem[v.last], v.own())
    v.eng.tensor_scalar(b.col[:, 164:168], mids, -DECAY, None, ALU.mult).then_inc(v.sem["dve_step"], v.up("dve_step"))
    v.eng.wait_ge(v.sem[v.last], v.own())
    v.eng.tensor_scalar(b.col[:, 160:164], mids, DECAY, None, ALU.mult)\
        .then_inc(v.sem["cum_ready"], v.up("cum_ready"))
    v.eng.wait_ge(v.sem["kk_std"], v.due("kk_std"))
    v.eng.wait_ge(v.sem[v.last], v.own())
    v.eng.tensor_scalar(b.R_SW, b.R_SW, 1e-12, None, ALU.max).then_inc(v.sem["dve_step"], v.up("dve_step"))
    v.eng.wait_ge(v.sem[v.last], v.own())
    v.eng.reciprocal(b.R_SW, b.R_SW).then_inc(v.sem["dve_step"], v.up("dve_step"))
    v.eng.wait_ge(v.sem[v.last], v.own())
    v.eng.scalar_tensor_tensor(b.R_KK, b.R_K, b.pc("k_k", j), b.R_SW, ALU.mult, ALU.mult)\
        .then_inc(v.sem["dve_step"], v.up("dve_step"))
    v.eng.wait_ge(v.sem[v.last], v.own())
    v.eng.tensor_scalar(b.R_KP, b.R_AA, -1.0, b.pc("k_a", j), ALU.add, ALU.mult)\
        .then_inc(v.sem["dve_step"], v.up("dve_step"))
    v.eng.wait_ge(v.sem[v.last], v.own())
    v.eng.scalar_tensor_tensor(b.R_KP, b.R_KP, 1.0, b.R_K, ALU.add, ALU.mult)\
        .then_inc(v.sem["dve_step"], v.up("dve_step"))
    v.eng.wait_ge(v.sem[v.last], v.own())
    v.eng.tensor_tensor(b.R_AA, b.R_KK, b.R_AA, ALU.mult).then_inc(v.sem["dve_step"], v.up("dve_step"))
    v.eng.wait_ge(v.sem["decays"], v.due("decays"))
    chunks = lambda t: t.rearrange("p (c n) -> p c n", c=NQ)
    v.eng.wait_ge(v.sem[v.last], v.own())
    v.eng.scalar_tensor_tensor(b.R_AR[:, :, 0], chunks(b.R_KK), -1.0, b.R_PB[:, :, 0:P], ALU.mult, ALU.mult)\
        .then_inc(v.sem["dve_step"], v.up("dve_step"))
    v.eng.wait_ge(v.sem[v.last], v.own())
    v.eng.tensor_tensor(b.R_AR[:, :, 1], chunks(b.R_R), b.R_PB[:, :, 1:], ALU.mult)\
        .then_inc(v.sem["dve_step"], v.up("dve_step"))
    v.eng.wait_ge(v.sem[v.last], v.own())
    v.eng.tensor_tensor(b.R_BH, b.R_AA, b.R_CUM, ALU.mult).then_inc(v.sem["dve_step"], v.up("dve_step"))
    v.eng.wait_ge(v.sem[v.last], v.own())
    v.eng.tensor_tensor(b.R_KH, b.R_KP, b.R_CUM, ALU.mult).then_inc(v.sem["dve_step"], v.up("dve_step"))
    v.eng.wait_ge(v.sem[v.last], v.own())
    v.eng.tensor_tensor(b.col[:, 172:175], b.R_PB[:, 0:3, P], b.col[:, 169:172], ALU.mult)\
        .then_inc(v.sem["dve_step"], v.up("dve_step"))
    v.eng.wait_ge(v.sem[v.last], v.own())
    v.eng.scalar_tensor_tensor(b.R_T, b.R_R, b.pc("r_k", j), b.R_KP, ALU.mult, ALU.mult)\
        .then_inc(v.sem["rk_ready"], v.up("rk_ready"))
    v.eng.wait_ge(v.sem["full_d"], v.due("full_d"))
    v.eng.wait_ge(v.sem[v.last], v.own())
    v.eng.tensor_tensor(b.R_BV, v.bank(), b.R_V, ALU.mult).then_inc(v.sem["free_d"], v.up("free_d"))
    mask4 = b.const[:, C_MASK4:C_MASK4 + T]
    for u in range(8):
        v.eng.wait_ge(v.sem["full_d"], v.due("full_d"))
        v.eng.wait_ge(v.sem[v.last], v.own())
        v.eng.tensor_tensor(b.R_LM[:, u].rearrange("p m t -> p (m t)"), v.bank(), mask4, ALU.mult)\
            .then_inc(v.sem["free_d"], v.up("free_d"))
    low1, low1t = b.const[:, C_LOW1:C_LOW1 + P], b.const[:, C_LOW1T:C_LOW1T + P]
    eye = v.each(b.ident, 4)
    four = lambda ps: ps.rearrange("p (u t) -> p u t", u=4)
    for g in range(2):
        us = slice(4 * g, 4 * g + 4)
        v.eng.wait_ge(v.sem["full_d"], v.due("full_d"))
        v.eng.wait_ge(v.sem[v.last], v.own())
        v.eng.tensor_tensor(b.R_TN[:, us], four(v.bank()), v.each(low1, 4), ALU.mult)\
            .then_inc(v.sem["free_d"], v.up("free_d"))
        v.eng.wait_ge(v.sem[v.last], v.own())
        v.eng.tensor_tensor(b.R_TN[:, us], b.R_TN[:, us], eye, ALU.add).then_inc(v.sem["dve_step"], v.up("dve_step"))
        v.eng.wait_ge(v.sem[v.last], v.own())
        v.eng.tensor_tensor(b.R_TT[:, us], b.R_LM[:, us, 0], v.each(low1t, 4), ALU.mult)\
            .then_inc(v.sem["dve_step"], v.up("dve_step"))
        v.eng.wait_ge(v.sem[v.last], v.own())
        v.eng.tensor_tensor(b.R_TT[:, us], b.R_TT[:, us], eye, ALU.add)\
            .then_inc(v.sem["t_ready" if g else "dve_step"], v.up("t_ready" if g else "dve_step"))
    for k in range(1, 7):
        level = b.const[:, C_LEVEL + (k - 1) * P:C_LEVEL + k * P]
        for g in range(2):
            us = slice(4 * g, 4 * g + 4)
            v.eng.wait_ge(v.sem["full_d"], v.due("full_d"))
            v.eng.wait_ge(v.sem[v.last], v.own())
            v.eng.tensor_tensor(b.R_Z[:, us], four(v.bank()), v.each(level, 4), ALU.mult)\
                .then_inc(v.sem["free_d"], v.up("free_d"))
        for g in range(2):
            us = slice(4 * g, 4 * g + 4)
            for dst in ((b.R_TN, b.R_TT) if k < 6 else (b.R_TT,)):
                v.eng.wait_ge(v.sem["full_d"], v.due("full_d"))
                v.eng.wait_ge(v.sem[v.last], v.own())
                v.eng.tensor_tensor(dst[:, us], dst[:, us], four(v.bank()), ALU.add)\
                    .then_inc(v.sem["free_d"], v.up("free_d"))
    pre, own = b.R_WU[:, 4], b.R_WU[:, 5]
    for c in range(NQ):
        new, old = b.R_WU[:, 2 + (c + 1) % 2], b.R_WU[:, 2 + c % 2]
        if c < NQ - 1:
            e = b.col[:, 172 + c:173 + c]
            if c:
                v.eng.wait_ge(v.sem[v.last], v.own())
                v.eng.tensor_scalar(pre, old, e, None, ALU.mult).then_inc(v.sem["dve_step"], v.up("dve_step"))
                v.eng.wait_ge(v.sem["full_d"], v.due("full_d"))
                v.eng.wait_ge(v.sem[v.last], v.own())
                v.eng.scalar_tensor_tensor(own, v.bank()[:, 0:P], e, b.pair, ALU.mult, ALU.mult)\
                    .then_inc(v.sem["dve_step"], v.up("dve_step"))
                v.eng.wait_ge(v.sem[v.last], v.own())
                v.eng.tensor_tensor(new, own, pre, ALU.add).then_inc(v.sem["free_d"], v.up("free_d"))
            else:
                v.eng.wait_ge(v.sem["full_d"], v.due("full_d"))
                v.eng.wait_ge(v.sem[v.last], v.own())
                v.eng.scalar_tensor_tensor(new, v.bank()[:, 0:P], e, b.pair, ALU.mult, ALU.mult)\
                    .then_inc(v.sem["free_d"], v.up("free_d"))
        v.eng.wait_ge(v.sem["full_d"], v.due("full_d"))
        v.eng.wait_ge(v.sem[v.last], v.own())
        v.eng.tensor_copy(b.R_Y[:, c * P:(c + 1) * P], v.bank()[:, 0:P]).then_inc(v.sem["free_d"], v.up("free_d"))
    v.eng.wait_ge(v.sem["full_d"], v.due("full_d"))
    v.eng.wait_ge(v.sem[v.last], v.own())
    v.eng.scalar_tensor_tensor(b.R_YC, v.bank(), -1.0 / HD, b.R_Y, ALU.mult, ALU.add)\
        .then_inc(v.sem["free_d"], v.up("free_d"))
    v.eng.wait_ge(v.sem[v.last], v.own())
    v.eng.sem_inc(v.sem["centered"], v.up("centered"))
    v.eng.wait_ge(v.sem["gn_std"], v.due("gn_std"))
    v.eng.wait_ge(v.sem[v.last], v.own())
    v.eng.reciprocal(b.R_SW, b.R_SW).then_inc(v.sem["dve_step"], v.up("dve_step"))
    v.eng.wait_ge(v.sem[v.last], v.own())
    v.eng.scalar_tensor_tensor(b.R_YC, b.R_YC, b.pc("gn_w", j), b.R_SW, ALU.mult, ALU.mult)\
        .then_inc(v.sem["dve_step"], v.up("dve_step"))
    v.eng.wait_ge(v.sem[v.last], v.own())
    v.eng.scalar_tensor_tensor(b.R_YC, b.R_YC, b.pc("gn_b", j), b.R_BV, ALU.add, ALU.add)\
        .then_inc(v.sem["dve_step"], v.up("dve_step"))
    v.eng.wait_ge(v.sem[v.last], v.own())
    v.eng.tensor_tensor(b.R_O, b.R_YC, b.R_G, ALU.mult).then_inc(v.sem["mixed"], v.up("mixed"))
    v.eng.wait_ge(v.sem["act_hi"], v.due("act_hi"))
    v.eng.wait_ge(v.sem[v.last], v.own())
    v.eng.tensor_tensor(b.o_lo[:, j], b.R_O, b.o_hi[:, j].bitcast(F32), ALU.subtract)\
        .then_inc(v.sem["act_lo"], v.up("act_lo"))


def dve_attention(v, us, extra=None):
    b, eng = v.b, v.eng
    base = v.counts.get("e_done", 0)
    for s in range(len(us) + 3):
        if s < len(us):
            u = us[s]
            if base + s - 1 > 0:
                v.eng.wait_ge(v.sem["e_done"], v.value("e_done", base + s - 1))
            if u.masks:
                at = 0
                for m in u.masks:
                    w = m.shape[1]
                    v.eng.wait_ge(v.sem["full_d"], v.due("full_d"))
                    v.eng.wait_ge(v.sem[v.last], v.own())
                    v.eng.tensor_tensor(u.s[:, at:at + w], v.bank()[:, 0:w], m, ALU.add)\
                        .then_inc(v.sem["free_d"], v.up("free_d"))
                    at += w
            elif u.dist is not None:
                v.eng.wait_ge(v.sem["full_d"], v.due("full_d"))
                v.eng.wait_ge(v.sem[v.last], v.own())
                v.eng.scalar_tensor_tensor(u.s, u.dist, -u.slope, v.bank()[:, 0:u.s.shape[1]], ALU.mult, ALU.add)\
                    .then_inc(v.sem["free_d"], v.up("free_d"))
            else:
                v.eng.wait_ge(v.sem["full_d"], v.due("full_d"))
                v.eng.wait_ge(v.sem[v.last], v.own())
                v.eng.tensor_copy(u.s, v.bank()).then_inc(v.sem["free_d"], v.up("free_d"))
            v.eng.wait_ge(v.sem[v.last], v.own())
            eng.tensor_reduce(u.top, u.s, AX, ALU.max).then_inc(v.sem["dve_step"], v.up("dve_step"))
            if u.sink is not None:
                v.eng.wait_ge(v.sem[v.last], v.own())
                v.eng.tensor_tensor(u.top, u.top, u.sink, ALU.max).then_inc(v.sem["dve_step"], v.up("dve_step"))
            v.eng.wait_ge(v.sem[v.last], v.own())
            v.eng.tensor_scalar(u.neg, u.top, -1.0, None, ALU.mult).then_inc(v.sem["s_ready"], v.up("s_ready"))
            if extra:
                extra(s)
        if 0 <= s - 2 < len(us) and us[s - 2].ready == "p_ready" and us[s - 2].v:
            u0, u1 = us[s - 3], us[s - 2]
            if base + s - 1 > 0:
                v.eng.wait_ge(v.sem["e_done"], v.value("e_done", base + s - 1))
            v.eng.wait_ge(v.sem[v.last], v.own())
            v.eng.reciprocal(u0.inv, u0.sum).then_inc(v.sem["dve_step"], v.up("dve_step"))
            v.eng.wait_ge(v.sem[v.last], v.own())
            v.eng.reciprocal(u1.inv, u1.sum).then_inc(v.sem["dve_step"], v.up("dve_step"))
            v.eng.wait_ge(v.sem[v.last], v.own())
            v.eng.tensor_tensor(u1.inv, u1.inv, u1.neg_lam, ALU.mult).then_inc(v.sem["dve_step"], v.up("dve_step"))
            v.eng.wait_ge(v.sem[v.last], v.own())
            v.eng.tensor_scalar(u1.e, u1.e, u1.inv, None, ALU.mult).then_inc(v.sem["dve_step"], v.up("dve_step"))
            v.eng.wait_ge(v.sem[v.last], v.own())
            v.eng.scalar_tensor_tensor(u1.e, u0.e, u0.inv, u1.e, ALU.mult, ALU.add)\
                .then_inc(v.sem["p_ready"], v.up("p_ready"))
        if 0 <= s - 3 < len(us) and us[s - 3].v:
            u = us[s - 3]
            if u.ready == "p_ready":
                v.eng.wait_ge(v.sem["full_d"], v.due("full_d"))
                v.eng.wait_ge(v.sem[v.last], v.own())
                v.eng.tensor_copy(u.o, v.bank()[:, 0:u.width]).then_inc(v.sem["free_d"], v.up("free_d"))
            else:
                if u.sink is not None:
                    v.eng.wait_ge(v.sem[v.last], v.own())
                    v.eng.tensor_tensor(u.sum, u.sum, u.sunk, ALU.add).then_inc(v.sem["dve_step"], v.up("dve_step"))
                v.eng.wait_ge(v.sem[v.last], v.own())
                v.eng.reciprocal(u.inv, u.sum).then_inc(v.sem["dve_step"], v.up("dve_step"))
                v.eng.wait_ge(v.sem["full_d"], v.due("full_d"))
                v.eng.wait_ge(v.sem[v.last], v.own())
                v.eng.tensor_scalar(u.o, v.bank()[:, 0:u.width], u.inv, None, ALU.mult)\
                    .then_inc(v.sem["free_d"], v.up("free_d"))
    v.counts["e_done"] = base + len(us)


def dve_shift(v, n, dst, mu):
    b = v.b
    u = b.R_U[:, n % 2]
    v.eng.wait_ge(v.sem["u_ready"], v.due("u_ready"))
    v.eng.wait_ge(v.sem[v.last], v.own())
    v.eng.tensor_tensor(b.R_T, u[:, 0:T], u[:, 1:T + 1], ALU.subtract).then_inc(v.sem["dve_step"], v.up("dve_step"))
    v.eng.wait_ge(v.sem[v.last], v.own())
    v.eng.scalar_tensor_tensor(dst, b.R_T, b.pc("shift_mu", mu), u[:, 1:T + 1], ALU.mult, ALU.add)\
        .then_inc(v.sem["shifted"], v.up("shifted"))


def dve_head_norms(v, heads, rope=False):
    b, N = v.b, v.b.NH
    for n, (t, gain, rows) in enumerate(heads):
        std = N.std if n % 2 else N.acc
        v.eng.wait_ge(v.sem["head_std"], v.due("head_std"))
        v.eng.wait_ge(v.sem[v.last], v.own())
        v.eng.reciprocal(N.inv[rows], std[rows]).then_inc(v.sem["dve_step"], v.up("dve_step"))
        v.eng.wait_ge(v.sem[v.last], v.own())
        v.eng.scalar_tensor_tensor(t[rows], t[rows], gain[rows], N.inv[rows], ALU.mult, ALU.mult)\
            .then_inc(v.sem["head_normed"], v.up("head_normed"))
    if rope:
        for n, (t, gain, rows) in enumerate(heads):
            v.eng.wait_ge(v.sem["full_d"], v.due("full_d"))
            v.eng.wait_ge(v.sem[v.last], v.own())
            v.eng.tensor_tensor(N.tmp[rows, 0], v.bank()[rows], b.L_SIN[rows], ALU.mult)\
                .then_inc(v.sem["free_d"], v.up("free_d"))
            v.eng.wait_ge(v.sem[v.last], v.own())
            v.eng.tensor_tensor(t[rows], t[rows], b.L_COS[rows], ALU.mult)\
                .then_inc(v.sem["dve_step"], v.up("dve_step"))
            v.eng.wait_ge(v.sem[v.last], v.own())
            v.eng.tensor_tensor(t[rows], t[rows], N.tmp[rows, 0], ALU.add)\
                .then_inc(v.sem["dve_step"], v.up("dve_step"))
    v.eng.wait_ge(v.sem[v.last], v.own())
    v.eng.sem_inc(v.sem["heads_ready"], v.up("heads_ready"))


def dve_branch(v, first):
    b = v.b
    for n in range(KD):
        v.eng.wait_ge(v.sem["gate_ready"], v.due("gate_ready"))
        sg = b.L_SG[:, n % 2]
        if first:
            v.eng.wait_ge(v.sem["full_d"], v.due("full_d"))
            v.eng.wait_ge(v.sem[v.last], v.own())
            v.eng.tensor_tensor(b.L_M[:, n], v.bank(), sg, ALU.mult).then_inc(v.sem["free_d"], v.up("free_d"))
            v.eng.wait_ge(v.sem[v.last], v.own())
            v.eng.sem_inc(v.sem["merged"], v.up("merged"))
        else:
            v.eng.wait_ge(v.sem["full_d"], v.due("full_d"))
            v.eng.wait_ge(v.sem[v.last], v.own())
            v.eng.tensor_tensor(b.NH.tmp[:, 0], v.bank(), sg, ALU.mult).then_inc(v.sem["free_d"], v.up("free_d"))
            v.eng.wait_ge(v.sem[v.last], v.own())
            v.eng.tensor_tensor(b.L_M[:, n], b.L_M[:, n], b.NH.tmp[:, 0], ALU.add)\
                .then_inc(v.sem["merged"], v.up("merged"))


def dve_splits(v, n, lo, src, hi):
    for f in range(n):
        v.eng.wait_ge(v.sem["o_plain"], v.due("o_plain"))
        v.eng.wait_ge(v.sem["act_hi"], v.due("act_hi"))
        v.eng.wait_ge(v.sem[v.last], v.own())
        v.eng.tensor_tensor(lo[:, f], src(f), hi[:, f].bitcast(F32), ALU.subtract)\
            .then_inc(v.sem["act_lo"], v.up("act_lo"))


def dve_setup(v):
    b = v.b
    v.eng.wait_ge(v.sem["positions"], v.due("positions", 16))
    v.eng.wait_ge(v.sem[v.last], v.own())
    v.eng.tensor_copy(b.L_POS, b.L_KR.bitcast(I32)).then_inc(v.sem["dve_step"], v.up("dve_step"))
    for quarter, dst in ((0, b.L_SIN), (1, b.L_COS)):
        dve_angles(v, b.L_POS, b.const[:, C_INV + 1:C_INV + 2], quarter, b.L_DW_TMP)
    inc, strict = b.const[:, C_MASK4 + P:C_MASK4 + 2 * P], b.const[:, C_MASK4:C_MASK4 + P]
    for i in range(NQ):
        v.eng.wait_ge(v.sem[v.last], v.own())
        v.eng.tensor_scalar(b.L_D[:, i], b.L_POS, b.col[:, 180 + i:181 + i], None, ALU.subtract)\
            .then_inc(v.sem["dve_step"], v.up("dve_step"))
        v.eng.wait_ge(v.sem[v.last], v.own())
        v.eng.scalar_tensor_tensor(b.L_D[:, i], b.L_D[:, i], -1.0, b.L_D[:, i], ALU.mult, ALU.max)\
            .then_inc(v.sem["dve_step"], v.up("dve_step"))
    for i in range(NQ):
        own = slice(i * P, (i + 1) * P)
        v.eng.wait_ge(v.sem[v.last], v.own())
        v.eng.tensor_copy(b.L_DW[:, i, P:2 * P], b.L_D[:, i, own]).then_inc(v.sem["dve_step"], v.up("dve_step"))
        if i:
            v.eng.wait_ge(v.sem[v.last], v.own())
            v.eng.tensor_scalar(b.L_DW[:, i, 0:P], inc, NEG, -NEG, ALU.mult, ALU.add)\
                .then_inc(v.sem["dve_step"], v.up("dve_step"))
            v.eng.wait_ge(v.sem[v.last], v.own())
            v.eng.tensor_tensor(b.L_DW[:, i, 0:P], b.L_DW[:, i, 0:P], b.L_D[:, i, (i - 1) * P:i * P], ALU.add)\
                .then_inc(v.sem["dve_step"], v.up("dve_step"))
        if i < NQ - 1:
            v.eng.wait_ge(v.sem[v.last], v.own())
            v.eng.scalar_tensor_tensor(b.L_DW[:, i, 2 * P:], strict, -NEG, b.L_D[:, i, (i + 1) * P:(i + 2) * P], ALU.mult, ALU.add)\
                .then_inc(v.sem["dve_step"], v.up("dve_step"))


def dve_layer(v, l):
    b, N = v.b, v.b.N1
    h, hl = of(b.h_hi, b.h_lo)
    o = of(b.o_hi, b.o_lo)
    g = lambda name: (lambda t: b.pc(name, t, l))
    gq, nlam = b.col[:, 140:146], b.col[:, 150:151]
    for k, (name, scale) in enumerate((("g_mla_q_2", MQ ** -0.5), ("g_diff_q_2", HD ** -0.5),
                                       ("g_win_q_2", HD ** -0.5), ("g_diff_out_2", 1 - LAM0[l]))):
        v.eng.wait_ge(v.sem[v.last], v.own())
        v.eng.tensor_scalar(gq[:, k:k + 1], b.pc(name, 0, l), scale, None, ALU.mult)\
            .then_inc(v.sem["dve_step"], v.up("dve_step"))
    for k in range(2):
        v.eng.wait_ge(v.sem[v.last], v.own())
        v.eng.tensor_tensor(b.col[0:HD, 152 + k:153 + k], b.pc(f"lam_q{k + 1}_2", 0, l)[0:HD], b.pc(f"lam_k{k + 1}_2", 0, l)[0:HD], ALU.mult)\
            .then_inc(v.sem["lam_parts" if k else "dve_step"], v.up("lam_parts" if k else "dve_step"))
    v.eng.wait_ge(v.sem["lam_exp"], v.due("lam_exp"))
    v.eng.wait_ge(v.sem[v.last], v.own())
    v.eng.scalar_tensor_tensor(nlam, b.col[:, 155:156], -LAM0[l], b.col[:, 154:155], ALU.add, ALU.subtract)\
        .then_inc(v.sem["dve_step"], v.up("dve_step"))
    dve_norm_split(v, N, KD, lambda t: b.x[:, t], g("g_mix_2"), h, hl)
    s_hi, s_lo = of(b.s_hi, b.s_lo)
    dve_norm_split(v, N, 2, lambda t: b.L_C[:, t], g("g_q_lora_2"), s_hi, s_lo)
    kv = of(b.s_hi, b.s_lo, 2)
    dve_norm_split(v, N, 1, lambda t: b.L_C[:, 2], g("g_kv_lora_2"), *kv)
    for half in range(2):
        dve_head_norms(v, mla_heads(b, l), rope=True)
        dve_attention(v, columns(units_mla(b, half), b))
    v.eng.wait_ge(v.sem[v.last], v.own())
    v.eng.sem_inc(v.sem["o_done"], v.up("o_done"))
    dve_splits(v, 4, b.o_lo, lambda f: b.L_E[:, f], b.o_hi)
    dve_branch(v, True)
    dve_head_norms(v, diff_heads(b, l))
    dve_attention(v, columns(units_diff(b, nlam), b))
    ss = b.col[:, 100:116]
    for i in range(NQ):
        for k in range(DH):
            u = b.L_O[:, i, k * DV:(k + 1) * DV]
            v.eng.wait_ge(v.sem[v.last], v.own())
            v.eng.tensor_tensor_reduce(out=b.NH.tmp[:, 0, 0:DV], in0=u, in1=u, scale=1.0, scalar=0.0, op0=ALU.mult, op1=ALU.add, accum_out=ss[:, NQ * i + k:NQ * i + k + 1])\
                .then_inc(v.sem["dve_step"], v.up("dve_step"))
    v.eng.wait_ge(v.sem[v.last], v.own())
    v.eng.sem_inc(v.sem["out_squares"], v.up("out_squares"))
    v.eng.wait_ge(v.sem["out_std"], v.due("out_std"))
    v.eng.wait_ge(v.sem[v.last], v.own())
    v.eng.reciprocal(ss, ss).then_inc(v.sem["dve_step"], v.up("dve_step"))
    v.eng.wait_ge(v.sem[v.last], v.own())
    v.eng.tensor_tensor(b.L_O.rearrange("p q (h n) -> p (q h) n", h=DH), b.L_O.rearrange("p q (h n) -> p (q h) n", h=DH), ss.unsqueeze(2).to_broadcast([P, NQ * DH, DV]), ALU.mult)\
        .then_inc(v.sem["dve_step"], v.up("dve_step"))
    v.eng.wait_ge(v.sem[v.last], v.own())
    v.eng.sem_inc(v.sem["o_done"], v.up("o_done"))
    dve_splits(v, 4, b.o_lo, lambda f: b.L_E[:, f], b.o_hi)
    dve_branch(v, False)
    dve_head_norms(v, win_heads(b, l))
    dve_attention(v, columns(units_win(b, l), b))
    v.eng.wait_ge(v.sem[v.last], v.own())
    v.eng.sem_inc(v.sem["o_done"], v.up("o_done"))
    dve_splits(v, 4, b.o_lo, lambda f: b.L_E[:, f], b.o_hi)
    dve_branch(v, False)
    for n in range(KD):
        v.eng.wait_ge(v.sem["act_hi"], v.due("act_hi"))
        v.eng.wait_ge(v.sem[v.last], v.own())
        v.eng.tensor_tensor(b.h_lo[:, n], b.L_M[:, n], b.h_hi[:, n].bitcast(F32), ALU.subtract)\
            .then_inc(v.sem["act_lo"], v.up("act_lo"))
    for n in range(KD):
        v.eng.wait_ge(v.sem["full_d"], v.due("full_d"))
        v.eng.wait_ge(v.sem[v.last], v.own())
        v.eng.tensor_tensor(b.x[:, n], b.x[:, n], v.bank(), ALU.add).then_inc(v.sem["free_d"], v.up("free_d"))
        v.eng.wait_ge(v.sem[v.last], v.own())
        v.eng.sem_inc(v.sem["x_ready"], v.up("x_ready"))
    v.eng.wait_ge(v.sem[v.last], v.own())
    v.eng.memset(b.F_G[:, :, 0:1], 0.0).then_inc(v.sem["dve_step"], v.up("dve_step"))
    v.eng.wait_ge(v.sem[v.last], v.own())
    v.eng.memset(b.F_G[:, :, T + 1:T + 2], 0.0).then_inc(v.sem["mlp_clear"], v.up("mlp_clear"))
    dve_norm_split(v, N, KD, lambda t: b.x[:, t], g("g_ffn_2"), h, hl)

    def hidden(n):
        G = b.F_G[:, n % 2]
        v.eng.wait_ge(v.sem["gu_ready"], v.due("gu_ready"))
        v.eng.wait_ge(v.sem[v.last], v.own())
        v.eng.tensor_scalar(b.F_C, G[:, 0:T], b.pc("conv_w_2", n, l), None, ALU.mult)\
            .then_inc(v.sem["dve_step"], v.up("dve_step"))
        v.eng.wait_ge(v.sem[v.last], v.own())
        v.eng.scalar_tensor_tensor(b.F_C, G[:, 1:T + 1], b.pc("conv_w_2", 22 + n, l), b.F_C, ALU.mult, ALU.add)\
            .then_inc(v.sem["dve_step"], v.up("dve_step"))
        v.eng.wait_ge(v.sem[v.last], v.own())
        v.eng.scalar_tensor_tensor(b.F_C, G[:, 2:T + 2], b.pc("conv_w_2", 44 + n, l), b.F_C, ALU.mult, ALU.add)\
            .then_inc(v.sem["conv"], v.up("conv"))
        v.eng.wait_ge(v.sem["gelu"], v.due("gelu"))
        v.eng.wait_ge(v.sem[v.last], v.own())
        v.eng.tensor_tensor(b.F_F, b.F_A, b.F_U[:, n % 2], ALU.mult).then_inc(v.sem["f_ready"], v.up("f_ready"))
        v.eng.wait_ge(v.sem["act_hi"], v.due("act_hi"))
        v.eng.wait_ge(v.sem[v.last], v.own())
        v.eng.tensor_tensor(b.o_lo[:, n % 4], b.F_F, b.o_hi[:, n % 4].bitcast(F32), ALU.subtract)\
            .then_inc(v.sem["hid_lo"], v.up("hid_lo"))

    groups = FF2 // P // 2
    for grp in range(groups + 1):
        if grp < groups:
            hidden(2 * grp)
            hidden(2 * grp + 1)
        if grp:
            for n in range(KD):
                v.eng.wait_ge(v.sem["full_d"], v.due("full_d"))
                v.eng.wait_ge(v.sem[v.last], v.own())
                v.eng.tensor_tensor(b.x[:, n], b.x[:, n], v.bank(), ALU.add).then_inc(v.sem["free_d"], v.up("free_d"))
                if grp == groups:
                    v.eng.wait_ge(v.sem[v.last], v.own())
                    v.eng.sem_inc(v.sem["x_ready"], v.up("x_ready"))
    for t in range(2):
        v.eng.wait_ge(v.sem["act_hi"], v.due("act_hi"))
        v.eng.wait_ge(v.sem[v.last], v.own())
        v.eng.tensor_tensor(b.s_lo[:, t], b.L_PE[:, t], b.s_hi[:, t].bitcast(F32), ALU.subtract)\
            .then_inc(v.sem["act_lo"], v.up("act_lo"))
    for n in range(KD):
        v.eng.wait_ge(v.sem["full_d"], v.due("full_d"))
        v.eng.wait_ge(v.sem[v.last], v.own())
        v.eng.tensor_copy(b.Y8[:, n], v.bank()).then_inc(v.sem["free_d"], v.up("free_d"))
        v.eng.wait_ge(v.sem[v.last], v.own())
        v.eng.sem_inc(v.sem["y_ready"], v.up("y_ready"))
    dve_norm(v, N, KD)
    for t in range(KD):
        v.eng.wait_ge(v.sem[v.last], v.own())
        v.eng.scalar_tensor_tensor(b.Y8[:, t], b.Y8[:, t], b.pc("g_ple_2", t, l), N.inv, ALU.mult, ALU.mult)\
            .then_inc(v.sem["dve_step"], v.up("dve_step"))
    dve_norm_split(v, N, KD, lambda t: b.x[:, t], g("g_ple_in_2"), h, hl)
    for n in range(KD):
        v.eng.wait_ge(v.sem["gate_ready"], v.due("gate_ready"))
        v.eng.wait_ge(v.sem[v.last], v.own())
        v.eng.tensor_tensor(N.tmp[:, 0], b.F_SG[:, n % 2], b.Y8[:, n], ALU.mult)\
            .then_inc(v.sem["merged"], v.up("merged"))
        v.eng.wait_ge(v.sem[v.last], v.own())
        v.eng.tensor_tensor(b.x[:, n], b.x[:, n], N.tmp[:, 0], ALU.add)\
            .then_inc(v.sem["x_final" if l == LAYERS - 1 and n == KD - 1 else "x_ready"], v.up("x_final" if l == LAYERS - 1 and n == KD - 1 else "x_ready"))


def dve_program(eng, sig, b):
    v = Dve(eng, sig, b)
    eng.sem_inc(sig["free_d"], BANKS)
    v.raised["free_d"] = BANKS
    gain = lambda at: (lambda t: b.col[:, at + t:at + t + 1])
    v.eng.wait_ge(v.sem["loaded"], v.due("loaded", NLOAD * 16))
    v.eng.wait_ge(v.sem["sigmoid_c"], v.due("sigmoid_c"))
    v.eng.tensor_tensor(b.col[:, 0:8], b.col[:, 0:8], b.pcs("c", KD), ALU.mult)\
        .then_inc(v.sem["dve_step"], v.up("dve_step"))
    v.eng.wait_ge(v.sem[v.last], v.own())
    v.eng.tensor_copy(b.c_pair[:, :, 0], b.col[:, 0:8]).then_inc(v.sem["dve_step"], v.up("dve_step"))
    v.eng.wait_ge(v.sem[v.last], v.own())
    v.eng.tensor_tensor(b.c_pair[:, :, 1], b.col[:, 0:8], b.c_pair[:, :, 0].bitcast(F32), ALU.subtract)\
        .then_inc(v.sem["c_ready"], v.up("c_ready"))
    pos = b.Y8[:, 7]
    v.eng.wait_ge(v.sem[v.last], v.own())
    v.eng.tensor_copy(pos, b.posrow_i).then_inc(v.sem["dve_step"], v.up("dve_step"))
    v.eng.wait_ge(v.sem[v.last], v.own())
    v.eng.tensor_copy(b.col[:, 180:184], b.posi[:, :]).then_inc(v.sem["dve_step"], v.up("dve_step"))
    v.eng.wait_ge(v.sem[v.last], v.own())
    v.eng.tensor_copy(b.col[:, 184:188], b.col[:, 180:184]).then_inc(v.sem["dve_step"], v.up("dve_step"))
    for quarter in (0, 1):
        dve_angles(v, pos, b.const[:, C_INV:C_INV + 1], quarter, b.A_T)
    dve_ada(v, 2 * KD, 0)
    v.eng.wait_ge(v.sem[v.last], v.own())
    v.eng.scalar_tensor_tensor(b.col[:, 16:24], b.mod[:, 8:16], 1.0, b.pcs("norm_mix_pre", KD), ALU.add, ALU.mult)\
        .then_inc(v.sem["dve_step"], v.up("dve_step"))
    h, hl = of(b.h_hi, b.h_lo)
    dve_norm_split(v, b.N0, KD, lambda t: b.x[:, t], gain(16), h, hl, bias=lambda t: b.mod[:, t:t + 1])
    for n in range(12):
        t = (b.A_Q if n < 6 else b.A_K)[:, n % 6]
        v.eng.wait_ge(v.sem["full_d"], v.due("full_d"))
        v.eng.wait_ge(v.sem[v.last], v.own())
        v.eng.tensor_tensor(b.A_T[:, n % 4], v.bank(), b.A_SN, ALU.mult).then_inc(v.sem["free_d"], v.up("free_d"))
        v.eng.wait_ge(v.sem[v.last], v.own())
        v.eng.tensor_tensor(t, t, b.A_C, ALU.mult).then_inc(v.sem["dve_step"], v.up("dve_step"))
        v.eng.wait_ge(v.sem[v.last], v.own())
        v.eng.tensor_tensor(t, t, b.A_T[:, n % 4], ALU.add)\
            .then_inc(v.sem["qk_ready" if n == 11 else "dve_step"], v.up("qk_ready" if n == 11 else "dve_step"))
    dve_attention(v, columns(units_1(b), b), extra=lambda s: dve_ada(v, 2, 16 + 2 * s))
    v.eng.wait_ge(v.sem[v.last], v.own())
    v.eng.scalar_tensor_tensor(b.col[:, 24:32], b.mod[:, 32:40], 1.0, b.pcs("norm_ffn_pre", KD), ALU.add, ALU.mult)\
        .then_inc(v.sem["dve_step"], v.up("dve_step"))
    v.eng.wait_ge(v.sem[v.last], v.own())
    v.eng.tensor_tensor(b.mod[:, 16:24], b.mod[:, 16:24], b.pcs("norm_mix_post", KD), ALU.mult)\
        .then_inc(v.sem["dve_step"], v.up("dve_step"))
    v.eng.wait_ge(v.sem[v.last], v.own())
    v.eng.tensor_tensor(b.mod[:, 40:48], b.mod[:, 40:48], b.pcs("norm_ffn_post", KD), ALU.mult)\
        .then_inc(v.sem["dve_step"], v.up("dve_step"))
    for f in range(2):
        v.eng.wait_ge(v.sem["o_plain"], v.due("o_plain"))
        v.eng.wait_ge(v.sem["act_hi"], v.due("act_hi"))
        v.eng.wait_ge(v.sem[v.last], v.own())
        v.eng.tensor_tensor(b.s_lo[:, 2 + f], b.A_T[:, f], b.s_hi[:, 2 + f].bitcast(F32), ALU.subtract)\
            .then_inc(v.sem["act_lo"], v.up("act_lo"))
    v.eng.wait_ge(v.sem[v.last], v.own())
    eng.memset(b.R_U[:, :, 0:1], 0.0).then_inc(v.sem["rwkv_clear"], v.up("rwkv_clear"))
    dve_shift(v, 0, b.R_K, 24)
    dve_shift(v, 1, b.R_V, 25)
    for n, src in enumerate((b.R_K, b.R_V)):
        v.eng.wait_ge(v.sem["lora_act"], v.due("lora_act"))
        v.eng.wait_ge(v.sem["act_hi"], v.due("act_hi"))
        v.eng.wait_ge(v.sem[v.last], v.own())
        v.eng.tensor_tensor(b.s_lo[:, n], src, b.s_hi[:, n].bitcast(F32), ALU.subtract)\
            .then_inc(v.sem["act_lo"], v.up("act_lo"))
    for j in range(KD):
        dve_rwkv(v, j)
    v.eng.wait_ge(v.sem[v.last], v.own())
    v.eng.sem_inc(v.sem["mix_clear"], v.up("mix_clear"))
    for n in range(KD):
        v.eng.wait_ge(v.sem["gate_ready"], v.due("gate_ready"))
        sg = [b.G_SG[:, 2 * (n % 2) + part] for part in range(2)]
        v.eng.wait_ge(v.sem["full_d"], v.due("full_d"))
        v.eng.wait_ge(v.sem[v.last], v.own())
        v.eng.tensor_tensor(b.F_T, v.bank(), sg[0], ALU.mult).then_inc(v.sem["free_d"], v.up("free_d"))
        v.eng.wait_ge(v.sem["full_d"], v.due("full_d"))
        v.eng.wait_ge(v.sem[v.last], v.own())
        v.eng.tensor_tensor(b.G_M[:, n], v.bank(), sg[1], ALU.mult).then_inc(v.sem["free_d"], v.up("free_d"))
        v.eng.wait_ge(v.sem[v.last], v.own())
        v.eng.tensor_tensor(b.G_M[:, n], b.G_M[:, n], b.F_T, ALU.add).then_inc(v.sem["merged"], v.up("merged"))
    for n in range(KD):
        v.eng.wait_ge(v.sem["act_hi"], v.due("act_hi"))
        v.eng.wait_ge(v.sem[v.last], v.own())
        v.eng.tensor_tensor(b.h_lo[:, n], b.G_M[:, n], b.h_hi[:, n].bitcast(F32), ALU.subtract)\
            .then_inc(v.sem["act_lo"], v.up("act_lo"))
    for n in range(KD):
        v.eng.wait_ge(v.sem["full_d"], v.due("full_d"))
        v.eng.wait_ge(v.sem[v.last], v.own())
        v.eng.tensor_copy(b.Y8[:, n], v.bank()).then_inc(v.sem["free_d"], v.up("free_d"))
        v.eng.wait_ge(v.sem[v.last], v.own())
        v.eng.sem_inc(v.sem["y_ready"], v.up("y_ready"))
    dve_norm_add(v, b.N1, lambda t: b.mod[:, 16 + t:17 + t])
    dve_norm_split(v, b.N1, KD, lambda t: b.x[:, t], gain(24), h, hl, bias=lambda t: b.mod[:, 24 + t:25 + t])

    def lows(g):
        for n in range(4):
            at = (4 * g + n) % 8
            v.eng.wait_ge(v.sem["hid_hi"], v.due("hid_hi"))
            v.eng.wait_ge(v.sem[v.last], v.own())
            v.eng.tensor_tensor(b.F_T, b.F_R[:, n], b.F_R[:, n], ALU.mult)\
                .then_inc(v.sem["dve_step"], v.up("dve_step"))
            v.eng.wait_ge(v.sem[v.last], v.own())
            v.eng.tensor_tensor(b.o_lo[:, at], b.F_T, b.o_hi[:, at].bitcast(F32), ALU.subtract)\
                .then_inc(v.sem["hid_lo"], v.up("hid_lo"))

    def downs(g):
        for n in range(KD):
            if g:
                v.eng.wait_ge(v.sem["full_d"], v.due("full_d"))
                v.eng.wait_ge(v.sem[v.last], v.own())
                v.eng.tensor_tensor(b.Y8[:, n], b.Y8[:, n], v.bank(), ALU.add)\
                    .then_inc(v.sem["free_d"], v.up("free_d"))
            else:
                v.eng.wait_ge(v.sem["full_d"], v.due("full_d"))
                v.eng.wait_ge(v.sem[v.last], v.own())
                v.eng.tensor_copy(b.Y8[:, n], v.bank()).then_inc(v.sem["free_d"], v.up("free_d"))
            if g == FF1 // P // 4 - 1:
                v.eng.wait_ge(v.sem[v.last], v.own())
                v.eng.sem_inc(v.sem["y_ready"], v.up("y_ready"))

    lows(0)
    for g in range(FF1 // P // 4 - 1):
        lows(g + 1)
        downs(g)
    downs(FF1 // P // 4 - 1)
    dve_norm_add(v, b.N1, lambda t: b.mod[:, 40 + t:41 + t])
    dve_setup(v)
    for l in range(LAYERS):
        dve_layer(v, l)


NLOAD = 6


def build(nc, ins, out, plan):
    blocks = len(plan) // TILES
    cols, ncols = param_columns()
    with ExitStack() as ctx:
        b = Buffers(nc, ctx, ncols, cols)
        sig = Signals(nc, ctx)
        for name in ([f"raw_loaded{s}" for s in range(RAW)]
                     + ["w_ready", "w_used", "w_high", "x_final", "stored", "loaded", "c_ready", "free_a", "free_d",
                        "full_a", "full_d"]):
            sig[name]
        block = ctx.enter_context(nc.Block())

        @block.sync
        def _(eng):
            w = ins["weights"]
            for s in range(RAW):
                eng.dma_start(b.raw[:, s], w[s]).then_inc(sig[f"raw_loaded{s}"], 16)
            with eng.Fori(1, blocks // RAW) as i:
                for s in range(RAW):
                    eng.wait_ge(sig["w_ready"], i * RAW + (s + 1 - RAW))
                    eng.dma_start(b.raw[:, s], w[i * RAW + s]).then_inc(sig[f"raw_loaded{s}"], 16)
            eng.wait_ge(sig["x_final"], 1)
            eng.dma_start(out.rearrange("(k p) t -> p k t", p=P), b.x[:, :, :]).then_inc(sig["stored"], 16)
            eng.wait_ge(sig["stored"], 16)

        @block.gpsimd
        def _(eng):
            def split(i, s, used):
                eng.wait_ge(sig[f"raw_loaded{s}"], i * 16 + 16)
                if used is not None:
                    eng.wait_ge(sig["w_used"], used)
                hi, lo = b.w_hi[:, s % SPLIT], b.w_lo[:, s % SPLIT]
                if used is not None:
                    eng.tensor_tensor(b.mark[:, 1:2], b.mark[:, 0:1], b.mark[:, 0:1], ALU.add)
                eng.tensor_scalar(hi, b.raw[:, s], 1.0, 0.0, ALU.mult, ALU.add).then_inc(sig["w_high"], 1)
                eng.wait_ge(sig["w_high"], i * RAW + s + 2)
                eng.tensor_tensor(lo, b.raw[:, s], hi.bitcast(F32), ALU.subtract).then_inc(sig["w_ready"], 1)

            eng.memset(b.mark[:, :], 0.0).then_inc(sig["w_high"], 1)
            eng.wait_ge(sig["w_high"], 1)
            for s in range(RAW):
                split(0, s, s - SPLIT + 1 if s >= SPLIT else None)
            with eng.Fori(1, blocks // RAW) as i:
                for s in range(RAW):
                    split(i, s, i * RAW + (s - SPLIT + 1))

        @block.tensor
        def _(eng):
            pe_program(eng, sig, b, plan)

        @block.scalar
        def _(eng):
            act_program(eng, sig, b, ins)

        @block.vector
        def _(eng):
            dve_program(eng, sig, b)


def pack_weights(inputs, plan):
    w = np.zeros((len(plan) // TILES, P, TILES, P), np.float32)
    for t, (_, pieces) in enumerate(plan):
        for name, layer, row, rows, col, cols, at_row, at_col in pieces:
            w[t // TILES, at_row:at_row + rows, t % TILES, at_col:at_col + cols] = \
                inputs[name][layer][row:row + rows, col:col + cols]
    return w.reshape(len(plan) // TILES, P, TILES * P)


def pack_params(inputs):
    cols, n = param_columns()
    p = np.zeros((P, n), np.float32)

    def put(at, v):
        v = np.asarray(v).reshape(-1)
        if v.size == HD:
            v = np.concatenate([v, v])
        if v.size < P:
            p[:v.size, at] = v
        else:
            p[:, at:at + v.size // P] = v.reshape(-1, P).T

    for key, at in cols.items():
        if isinstance(key, str):
            put(at, inputs[key] if key == "c" else inputs[key][0])
        elif key[0] == "win_sink_2":
            p[:, at:at + WH] = inputs[key[0]][key[1]][None, :]
        else:
            put(at, inputs[key[0]][key[1]])
    return p


def kernel(**inputs):
    import concourse.bacc as bacc
    from concourse.bass_utils import run_bass_kernel_spmd

    plan = weight_plan()
    inputs = {k: np.asarray(v) for k, v in inputs.items()}
    const, masks = constants()
    positions = inputs["positions"][0], inputs["positions_2"][0]
    arrays = {
        "weights": pack_weights(inputs, plan),
        "params": pack_params(inputs),
        "const": const,
        "masks": masks,
        "x": np.ascontiguousarray(inputs["x"][0].T),
        "pe": np.ascontiguousarray(inputs["p_2"][:, 0].transpose(0, 2, 1)),
        "pos_rows": np.ascontiguousarray(np.broadcast_to(positions[0], (P, T))),
        "pos_rows_2": np.ascontiguousarray(np.broadcast_to(positions[1], (P, T))),
        "pos_cols": np.ascontiguousarray(positions[1].reshape(NQ, P).T),
    }
    nc = bacc.Bacc("TRN2", target_bir_lowering=False, num_devices=1, dynamic_dma_scratch_size=1024)
    ins = {k: nc.dram_tensor(f"in_{k}", a.shape, mybir.dt.from_np(a.dtype), kind="ExternalInput").ap()
           for k, a in arrays.items()}
    out = nc.dram_tensor("out", (D, T), F32, kind="ExternalOutput").ap()
    build(nc, ins, out, plan)
    r = run_bass_kernel_spmd(nc, [{f"in_{k}": a for k, a in arrays.items()}], core_ids=[0])
    return np.ascontiguousarray(r.results[0]["out"].T)[None]
```

```python
from contextlib import ExitStack

import numpy as np

import concourse.bass as bass
from concourse import mybir

F32 = mybir.dt.float32
F32R = mybir.dt.float32r
I32 = mybir.dt.int32
ALU = mybir.AluOpType
ACT = mybir.ActivationFunctionType
AX = mybir.AxisListType.X

P = 128
T = 512
NQ = T // P
D = 1024
KD = D // P
TILES = 8
RAW = 2
SPLIT = 2
BANKS = 4
ARENA = 45

AH, HD = 12, 64
AW = AH * HD
GH = 4
FF1 = 4096
LORA = 64
EPS = 1e-6
GN_EPS = 64e-5
DECAY = float(np.exp(-0.5))
LAYERS = 2
MH, NOPE, ROPE, MV = 8, 64, 32, 64
MQ = NOPE + ROPE
QR, KVR = 256, 128
DH, DV = 4, 128
WH, WKV = 8, 2
BW = 512
FF2 = 2816
PLE = 256
KRV = (1, 0, 2)
ADA_FIRST = 2 * D // T
NEG = -1e30
FLOOR = -3.4e38
G_MLA = (3, 3, 0, 1, 1)
G_DIFF = (4, 2, 1, 1)
G_WIN = (3, 3, 1, 1)
LAG_MLA, LAG_DIFF, LAG_WIN = 2, 4, 2
SLOPES = [2.0 ** (-8.0 * (n + 1) / (DH + WH)) for n in range(DH + WH)]
LAM0 = [0.8 - 0.6 * float(np.exp(-0.3 * n)) for n in range(LAYERS)]


def tile_of(name, layer, row, col, rows=P, cols=P, at_row=0, at_col=0):
    return (name, layer, row, rows, col, cols, at_row, at_col)


def weight_plan():
    plan = []

    def mat(tag, name, layer, col, k=KD, row=0):
        for t in range(k):
            plan.append((tag, [tile_of(name, layer, row + t * P, col)]))

    def pad():
        while len(plan) % TILES:
            plan.append(("pad", []))

    def ada(g):
        for t in range(KD):
            for n in range(4):
                plan.append(("ada", [tile_of("ada_w", 0, t * P, (4 * g + n) * P)]))

    for g in range(ADA_FIRST):
        ada(g)
    for n in range(2 * AW // P):
        mat("qk", "w_in", 0, n * P)
    for t in range(KD):
        for n in range(4):
            plan.append(("v4", [tile_of("w_in", 0, t * P, 2 * AW + n * P)]))
    for t in range(KD):
        for n in range(4, 6):
            plan.append(("v2", [tile_of("w_in", 0, t * P, 2 * AW + n * P)]))
    for g in range(ADA_FIRST, 6 * D // T):
        ada(g)
    r0 = 3 * AW
    mat("lora", "w_in", 0, r0 + 3 * D)
    mat("lora", "w_in", 0, r0 + 3 * D + P)
    for j in range(KD):
        plan.append(("w2", [tile_of("decay_w2", 0, 0, j * P, rows=LORA)]))
        plan.append(("a2", [tile_of("iclr_a2", 0, 0, j * P, rows=LORA, at_row=LORA)]))
        for part in KRV:
            mat("rkv", "w_in", 0, r0 + part * D + j * P)
        plan.append(("g2", [tile_of("gate_g2", 0, 0, j * P)]))
    g0 = r0 + 3 * D + 2 * P
    for n in range(KD):
        mat("gate", "w_in", 0, g0 + n * P)
        mat("gate", "w_in", 0, g0 + D + n * P)
        mat("branch", "w_branch", 0, n * P, k=2)
        mat("branch", "w_branch", 0, n * P, row=2 * P)
    for n in range(KD):
        mat("out", "w_out", 0, n * P)
    G1 = 4

    def up1(g):
        for n in range(G1):
            mat("up1", "w_ff1", 0, (g * G1 + n) * P)

    def down1(g):
        for n in range(KD):
            mat("down1", "w_ff2", 0, n * P, k=G1, row=g * G1 * P)

    up1(0)
    for g in range(FF1 // P // G1 - 1):
        up1(g + 1)
        down1(g)
    down1(FF1 // P // G1 - 1)

    for l in range(LAYERS):
        assert len(plan) % TILES == 0
        for n in range(3):
            mat("c", "w_in_2", l, n * P)
        for t in range(KD):
            plan.append(("kr", [tile_of("w_in_2", l, t * P, QR + KVR, cols=ROPE, at_col=NOPE)]))
        c0 = QR + KVR + ROPE
        gates = c0 + 3 * 512 + 512 + 256

        def gate(b, n0, n):
            for k in range(n0, n0 + n):
                mat("gate2", "w_in_2", l, gates + b * D + k * P)

        for half in range(2):
            for h in range(4 * half, 4 * half + 4):
                for t in range(2):
                    plan.append(("uq", [tile_of("w_uq_2", l, t * P, h * MQ, cols=MQ)]))
                plan.append(("uk", [tile_of("w_ukv_2", l, 0, h * P, cols=NOPE)]))
            for hp in range(2 * half, 2 * half + 2):
                plan.append(("uv", [tile_of("w_ukv_2", l, 0, (2 * hp + i) * P + NOPE, cols=MV, at_col=i * MV)
                                    for i in range(2)]))
            if half:
                gate(0, G_MLA[0], KD - G_MLA[0])
                pad()
            else:
                gate(0, 0, G_MLA[0])

        def branch(b):
            for n in range(KD):
                for t in range(BW // P):
                    plan.append(("branch2", [("w_branch_2", (l, b), t * P, P, n * P, P, 0, 0)]))

        branch(0)
        for n in range(8):
            mat("dqk", "w_in_2", l, c0 + n * P)
        for t in range(KD):
            for n in range(4):
                plan.append(("dv", [tile_of("w_in_2", l, t * P, c0 + 1024 + n * P)]))
        gate(1, 0, KD)
        branch(1)
        for n in range(4):
            mat("sqk", "w_in_2", l, c0 + 1536 + n * P)
        for kv in range(WKV):
            for t in range(KD):
                plan.append(("sqk", [tile_of("w_in_2", l, t * P, c0 + 2048 + kv * HD, cols=HD, at_col=i * HD)
                                     for i in range(2)]))
        mat("sv", "w_in_2", l, c0 + 1536 + 640)
        gate(2, 0, KD)
        branch(2)
        for n in range(KD):
            mat("out2", "w_out_2", l, n * P)

        def up2(g):
            for n in range(2):
                mat("gate_up", "w_ffn_gate_2", l, (2 * g + n) * P)
                mat("gate_up", "w_ffn_up_2", l, (2 * g + n) * P)

        def down2(g):
            for n in range(KD):
                mat("down2", "w_ffn_down_2", l, n * P, k=2, row=2 * g * P)

        up2(0)
        for g in range(FF2 // P // 2 - 1):
            up2(g + 1)
            down2(g)
        down2(FF2 // P // 2 - 1)
        for n in range(KD):
            mat("ple", "w_ple_proj_2", l, n * P, k=2)
        for n in range(KD):
            mat("pgate", "w_ple_gate_2", l, n * P)
    while len(plan) % (RAW * TILES):
        plan.append(("pad", []))
    return plan


def param_columns():
    at, n = {}, 0
    for name, cols in [("c", 8), ("ada_b", 48), ("norm_mix_pre", 8), ("norm_mix_post", 8), ("norm_ffn_pre", 8),
                       ("norm_ffn_post", 8), ("shift_mu", 26), ("decay_w0", 8), ("iclr_a0", 8), ("k_k", 8),
                       ("k_a", 8), ("r_k", 8), ("gn_w", 8), ("gn_b", 8)]:
        at[name] = n
        n += cols
    for name, cols in [("g_mix_2", 8), ("g_q_lora_2", 2), ("g_kv_lora_2", 1), ("g_mla_q_2", 1), ("g_mla_k_2", 1),
                       ("g_diff_q_2", 1), ("g_diff_k_2", 1), ("lam_q1_2", 1), ("lam_k1_2", 1), ("lam_q2_2", 1),
                       ("lam_k2_2", 1), ("g_diff_out_2", 1), ("g_win_q_2", 1), ("g_win_k_2", 1), ("win_sink_2", 8),
                       ("g_ffn_2", 8), ("conv_w_2", 66), ("conv_b_2", 22), ("g_ple_2", 8), ("g_ple_in_2", 8)]:
        for l in range(LAYERS):
            at[name, l] = n
            n += cols
    return at, n


C_IDENT, C_ONES, C_PAIR, C_MASK4, C_LOW1, C_LOW1T, C_LEVEL = 0, 128, 256, 384, 896, 1024, 1152
C_PERM1, C_PERM2 = 1152 + 6 * 128, 1152 + 7 * 128
C_INV = 1152 + 8 * 128
C_END = C_INV + 8
M_NEAR, M_MOD4, M_MOD16, M_BAND, M_END = 0, 256, 768, 1280, 1664


def constants():
    c = np.zeros((P, C_END), np.float32)
    i = np.arange(P)
    row, col = i[:, None], i[None, :]
    c[:, C_IDENT:C_IDENT + P] = row == col
    c[:, C_ONES:C_ONES + P] = 1.0
    c[:, C_PAIR:C_PAIR + P] = row // HD == col // HD
    c[:, C_MASK4:C_MASK4 + 512] = np.concatenate([col > row, col >= row] * 2, 1)
    low1 = (row // 2 == col // 2) & (row > col)
    c[:, C_LOW1:C_LOW1 + P] = low1
    c[:, C_LOW1T:C_LOW1T + P] = low1.T
    for k in range(1, 7):
        h = 1 << k
        m = (row // (2 * h) == col // (2 * h)) & (row // h % 2 == 1) & (col // h % 2 == 0)
        c[:, C_LEVEL + (k - 1) * P:C_LEVEL + k * P] = m
    for m in range(P):
        if m % HD < 8:
            c[m + 8, C_PERM1 + m] = -1.0
        elif m % HD < 16:
            c[m - 8, C_PERM1 + m] = 1.0
        if 64 <= m < 80:
            c[m + 16, C_PERM2 + m] = -1.0
        elif 80 <= m < 96:
            c[m - 16, C_PERM2 + m] = 1.0
    f1 = 500000.0 ** (-np.arange(8) * 2.0 / 16)
    f2 = 10000.0 ** (-np.arange(16) / 16.0)
    for m in range(P):
        if m % HD < 16:
            c[m, C_INV] = f1[m % 8]
        if 64 <= m < 96:
            c[m, C_INV + 1] = f2[m % 16]
    c[:, C_INV + 2] = EPS
    c[:, C_INV + 3] = GN_EPS
    m = np.zeros((P, M_END), np.float32)
    off = lambda keep: np.where(keep, 0.0, NEG).astype(np.float32)
    m[:, M_NEAR:M_NEAR + 256] = np.concatenate([off(col >= row), off(col <= row)], 1)
    for at, d in ((M_MOD4, 4), (M_MOD16, 16)):
        same = (row - col) % d == 0
        m[:, at:at + 512] = np.concatenate([off(same)] * 3 + [off(same & (col <= row))], 1)
    m[:, M_BAND:M_END] = np.concatenate([off(col >= row), off(row + col >= 0), off(col <= row)], 1)
    return c, m


class Signals:

    def __init__(self, nc, ctx):
        self.nc, self.ctx, self.of = nc, ctx, {}

    def __getitem__(self, name):
        if name not in self.of:
            self.of[name] = self.ctx.enter_context(self.nc.semaphore(name))
        return self.of[name]


class Counts:

    def __init__(self, eng, sem, step):
        self.eng, self.sem, self.last = eng, sem, step
        self.raised, self.seen = {}, {}
        self.turn = None

    def value(self, name, count):
        per = self.turn[1].get(name, 0) if self.turn else 0
        return count + self.turn[0] * per if per else count

    def up(self, name):
        self.raised[name] = self.raised.get(name, 0) + 1
        self.last = name
        return 1

    def own(self):
        return self.value(self.last, self.raised[self.last])

    def due(self, name, n=1):
        self.seen[name] = self.seen.get(name, 0) + n
        return self.value(name, self.seen[name])

    def loop(self, n, **per):
        return Turns(self, n, per)


class Turns:

    def __init__(self, counts, n, per):
        self.counts, self.n, self.per = counts, n, per

    def __enter__(self):
        self.fori = self.counts.eng.Fori(0, self.n)
        self.counts.turn = (self.fori.__enter__(), self.per)
        self.start = (dict(self.counts.raised), dict(self.counts.seen))

    def __exit__(self, *exc):
        self.fori.__exit__(*exc)
        self.counts.turn = None
        if exc[0]:
            return
        for now, was in zip((self.counts.raised, self.counts.seen), self.start):
            for name in now:
                d = now[name] - was.get(name, 0)
                assert d == self.per.get(name, 0), (name, d)
                now[name] += (self.n - 1) * d


def heads_of_first_block(i, h):
    return [(h, max(i - 1, 0), M_NEAR + 256 - (min(i, 1) + 1) * P),
            (GH + h, 0, M_MOD4 + (3 - i) * P),
            (2 * GH + h, 0, M_MOD16 + (3 - i) * P)]


class Buffers:

    def __init__(self, nc, ctx, ncols, cols):
        def sb(name, shape, dt=F32):
            return ctx.enter_context(nc.sbuf_tensor(name, shape, dt))

        self.cols = cols
        self.raw = sb("raw", [P, RAW, TILES * P])
        self.w_hi = sb("w_hi", [P, SPLIT, TILES * P], F32R)
        self.w_lo = sb("w_lo", [P, SPLIT, TILES * P], F32R)
        self.x = sb("x", [P, KD, T])
        self.h_hi, self.h_lo = sb("h_hi", [P, KD, T], F32R), sb("h_lo", [P, KD, T], F32R)
        with nc.sbuf_tensor("plain", [P, 2 * KD + 8, T], F32) as plain:
            self.plain = plain
        split = sb("split", [P, 2 * KD + 8, T], F32R)
        self.o_hi, self.o_lo = split[:, 0:KD], split[:, KD:2 * KD]
        self.s_hi, self.s_lo = split[:, 2 * KD:2 * KD + 4], split[:, 2 * KD + 4:]
        self.c_pair = sb("c_pair", [P, KD, 2], F32R)
        self.const = sb("const", [P, C_END])
        self.par = sb("par", [P, ncols])
        self.mark = sb("mark", [P, 2])
        self.mod = sb("mod", [P, 6 * KD])
        self.col = sb("col", [P, 192])
        self.posi = sb("posi", [P, NQ], I32)
        self.arena = sb("arena", [P, ARENA * T])
        self.posrow_i = self.arena[:, 44 * T:45 * T].bitcast(I32)
        self.psum = {"a": ctx.enter_context(nc.psum_tensor("psum_a", [P, BANKS, T], F32)),
                     "d": ctx.enter_context(nc.psum_tensor("psum_d", [P, BANKS, T], F32))}
        c = self.const
        self.ident, self.ones = c[:, C_IDENT:C_IDENT + P], c[:, C_ONES:C_ONES + P]
        self.pair = c[:, C_PAIR:C_PAIR + P]
        self.zero = c[:, C_LOW1 + P - 1:C_LOW1 + P]
        self.eps, self.gn_eps = c[:, C_INV + 2:C_INV + 3], c[:, C_INV + 3:C_INV + 4]
        ar, art = self.ar, self.art
        self.A_Q, self.A_K = art(0, 6), art(6, 6)
        self.A_V = ar(12, 6).rearrange("p (q n) -> p q n", q=NQ)
        self.A_O = ar(18, 2)[:, 0:NQ * 256].rearrange("p (q n) -> p q n", q=NQ)
        self.A_S, self.A_E, self.A_P = (ar(a, 5).rearrange("p (s n) -> p s n", s=2) for a in (20, 25, 30))
        self.MASKS = ar(35, width=M_BAND)
        self.A_C, self.A_SN, self.A_T = ar(38), ar(39), art(40, 4)
        self.ADA = ar(44)[0:2]
        self.N0 = Norm(self, 18)
        self.R_U = ar(0, width=2 * 513).rearrange("p (s n) -> p s n", s=2)
        self.R_PB = self.arena[:, 1028:1028 + 4 * 129].rearrange("p (c n) -> p c n", c=NQ)
        (self.R_R, self.R_K, self.R_V, self.R_T, self.R_SW, self.R_AA, self.R_CUM, self.R_KK) = (
            ar(4 + n) for n in range(8))
        self.R_AR = ar(12, 2).rearrange("p (c a t) -> p c a t", c=NQ, a=2)
        self.R_BH, self.R_KP, self.R_KH = (ar(14 + n) for n in range(3))
        self.R_BV, self.R_G = (ar(17), ar(43)), (ar(40), ar(44))
        self.R_VN, self.R_BN, self.R_KN = (ar(18 + n).rearrange("p (c n) -> p c n", c=NQ) for n in range(3))
        self.R_LM = ar(21, 8).rearrange("p (u m t) -> p u m t", u=8, m=4)
        self.R_Z, self.R_TN, self.R_TT = (ar(a, 2).rearrange("p (u t) -> p u t", u=8) for a in (29, 31, 33))
        self.R_WU = ar(35, width=1024).rearrange("p (s n) -> p s n", s=8)
        self.R_Y, self.R_YC, self.R_O, self.R_SQ, self.R_STD = (ar(n) for n in (37, 38, 39, 41, 42))
        self.G_SG, self.G_M = art(0, 4), art(4, 8)
        self.Y8, self.N1 = art(12, 8), Norm(self, 20)
        self.F_R, self.F_T = art(0, 4), ar(29)

        self.L_M, self.L_Q, self.L_K = art(0, 8), art(8, 4), art(12, 4)
        self.L_V, self.L_O = (ar(a, 4).rearrange("p (q n) -> p q n", q=NQ) for a in (16, 20))
        self.L_C, self.L_S, self.L_E, self.L_P = art(8, 3), art(24, 2), art(26, 4), art(30, 2)
        self.L_GATE = [self.plain[:, at + n] for at in (0, KD) for n in range(BW // P, KD)]
        self.L_BIAS, self.L_E6 = self.plain[:, 2 * KD:2 * KD + 2], self.plain[:, 2 * KD + 2:]
        self.NH = Norm(self, 24)
        self.L_D = ar(32, 4).rearrange("p (q n) -> p q n", q=NQ)
        self.L_DW = ar(36, 3).rearrange("p (q n) -> p q n", q=NQ)
        self.L_COS, self.L_SIN, self.L_KR, self.L_PE, self.L_POS = ar(39), ar(40), ar(41), art(42, 2), ar(44)
        self.F_G = ar(0, width=2 * 514).rearrange("p (s n) -> p s n", s=2)
        self.F_SG = art(8, 2)
        self.L_DW_TMP = art(32, 4)
        self.F_U, self.F_C, self.F_A, self.F_F = art(3, 2), ar(5), ar(6), ar(7)

    def ar(self, at, n=1, width=None):
        w = width if width is not None else n * T
        return self.arena[:, at * T:at * T + w]

    def art(self, at, n):
        return self.ar(at, n).rearrange("p (n t) -> p n t", n=n)

    def pc(self, name, k=0, l=None):
        at = (self.cols[name] if l is None else self.cols[name, l]) + k
        return self.par[:, at:at + 1]

    def pcs(self, name, n, l=None):
        at = self.cols[name] if l is None else self.cols[name, l]
        return self.par[:, at:at + n]


class Norm:

    def __init__(self, b, base):
        self.sq, self.acc = b.art(base, 2), b.ar(base + 2)
        self.std, self.inv = b.ar(base + 3), b.ar(base + 4)
        self.tmp = b.art(base + 5, 4)


class Tile:

    def __init__(self, ring, n, ps, full, free):
        self.ring, self.n, self.ps, self.full, self.free = ring, n, ps, full, free


class Pe(Counts):

    def __init__(self, eng, sem, b, plan):
        super().__init__(eng, sem, "pe_step")
        self.b, self.plan, self.at, self.old_block = b, plan, 0, False
        self.opened = {"a": 0, "d": 0}
        self.input = self.output = None

    def tile(self, ring):
        n = self.opened[ring]
        self.opened[ring] += 1
        return Tile(ring, n, self.b.psum[ring][:, n % BANKS], self.sem["full_" + ring], self.sem["free_" + ring])

    def emptied(self, tile):
        return self.value("full_" + tile.ring, tile.n + 1)

    def taken(self, tile):
        return self.value("full_" + tile.ring, tile.n + 1 + BANKS)

    def new_block(self):
        return self.at % TILES == 0

    def take(self, tag, n=1):
        t = self.at
        assert all(self.plan[t + i][0] == tag for i in range(n)), (tag, self.plan[t][0], t)
        assert t // TILES == (t + n - 1) // TILES
        if t % TILES == 0:
            self.old_block = t > 0
        s, c0 = (t // TILES) % SPLIT, (t % TILES) * P
        self.at = t + n
        return self.b.w_hi[:, s, c0:c0 + n * P], self.b.w_lo[:, s, c0:c0 + n * P]

    def done_with_block(self):
        was, self.old_block = self.old_block, False
        return was

    def skip_turns(self, turns, at, opened):
        self.at += (turns - 1) * (self.at - at)
        for ring, n in opened.items():
            self.opened[ring] += (turns - 1) * (self.opened[ring] - n)


def pe_product(pe, dst, tag, hi, lo, k, ready, part=None):
    for t in part or range(k):
        if ready:
            pe.eng.wait_ge(pe.sem[ready], pe.due(ready))
        if pe.new_block():
            pe.eng.wait_ge(pe.sem["w_ready"], pe.due("w_ready"))
        wh, wl = pe.take(tag)
        m = pe.eng.matmul(dst, wh, hi(t), start=t == 0, stop=False)
        if pe.done_with_block():
            m.then_inc(pe.sem["w_used"], pe.up("w_used"))
        pe.eng.matmul(dst, wh, lo(t), start=False, stop=False)
        m = pe.eng.matmul(dst, wl, hi(t), start=False, stop=t == k - 1)
    return m


def pe_features(pe, ring, tag, act, k=KD, ready=None):
    tl = pe.tile(ring)
    pe.eng.wait_ge(tl.free, pe.emptied(tl))
    pe_product(pe, tl.ps, tag, *act, k, ready).then_inc(tl.full, pe.up("full_" + ring))
    return tl


def pe_tokens(pe, ring, tag, n, act, k=KD):
    tiles = [pe.tile(ring) for _ in range(NQ)]
    pe.eng.wait_ge(tiles[-1].free, pe.emptied(tiles[-1]))
    for t in range(k):
        if pe.new_block():
            pe.eng.wait_ge(pe.sem["w_ready"], pe.due("w_ready"))
        wh, wl = pe.take(tag, n)
        for q in range(NQ):
            d = tiles[q].ps[:, 0:n * P]
            ah, al = (a(t)[:, q * P:(q + 1) * P] for a in act)
            m = pe.eng.matmul(d, ah, wh, start=t == 0, stop=False)
            if pe.done_with_block():
                m.then_inc(pe.sem["w_used"], pe.up("w_used"))
            pe.eng.matmul(d, al, wh, start=False, stop=False)
            m = pe.eng.matmul(d, ah, wl, start=False, stop=t == k - 1)
            if t == k - 1:
                m.then_inc(tiles[q].full, pe.up("full_" + ring))
    return tiles[-1]


def pe_plain(pe, ring, lhsT, rhs):
    tl = pe.tile(ring)
    pe.eng.wait_ge(tl.free, pe.emptied(tl))
    pe.eng.matmul(tl.ps[0:lhsT.shape[1], 0:rhs.shape[1]], lhsT, rhs, start=True, stop=True)\
        .then_inc(tl.full, pe.up("full_" + ring))
    return tl


def pe_sums(pe, src, w, which):
    tl = pe.tile("a")
    pe.eng.wait_ge(tl.free, pe.emptied(tl))
    for q in range(NQ):
        m = pe.eng.matmul(tl.ps[:, w * q:w * (q + 1)], src[:, q * P:(q + 1) * P], which, start=True, stop=True)
    m.then_inc(tl.full, pe.up("full_a"))


def pe_spread(pe, cols, w, rows):
    tl = pe.tile("d")
    pe.eng.wait_ge(tl.free, pe.emptied(tl))
    for q in range(NQ):
        for i in range(w):
            m = pe.eng.matmul(tl.ps[i * rows // w:(i + 1) * rows // w, q * P:(q + 1) * P],
                              cols[:, w * q + i:w * q + i + 1].to_broadcast([P, rows // w]), pe.b.ident,
                              start=True, stop=True)
    m.then_inc(tl.full, pe.up("full_d"))


def pe_norm(pe, N):
    pe.eng.wait_ge(pe.sem["sum_ready"], pe.due("sum_ready"))
    pe_sums(pe, N.acc, 1, pe.b.ones[:, 0:1])
    pe.eng.wait_ge(pe.sem["norm_inv"], pe.due("norm_inv"))
    pe_spread(pe, pe.b.col[:, 188:192], 1, P)


def pe_turned(pe, srcs):
    tl = pe.tile("a")
    pe.eng.wait_ge(tl.free, pe.emptied(tl))
    for q, s in enumerate(srcs):
        m = pe.eng.transpose(tl.ps[:, q * P:(q + 1) * P], s, pe.b.ident)
    m.then_inc(tl.full, pe.up("full_a"))
    return tl


def pe_gate(pe, n=1):
    for _ in range(n):
        pe_features(pe, "a", "gate2", of(pe.b.h_hi, pe.b.h_lo))


def gates_at(s, n_units, gates):
    return gates > 0 and s % (n_units // gates) == 1 and s // (n_units // gates) < gates


def pe_attention(pe, units, lag=2, extra=None, late=None):
    n_units, turned, tl = len(units), {}, None
    for s in range(n_units + lag + 1):
        if s < n_units:
            for lhsT, rhs in units[s].scores:
                pe_plain(pe, "d", lhsT, rhs)
        if extra:
            extra(s)
        if 0 <= s - lag < n_units and units[s - lag].v:
            u = units[s - lag]
            pe.eng.wait_ge(pe.sem[u.ready], pe.due(u.ready))
            if u.ready == "p_ready":
                pe.seen["e_done"] += 2
            blocks = [u.e[:, k * P:(k + 1) * P] for k in range(len(u.v))]
            for k in range(0, len(blocks), 4):
                turned[s - lag] = pe_turned(pe, blocks[k:k + 4])
        if 0 <= s - lag - 1 < n_units and units[s - lag - 1].v:
            u = units[s - lag - 1]
            pe.eng.wait_ge(turned[s - lag - 1].free, pe.taken(turned[s - lag - 1]))
            tl = pe.tile("d")
            pe.eng.wait_ge(tl.free, pe.emptied(tl))
            for k, v in enumerate(u.v):
                m = pe.eng.matmul(tl.ps[:, 0:u.width], u.pt[:, k * P:(k + 1) * P], v, start=k == 0,
                                  stop=k == len(u.v) - 1)
            m.then_inc(tl.full, pe.up("full_d"))
        if late:
            late(s)
    return tl


class Unit:

    def __init__(self, scores, v, width, s, e, pt, o, ready="e_done", masks=None, dist=None, slope=0.0, sink=None,
                 neg_lam=None):
        self.scores, self.v, self.width, self.s, self.e, self.pt, self.o = scores, v, width, s, e, pt, o
        self.ready, self.masks, self.dist, self.slope, self.sink, self.neg_lam = ready, masks, dist, slope, sink, neg_lam


def units_1(b):
    units = []
    for n in range(GH * NQ):
        h, i = n // NQ, n % NQ
        scores, v, masks = [], [], []
        for head, k0, m0 in heads_of_first_block(i, h):
            p0, t = head % 2 * HD, head // 2
            scores.append((b.A_Q[p0:p0 + HD, t, i * P:(i + 1) * P], b.A_K[p0:p0 + HD, t, k0 * P:(i + 1) * P]))
            masks.append(b.MASKS[:, m0:m0 + (i + 1 - k0) * P])
            v += [b.A_V[:, kt, head * HD:(head + 1) * HD] for kt in range(k0, i + 1)]
        w = len(v) * P
        units.append(Unit(scores, v, HD, b.A_S[:, n % 2, 0:w], b.A_E[:, n % 2, 0:w], b.A_P[:, n % 2, 0:w],
                          masks=masks, o=b.A_O[:, i, h * HD:(h + 1) * HD]))
    return units


def units_mla(b, half):
    units = []
    for h in range(4):
        for i in range(NQ):
            n, head = len(units), 4 * half + h
            units.append(Unit([(b.L_Q[0:MQ, h, i * P:(i + 1) * P], b.L_K[0:MQ, h])],
                              [b.L_V[:, kt, head * MV:(head + 1) * MV] for kt in range(NQ)], MV,
                              b.L_S[:, n % 2], b.L_E[:, n % 4], b.L_P[:, n % 2],
                              o=b.L_O[:, i, head * MV:(head + 1) * MV]))
    return units


def units_diff(b, neg_lam):
    units = []
    for h in range(DH):
        for i in range(NQ):
            dist = b.L_D[:, i]
            for m in range(2):
                n, t, r = len(units), 2 * m + h // 2, slice(h % 2 * HD, h % 2 * HD + HD)
                units.append(Unit([(b.L_Q[r, t, i * P:(i + 1) * P], b.L_K[r, t])],
                                  [b.L_V[:, kt, h * DV:(h + 1) * DV] for kt in range(NQ)] if m else [], DV,
                                  b.L_S[:, n % 2], b.L_E6[:, n % 6], b.L_P[:, n // 2 % 2], ready="p_ready",
                                  dist=dist, slope=SLOPES[WH + h], neg_lam=neg_lam,
                                  o=b.L_O[:, i, h * DV:(h + 1) * DV]))
    return units


def units_win(b, l):
    units = []
    for h in range(WH):
        for i in range(NQ):
            n, kv, r = len(units), h // (WH // WKV), slice(h % 2 * HD, h % 2 * HD + HD)
            k0, k1 = max(i - 1, 0), min(i + 2, NQ)
            w, d0 = (k1 - k0) * P, (k0 - i + 1) * P
            units.append(Unit([(b.L_Q[r, h // 2, i * P:(i + 1) * P], b.L_K[r, kv, k0 * P:k1 * P])],
                              [b.L_V[:, kt, kv * HD:(kv + 1) * HD] for kt in range(k0, k1)], HD,
                              b.L_S[:, n % 2, 0:w], b.L_E[:, n % 4, 0:w], b.L_P[:, n % 2, 0:w],
                              dist=b.L_DW[:, i, d0:d0 + w], slope=SLOPES[h], sink=b.pc("win_sink_2", h, l),
                              o=b.L_O[:, i, h * HD:(h + 1) * HD]))
    return units


def mla_heads(b, l):
    r, out = slice(0, MQ), []
    for n in range(4):
        out += [(b.L_Q[:, n], b.col[:, 140:141], r), (b.L_K[:, n], b.pc("g_mla_k_2", 0, l), r)]
    return out


def diff_heads(b, l):
    r = slice(0, P)
    return [(b.L_Q[:, n], b.col[:, 141:142], r) for n in range(4)] + \
        [(b.L_K[:, n], b.pc("g_diff_k_2", 0, l), r) for n in range(4)]


def win_heads(b, l):
    r = slice(0, P)
    return [(b.L_Q[:, n], b.col[:, 142:143], r) for n in range(4)] + \
        [(b.L_K[:, n], b.pc("g_win_k_2", 0, l), r) for n in range(2)]


def of(hi, lo, at=0):
    return (lambda t: hi[:, at + t, :]), (lambda t: lo[:, at + t, :])


def pe_ada(pe, ks):
    b, tl = pe.b, pe.tile("d")
    pe.eng.wait_ge(tl.free, pe.emptied(tl))
    for t in ks:
        if pe.new_block():
            pe.eng.wait_ge(pe.sem["w_ready"], pe.due("w_ready"))
        wh, wl = pe.take("ada", 4)
        m = pe.eng.matmul(tl.ps[0:2], b.c_pair[:, t, :], wh, start=t == ks[0], stop=False)
        if pe.done_with_block():
            m.then_inc(pe.sem["w_used"], pe.up("w_used"))
        m = pe.eng.matmul(tl.ps[0:2], b.c_pair[:, t, :], wl, start=False, stop=t == ks[-1])
    m.then_inc(tl.full, pe.up("full_d"))


def pe_ada_turn(pe):
    b, tl = pe.b, pe.tile("d")
    pe.eng.wait_ge(pe.sem["ada_rows"], pe.due("ada_rows"))
    pe.eng.wait_ge(tl.free, pe.emptied(tl))
    for i in range(4):
        m = pe.eng.matmul(tl.ps[:, i:i + 1], b.ADA[:, i * P:(i + 1) * P], b.ones[0:2, 0:1], start=True, stop=True)
    m.then_inc(tl.full, pe.up("full_d"))


def pe_skip_pad(pe):
    while pe.at < len(pe.plan) and pe.plan[pe.at][0] == "pad":
        if pe.new_block():
            pe.eng.wait_ge(pe.sem["w_ready"], pe.due("w_ready"))
        pe.take("pad")


def pe_rwkv_keys(pe, j):
    b = pe.b
    pe_features(pe, "a", "w2", of(b.s_hi, b.s_lo), 1)
    pe_features(pe, "a", "a2", of(b.s_hi, b.s_lo), 1)
    pe_features(pe, "a", "rkv", of(b.h_hi, b.h_lo))


def pe_rwkv_input(pe, slot):
    b = pe.b
    if slot == 6:
        pe.eng.wait_ge(pe.sem["kk_sq"], pe.due("kk_sq"))
        pe_plain(pe, "a", b.pair, b.R_KK)
    if slot % 3 < 2:
        part = (slot // 3 * 2 + slot % 3) % 4
        if part == 0:
            pe.input = pe.tile("a")
            pe.eng.wait_ge(pe.input.free, pe.emptied(pe.input))
        m = pe_product(pe, pe.input.ps, "rkv", *of(b.h_hi, b.h_lo), KD, None, part=range(2 * part, 2 * part + 2))
        if part == 3:
            m.then_inc(pe.input.full, pe.up("full_a"))


def pe_rwkv_mean(pe):
    pe.eng.wait_ge(pe.output.free, pe.taken(pe.output))
    pe_plain(pe, "d", pe.b.pair, pe.b.R_Y)


def pe_rwkv_variance(pe):
    pe.eng.wait_ge(pe.sem["yc_sq"], pe.due("yc_sq"))
    pe_plain(pe, "a", pe.b.pair, pe.b.R_SQ)


def pe_rwkv(pe, j):
    b, eng = pe.b, pe.eng
    rows = [slice(0, HD), slice(HD, P)]
    pe_features(pe, "d", "g2", of(b.s_hi, b.s_lo, 1), 1)
    pe.eng.wait_ge(pe.sem["rk_ready"], pe.due("rk_ready"))
    pe_plain(pe, "d", b.pair, b.R_T)
    for src in (b.R_V, b.R_BH, b.R_KH):
        tn = pe_turned(pe, [src[:, c * P:(c + 1) * P] for c in range(NQ)])
    for u in range(8):
        c, r = u % NQ, rows[u // NQ]
        tl = pe.tile("d")
        pe.eng.wait_ge(tl.free, pe.emptied(tl))
        eng.matmul(tl.ps[:, 0:2 * P], b.R_BH[r, c * P:(c + 1) * P], b.R_AR[r, c], start=True, stop=True)
        eng.matmul(tl.ps[:, 2 * P:], b.R_KH[r, c * P:(c + 1) * P], b.R_AR[r, c], start=True, stop=True)\
            .then_inc(tl.full, pe.up("full_" + tl.ring))
    for g in range(2):
        tl = pe.tile("d")
        pe.eng.wait_ge(tl.free, pe.emptied(tl))
        for i in range(4):
            u = 4 * g + i
            c, r = u % NQ, rows[u // NQ]
            m = eng.matmul(tl.ps[:, i * P:(i + 1) * P], b.R_AR[r, c, 0], b.R_BH[r, c * P:(c + 1) * P],
                           start=True, stop=True)
        m.then_inc(tl.full, pe.up("full_" + tl.ring))

    def four(g, lhsT, rhs):
        tl = pe.tile("d")
        pe.eng.wait_ge(tl.free, pe.emptied(tl))
        for i in range(4):
            u = 4 * g + i
            m = eng.matmul(tl.ps[:, i * P:(i + 1) * P], lhsT[:, u], rhs[:, u], start=True, stop=True)
        m.then_inc(tl.full, pe.up("full_" + tl.ring))
        return tl

    if j + 1 < KD:
        pe_rwkv_keys(pe, j + 1)
    pe.eng.wait_ge(pe.sem["t_ready"], pe.due("t_ready"))
    LT = b.R_LM[:, :, 0]
    for k in range(1, 7):
        z = [four(g, LT, b.R_TN) for g in range(2)]
        if j + 1 < KD:
            pe_rwkv_input(pe, 2 * k - 2)
        done = []
        for g in range(2):
            pe.eng.wait_ge(z[g].free, pe.taken(z[g]))
            if k < 6:
                done.append(four(g, b.R_TT, b.R_Z))
            done.append(four(g, b.R_Z, b.R_TT))
        if j and k == 1:
            pe_rwkv_mean(pe)
        if j + 1 < KD:
            pe_rwkv_input(pe, 2 * k - 1)
        if j and k == 3:
            pe_rwkv_variance(pe)
        pe.eng.wait_ge(done[-1].free, pe.taken(done[-1]))
    pe.eng.wait_ge(tn.free, pe.taken(tn))
    W, U = b.R_WU[:, 0], b.R_WU[:, 1]
    for c in range(NQ):
        state = b.R_WU[:, 2 + c % 2]
        heads = [(rows[i], NQ * i + c) for i in range(2)]
        if c:
            pe.eng.wait_ge(new.free, pe.taken(new))
        tl = pe.tile("a")
        pe.eng.wait_ge(tl.free, pe.emptied(tl))
        if c:
            eng.matmul(tl.ps[:, 0:P], b.R_AR[:, c, 0], state, start=True, stop=False)
        for r, u in heads:
            m = eng.matmul(tl.ps[:, r], b.R_LM[:, u, 2], b.R_VN[:, c, r], start=c == 0, stop=c == 0 or r is rows[1])
        m.then_inc(tl.full, pe.up("full_" + tl.ring))
        pe.eng.wait_ge(tl.free, pe.taken(tl))
        tl = pe.tile("a")
        pe.eng.wait_ge(tl.free, pe.emptied(tl))
        for r, u in heads:
            m = eng.matmul(tl.ps[:, r], b.R_TT[:, u], W[:, r], start=True, stop=True)
        m.then_inc(tl.full, pe.up("full_" + tl.ring))
        pe.eng.wait_ge(tl.free, pe.taken(tl))
        if c < NQ - 1:
            new = pe.tile("d")
            pe.eng.wait_ge(new.free, pe.emptied(new))
            eng.matmul(new.ps[:, 0:P], b.R_BN[:, c], U, start=True, stop=False)
            eng.matmul(new.ps[:, 0:P], b.R_KN[:, c], b.R_VN[:, c], start=False, stop=True)\
                .then_inc(new.full, pe.up("full_" + new.ring))
        tl = pe.tile("d")
        pe.eng.wait_ge(tl.free, pe.emptied(tl))
        if c:
            eng.matmul(tl.ps[:, 0:P], state, b.R_AR[:, c, 1], start=True, stop=False)
        for r, u in heads:
            eng.matmul(tl.ps[r, 0:P], U[:, r], b.R_LM[:, u, 1], start=c == 0, stop=False)
            m = eng.matmul(tl.ps[r, 0:P], b.R_VN[:, c, r], b.R_LM[:, u, 3], start=False, stop=True)
        m.then_inc(tl.full, pe.up("full_" + tl.ring))
    pe.output = tl


def pe_head_norms(pe, heads, w, rope=False, gates=0):
    b, N = pe.b, pe.b.NH
    for n in range(len(heads) + 1):
        if n < len(heads):
            _, _, rows = heads[n]
            pe.eng.wait_ge(pe.sem["head_sq"], pe.due("head_sq"))
            pe_sums(pe, N.sq[rows, n % 2], w, b.ones[rows, 0:1] if w == 1 else b.pair[:, 0:P:HD])
            if n % 2 == 0 and n // 2 < gates:
                pe_gate(pe)
        if n:
            pe.eng.wait_ge(pe.sem["head_inv"], pe.due("head_inv"))
            pe_spread(pe, N.inv[:, (n - 1) % 4 * 8:(n - 1) % 4 * 8 + w * NQ], w, MQ if w == 1 else P)
    if rope:
        pe.eng.wait_ge(pe.sem["head_normed"], pe.due("head_normed", len(heads)))
        for t, _, rows in heads:
            pe_plain(pe, "d", b.const[rows, C_PERM2:C_PERM2 + MQ], t[rows])
    pe.eng.wait_ge(pe.sem["heads_ready"], pe.due("heads_ready"))


def pe_branch(pe):
    b = pe.b
    for n in range(KD):
        pe_features(pe, "d", "branch2", of(b.o_hi, b.o_lo), BW // P, ready="act_lo" if n == 0 else None)


def pe_turn_out(pe, before, after):
    pe_gate(pe, before)
    pe.eng.wait_ge(pe.sem["o_done"], pe.due("o_done"))
    for f in range(4):
        pe_turned(pe, [pe.b.L_O[:, q, f * P:(f + 1) * P] for q in range(NQ)])
    pe_gate(pe, after)


def pe_layer(pe, l):
    b = pe.b
    H = of(b.h_hi, b.h_lo)
    pe.eng.wait_ge(pe.sem["lam_parts"], pe.due("lam_parts"))
    pe_plain(pe, "a", b.ones[0:HD], b.col[0:HD, 152:154])
    pe_norm(pe, b.N1)
    for n in range(3):
        pe_features(pe, "a", "c", H, ready="act_lo" if n == 0 else None)
    pe_features(pe, "a", "kr", H)
    pe_norm(pe, b.N1)
    pe_norm(pe, b.N1)
    pe.eng.wait_ge(pe.sem["act_lo"], pe.due("act_lo", 3))
    for half in range(2):
        for n in range(4):
            pe_features(pe, "a", "uq", of(b.s_hi, b.s_lo), 2)
            pe_features(pe, "a", "uk", of(b.s_hi, b.s_lo, 2), 1)
        v = pe_tokens(pe, "a", "uv", 2, of(b.s_hi, b.s_lo, 2), 1)
        pe_head_norms(pe, mla_heads(b, l), 1, rope=True, gates=G_MLA[half])
        pe.eng.wait_ge(v.free, pe.taken(v))
        pe_attention(pe, units_mla(b, half), LAG_MLA, extra=lambda s: pe_gate(pe, gates_at(s, 16, G_MLA[2] * half)))
    pe_turn_out(pe, *G_MLA[3:])
    pe_skip_pad(pe)
    pe_branch(pe)
    for n in range(8):
        pe_features(pe, "a", "dqk", H)
    v = pe_tokens(pe, "a", "dv", 4, H)
    pe_head_norms(pe, diff_heads(b, l), 2, gates=G_DIFF[0])
    pe.eng.wait_ge(v.free, pe.taken(v))
    pe_attention(pe, units_diff(b, None), LAG_DIFF, extra=lambda s: pe_gate(pe, gates_at(s, 32, G_DIFF[1])))
    pe_turn_out(pe, *G_DIFF[2:])
    pe_branch(pe)
    for n in range(6):
        pe_features(pe, "a", "sqk", H)
    v = pe_tokens(pe, "a", "sv", 1, H)
    pe_head_norms(pe, win_heads(b, l), 2, gates=G_WIN[0])
    pe.eng.wait_ge(v.free, pe.taken(v))
    pe_attention(pe, units_win(b, l), LAG_WIN, extra=lambda s: pe_gate(pe, gates_at(s, 32, G_WIN[1])))
    pe_turn_out(pe, *G_WIN[2:])
    pe_branch(pe)
    for n in range(KD):
        pe_features(pe, "d", "out2", H, ready="act_lo" if n == 0 else None)
    pe_norm(pe, b.N1)

    def up(ready=None):
        for n in range(4):
            pe_features(pe, "a", "gate_up", H, ready=ready if n == 0 else None)

    def down(half):
        pe.eng.wait_ge(pe.sem["hid_lo"], pe.due("hid_lo", 2))
        for n in range(KD):
            pe_features(pe, "d", "down2", of(b.o_hi, b.o_lo, 2 * half), 2)

    up("act_lo")
    turns = (FF2 // P // 2 - 1) // 2
    at, opened = pe.at, dict(pe.opened)
    with pe.loop(turns, w_ready=12, w_used=12, full_a=8, full_d=16, hid_lo=4):
        for half in range(2):
            up()
            down(half)
    pe.skip_turns(turns, at, opened)
    down(0)
    pe.eng.wait_ge(pe.sem["act_lo"], pe.due("act_lo", 2))
    for n in range(KD):
        pe_features(pe, "d", "ple", of(b.s_hi, b.s_lo), 2)
    pe_norm(pe, b.N1)
    pe_norm(pe, b.N1)
    for n in range(KD):
        pe_features(pe, "a", "pgate", H, ready="act_lo" if n == 0 else None)


def pe_program(eng, sig, b, plan):
    pe = Pe(eng, sig, b, plan)
    H, O = of(b.h_hi, b.h_lo), of(b.o_hi, b.o_lo)
    pe.eng.wait_ge(pe.sem["loaded"], pe.due("loaded", NLOAD * 16))
    pe.eng.wait_ge(pe.sem["c_ready"], pe.due("c_ready"))
    for _ in range(ADA_FIRST):
        pe_ada(pe, range(KD))
        pe_ada_turn(pe)
    pe_norm(pe, b.N0)
    raws = [pe_features(pe, "a", "qk", H, ready="act_lo" if n == 0 else None) for n in range(12)]
    for n in range(12):
        pe.eng.wait_ge(raws[n].free, pe.taken(raws[n]))
        tl = pe_plain(pe, "d", b.const[:, C_PERM1:C_PERM1 + P], (b.A_Q if n < 6 else b.A_K)[:, n % 6])
    pe_tokens(pe, "a", "v4", 4, H)
    v = pe_tokens(pe, "a", "v2", 2, H)
    pe.eng.wait_ge(pe.sem["qk_ready"], pe.due("qk_ready"))
    pe.eng.wait_ge(v.free, pe.taken(v))

    def ada(s, half=0):
        if s < 16 and s and s % 2 == 0 and not half:
            pe_ada_turn(pe)
        if s < 16:
            k = 2 * (s % 2 * 2 + half)
            pe_ada(pe, range(k, k + 2))

    last = pe_attention(pe, units_1(b), extra=ada, late=lambda s: ada(s, 1))
    pe_ada_turn(pe)
    pe.eng.wait_ge(last.free, pe.taken(last))
    for f in range(2):
        pe_turned(pe, [b.A_O[:, q, f * P:(f + 1) * P] for q in range(NQ)])
    for n in range(2):
        pe_features(pe, "a", "lora", H)
    pe.eng.wait_ge(pe.sem["act_lo"], pe.due("act_lo", 4))
    pe_rwkv_keys(pe, 0)
    for slot in range(12):
        pe_rwkv_input(pe, slot)
    for j in range(KD):
        pe_rwkv(pe, j)
    pe_rwkv_mean(pe)
    pe_rwkv_variance(pe)
    pe.eng.wait_ge(pe.sem["act_lo"], pe.due("act_lo", KD))
    for n in range(KD):
        for part in range(2):
            pe_features(pe, "a", "gate", H)
        pe_features(pe, "d", "branch", of(b.s_hi, b.s_lo, 2), 2)
        pe_features(pe, "d", "branch", O)
    for n in range(KD):
        pe_features(pe, "d", "out", H, ready="act_lo" if n == 0 else None)
    pe_norm(pe, b.N1)
    pe_norm(pe, b.N1)

    def up(ready=None):
        for n in range(4):
            pe_features(pe, "a", "up1", H, ready=ready if n == 0 else None)

    def down(half):
        pe.eng.wait_ge(pe.sem["hid_lo"], pe.due("hid_lo", 4))
        for n in range(KD):
            pe_features(pe, "d", "down1", of(b.o_hi, b.o_lo, 4 * half), 4)

    up("act_lo")
    turns = (FF1 // P // 4 - 2) // 2
    at, opened = pe.at, dict(pe.opened)
    with pe.loop(turns, w_ready=16, w_used=16, full_a=8, full_d=16, hid_lo=8):
        for half in range(2):
            up()
            down(half)
    pe.skip_turns(turns, at, opened)
    up()
    down(0)
    down(1)
    pe_norm(pe, b.N1)
    for l in range(LAYERS):
        pe_layer(pe, l)
    pe_skip_pad(pe)


class Act(Counts):
    def __init__(self, eng, sem, b):
        super().__init__(eng, sem, "act_step")
        self.b, self.n, self.counts = b, 0, {}
        self.gate = 0

    def bank(self):
        self.n += 1
        return self.b.psum["a"][:, (self.n - 1) % BANKS]


def act_norm(a, N, k, src, width, dst=None, bias=None, src_ready=None):
    base = a.counts.get("sq_used", 0)
    for t in range(k):
        if src_ready:
            a.eng.wait_ge(a.sem[src_ready], a.due(src_ready))
        if base + max(1, t - 2) > 0 and t >= 2:
            a.eng.wait_ge(a.sem["sq_used"], base + max(1, t - 2))
        a.eng.wait_ge(a.sem[a.last], a.own())
        a.eng.activation(N.sq[:, t % 2], src(t), ACT.Square).then_inc(a.sem["sq"], a.up("sq"))
    a.counts["sq_used"] = base + max(0, k - 2)
    a.eng.wait_ge(a.sem["full_a"], a.due("full_a"))
    a.eng.activation(a.b.col[:, 176:180], a.bank()[:, 0:NQ], ACT.Sqrt, bias=a.b.eps, scale=1.0 / width)\
        .then_inc(a.sem["free_a"], a.up("free_a"))
    a.eng.wait_ge(a.sem[a.last], a.own())
    a.eng.sem_inc(a.sem["std"], a.up("std"))
    if dst:
        for t in range(k):
            a.eng.wait_ge(a.sem["scaled"], a.due("scaled"))
            if bias is None:
                a.eng.activation(dst(t), N.tmp[:, t % 4], ACT.Copy).then_inc(a.sem["act_hi"], a.up("act_hi"))
            else:
                a.eng.activation(dst(t), N.tmp[:, t % 4], ACT.Identity, bias=bias(t))\
                    .then_inc(a.sem["act_hi"], a.up("act_hi"))


def act_rwkv_copy(a, n):
    if n - 1 > 0:
        a.eng.wait_ge(a.sem["shifted"], a.value("shifted", n - 1))
    a.eng.wait_ge(a.sem["full_a"], a.due("full_a"))
    a.eng.wait_ge(a.sem[a.last], a.own())
    a.eng.activation(a.b.R_U[:, n % 2, 1:], a.bank(), ACT.Copy).then_inc(a.sem["free_a"], a.up("free_a"))
    a.eng.wait_ge(a.sem[a.last], a.own())
    a.eng.sem_inc(a.sem["u_ready"], a.up("u_ready"))


def act_rwkv_keys(a, j):
    b, n = a.b, 2 + 3 * j
    a.eng.wait_ge(a.sem["full_a"], a.due("full_a"))
    a.eng.wait_ge(a.sem[a.last], a.own())
    a.eng.activation(b.R_SW, a.bank(), ACT.Sigmoid, bias=b.pc("decay_w0", j))\
        .then_inc(a.sem["free_a"], a.up("free_a"))
    a.eng.wait_ge(a.sem["full_a"], a.due("full_a"))
    a.eng.wait_ge(a.sem[a.last], a.own())
    a.eng.activation(b.R_AA, a.bank(), ACT.Sigmoid, bias=b.pc("iclr_a0", j)).then_inc(a.sem["free_a"], a.up("free_a"))
    a.eng.wait_ge(a.sem[a.last], a.own())
    a.eng.sem_inc(a.sem["wa_ready"], a.up("wa_ready"))
    a.eng.wait_ge(a.sem["cum_ready"], a.due("cum_ready"))
    plus, minus = b.col[:, 160:164], b.col[:, 164:168]
    for c in range(NQ):
        a.eng.wait_ge(a.sem[a.last], a.own())
        a.eng.activation(b.R_PB[:, c, 1:], b.R_CUM[:, c * P:(c + 1) * P], ACT.Exp, bias=plus[:, c:c + 1], scale=-DECAY)\
            .then_inc(a.sem["act_step"], a.up("act_step"))
    a.eng.wait_ge(a.sem[a.last], a.own())
    a.eng.activation(b.R_PB[:, :, 0], plus, ACT.Exp).then_inc(a.sem["act_step"], a.up("act_step"))
    a.eng.wait_ge(a.sem[a.last], a.own())
    a.eng.activation(b.col[:, 168:172], minus, ACT.Exp).then_inc(a.sem["act_step"], a.up("act_step"))
    for c in range(NQ):
        a.eng.wait_ge(a.sem[a.last], a.own())
        a.eng.activation(b.R_CUM[:, c * P:(c + 1) * P], b.R_CUM[:, c * P:(c + 1) * P], ACT.Exp, bias=minus[:, c:c + 1], scale=DECAY)\
            .then_inc(a.sem["decays" if c == NQ - 1 else "act_step"], a.up("decays" if c == NQ - 1 else "act_step"))
    act_rwkv_copy(a, n)


def act_rwkv_squares(a, j):
    b, n = a.b, 2 + 3 * j
    a.eng.wait_ge(a.sem["shifted"], a.value("shifted", n + 1))
    a.eng.wait_ge(a.sem[a.last], a.own())
    a.eng.activation(b.R_KK, b.R_K, ACT.Square, scale=b.pc("k_k", j)).then_inc(a.sem["kk_sq"], a.up("kk_sq"))
    act_rwkv_copy(a, n + 1)


def act_rwkv_length(a, j):
    b, n = a.b, 2 + 3 * j
    a.eng.wait_ge(a.sem["full_a"], a.due("full_a"))
    a.eng.wait_ge(a.sem[a.last], a.own())
    a.eng.activation(b.R_SW, a.bank(), ACT.Sqrt).then_inc(a.sem["free_a"], a.up("free_a"))
    a.eng.wait_ge(a.sem[a.last], a.own())
    a.eng.sem_inc(a.sem["kk_std"], a.up("kk_std"))
    act_rwkv_copy(a, n + 2)


def act_rwkv(a, j):
    b = a.b
    for dst in (b.R_VN, b.R_BN, b.R_KN):
        a.eng.wait_ge(a.sem["full_a"], a.due("full_a"))
        a.eng.wait_ge(a.sem[a.last], a.own())
        a.eng.activation(dst, a.bank().rearrange("p (c n) -> p c n", c=NQ), ACT.Copy)\
            .then_inc(a.sem["free_a"], a.up("free_a"))
    if j + 1 < KD:
        act_rwkv_keys(a, j + 1)
    if j:
        act_rwkv_centered(a)
    if j + 1 < KD:
        act_rwkv_squares(a, j + 1)
    if j:
        act_rwkv_deviation(a)
    if j + 1 < KD:
        act_rwkv_length(a, j + 1)
    for c in range(NQ):
        for s in range(2):
            a.eng.wait_ge(a.sem["full_a"], a.due("full_a"))
            a.eng.wait_ge(a.sem[a.last], a.own())
            a.eng.activation(b.R_WU[:, s], a.bank()[:, 0:P], ACT.Copy).then_inc(a.sem["free_a"], a.up("free_a"))
        if j and c == 2:
            act_rwkv_high(a, j - 1)


def act_rwkv_centered(a):
    b = a.b
    a.eng.wait_ge(a.sem["centered"], a.due("centered"))
    a.eng.wait_ge(a.sem[a.last], a.own())
    a.eng.activation(b.R_SQ, b.R_YC, ACT.Square).then_inc(a.sem["yc_sq"], a.up("yc_sq"))


def act_rwkv_deviation(a):
    b = a.b
    a.eng.wait_ge(a.sem["full_a"], a.due("full_a"))
    a.eng.wait_ge(a.sem[a.last], a.own())
    a.eng.activation(b.R_STD, a.bank(), ACT.Sqrt, bias=b.gn_eps, scale=1.0 / HD)\
        .then_inc(a.sem["free_a"], a.up("free_a"))
    a.eng.wait_ge(a.sem[a.last], a.own())
    a.eng.sem_inc(a.sem["gn_std"], a.up("gn_std"))


def act_rwkv_high(a, j):
    b = a.b
    a.eng.wait_ge(a.sem["mixed"], a.due("mixed"))
    a.eng.wait_ge(a.sem[a.last], a.own())
    a.eng.activation(b.o_hi[:, j], b.R_O, ACT.Copy).then_inc(a.sem["act_hi"], a.up("act_hi"))


def act_gate(a, n=1):
    b = a.b
    for _ in range(n):
        if a.gate == 0 and a.counts["merged"] > 0:
            a.eng.wait_ge(a.sem["merged"], a.value("merged", a.counts["merged"]))
        a.eng.wait_ge(a.sem["full_a"], a.due("full_a"))
        a.eng.wait_ge(a.sem[a.last], a.own())
        a.eng.activation(b.L_GATE[a.gate], a.bank(), ACT.Copy).then_inc(a.sem["free_a"], a.up("free_a"))
        a.gate += 1


def act_sigmoids(a):
    b = a.b
    for n in range(KD):
        a.eng.wait_ge(a.sem[a.last], a.own())
        a.eng.activation(b.L_GATE[n], b.L_GATE[n], ACT.Sigmoid).then_inc(a.sem["gate_ready"], a.up("gate_ready"))
    a.gate = 0
    a.counts["merged"] += KD


def act_attention(a, units, lag=2, gates=0):
    n_units = len(units)
    for s in range(n_units + lag + 1):
        if 0 <= s - 1 < n_units:
            u = units[s - 1]
            a.eng.wait_ge(a.sem["s_ready"], a.due("s_ready"))
            if u.sink is not None:
                a.eng.wait_ge(a.sem[a.last], a.own())
                a.eng.activation(u.sunk, u.sink, ACT.Exp, bias=u.neg).then_inc(a.sem["act_step"], a.up("act_step"))
            a.eng.wait_ge(a.sem[a.last], a.own())
            a.eng.activation(u.e, u.s, ACT.Exp, bias=u.neg, accum_out=u.sum).then_inc(a.sem["e_done"], a.up("e_done"))
        act_gate(a, gates_at(s, n_units, gates))
        if 0 <= s - lag < n_units and units[s - lag].v:
            u = units[s - lag]
            for b0 in range(0, len(u.v), 4):
                w = min(4, len(u.v) - b0) * P
                a.eng.wait_ge(a.sem["full_a"], a.due("full_a"))
                a.eng.wait_ge(a.sem[a.last], a.own())
                a.eng.activation(u.pt[:, b0 * P:b0 * P + w], a.bank()[:, 0:w], ACT.Copy)\
                    .then_inc(a.sem["free_a"], a.up("free_a"))


def act_head_norms(a, heads, lhs_width, gates=0):
    b, N = a.b, a.b.NH
    base = a.counts.get("head_normed", 0)
    for n in range(len(heads) + 1):
        if n < len(heads):
            t, _, rows = heads[n]
            a.eng.wait_ge(a.sem[a.last], a.own())
            a.eng.activation(N.sq[rows, n % 2], t[rows], ACT.Square).then_inc(a.sem["head_sq"], a.up("head_sq"))
        if n >= 2 and n % 2 == 0 and n // 2 <= gates:
            act_gate(a)
        if n:
            _, _, rows = heads[n - 1]
            if base + n - 2 > 0:
                a.eng.wait_ge(a.sem["head_normed"], a.value("head_normed", base + n - 2))
            a.eng.wait_ge(a.sem["full_a"], a.due("full_a"))
            a.eng.wait_ge(a.sem[a.last], a.own())
            w = (1 if lhs_width == MQ else 2) * NQ
            a.eng.activation(N.std[:, (n - 1) % 4 * 8:(n - 1) % 4 * 8 + w], a.bank()[:, 0:w], ACT.Sqrt, bias=b.eps, scale=1.0 / lhs_width)\
                .then_inc(a.sem["free_a"], a.up("free_a"))
            a.eng.wait_ge(a.sem[a.last], a.own())
            a.eng.sem_inc(a.sem["head_std"], a.up("head_std"))
    a.counts["head_normed"] = base + len(heads)


def act_turned(a, gain=None):
    b = a.b
    for f in range(4):
        a.eng.wait_ge(a.sem["full_a"], a.due("full_a"))
        a.eng.activation(b.L_E[:, f], a.bank(), ACT.Identity, scale=1.0 if gain is None else gain)\
            .then_inc(a.sem["free_a"], a.up("free_a"))
        a.eng.wait_ge(a.sem[a.last], a.own())
        a.eng.sem_inc(a.sem["o_plain"], a.up("o_plain"))
        a.eng.wait_ge(a.sem[a.last], a.own())
        a.eng.activation(b.o_hi[:, f], b.L_E[:, f], ACT.Copy).then_inc(a.sem["act_hi"], a.up("act_hi"))


def act_gates(a, slots):
    base = a.counts["merged"]
    for n in range(KD):
        if base + n - 1 > 0:
            a.eng.wait_ge(a.sem["merged"], a.value("merged", base + n - 1))
        a.eng.wait_ge(a.sem["full_a"], a.due("full_a"))
        a.eng.wait_ge(a.sem[a.last], a.own())
        a.eng.activation(slots[:, n % 2], a.bank(), ACT.Sigmoid).then_inc(a.sem["free_a"], a.up("free_a"))
        a.eng.wait_ge(a.sem[a.last], a.own())
        a.eng.sem_inc(a.sem["gate_ready"], a.up("gate_ready"))
    a.counts["merged"] = base + KD
    if base + KD > 0:
        a.eng.wait_ge(a.sem["merged"], a.value("merged", base + KD))


def act_layer(a, l, ins):
    b, N = a.b, a.b.N1
    h, _ = of(b.h_hi, b.h_lo)
    a.eng.wait_ge(a.sem["full_a"], a.due("full_a"))
    a.eng.wait_ge(a.sem[a.last], a.own())
    a.eng.activation(b.col[:, 154:156], a.bank()[:, 0:2], ACT.Exp).then_inc(a.sem["free_a"], a.up("free_a"))
    a.eng.wait_ge(a.sem[a.last], a.own())
    a.eng.sem_inc(a.sem["lam_exp"], a.up("lam_exp"))
    act_norm(a, N, KD, lambda t: b.x[:, t], D, h, src_ready=None if a.counts["x_seen"] else "x_ready")
    a.counts["x_seen"] = 0
    a.eng.dma_start(b.L_PE[:, :, :], ins["pe"][l].rearrange("(k p) t -> p k t", p=P)).then_inc(a.sem["pe_loaded"], 16)
    for n in range(3):
        a.eng.wait_ge(a.sem["full_a"], a.due("full_a"))
        a.eng.wait_ge(a.sem[a.last], a.own())
        a.eng.activation(b.L_C[:, n], a.bank(), ACT.Copy).then_inc(a.sem["free_a"], a.up("free_a"))
    a.eng.wait_ge(a.sem["full_a"], a.due("full_a"))
    a.eng.wait_ge(a.sem[a.last], a.own())
    a.eng.activation(b.L_KR, a.bank(), ACT.Copy).then_inc(a.sem["free_a"], a.up("free_a"))
    s_hi, _ = of(b.s_hi, b.s_lo)
    act_norm(a, N, 2, lambda t: b.L_C[:, t], QR, s_hi)
    act_norm(a, N, 1, lambda t: b.L_C[:, 2], KVR, of(b.s_hi, b.s_lo, 2)[0])
    for half in range(2):
        for n in range(4):
            a.eng.wait_ge(a.sem["full_a"], a.due("full_a"))
            a.eng.wait_ge(a.sem[a.last], a.own())
            a.eng.activation(b.L_Q[:, n], a.bank(), ACT.Copy).then_inc(a.sem["free_a"], a.up("free_a"))
            a.eng.wait_ge(a.sem["full_a"], a.due("full_a"))
            a.eng.wait_ge(a.sem[a.last], a.own())
            a.eng.activation(b.L_K[0:NOPE, n], a.bank()[0:NOPE], ACT.Copy).then_inc(a.sem["free_a"], a.up("free_a"))
            a.eng.wait_ge(a.sem[a.last], a.own())
            a.eng.activation(b.L_K[NOPE:MQ, n], b.L_KR[NOPE:MQ], ACT.Copy)\
                .then_inc(a.sem["act_step"], a.up("act_step"))
        for q in range(NQ):
            a.eng.wait_ge(a.sem["full_a"], a.due("full_a"))
            a.eng.wait_ge(a.sem[a.last], a.own())
            a.eng.activation(b.L_V[:, q, half * 256:half * 256 + 256], a.bank()[:, 0:256], ACT.Copy)\
                .then_inc(a.sem["free_a"], a.up("free_a"))
        act_head_norms(a, mla_heads(b, l), MQ, gates=G_MLA[half])
        act_attention(a, columns(units_mla(b, half), b), LAG_MLA, gates=G_MLA[2] * half)
    act_gate(a, G_MLA[3])
    act_turned(a)
    act_gate(a, G_MLA[4])
    act_sigmoids(a)
    for dst, n in ((b.L_Q, 4), (b.L_K, 4)):
        for t in range(n):
            a.eng.wait_ge(a.sem["full_a"], a.due("full_a"))
            a.eng.wait_ge(a.sem[a.last], a.own())
            a.eng.activation(dst[:, t], a.bank(), ACT.Copy).then_inc(a.sem["free_a"], a.up("free_a"))
    for q in range(NQ):
        a.eng.wait_ge(a.sem["full_a"], a.due("full_a"))
        a.eng.wait_ge(a.sem[a.last], a.own())
        a.eng.activation(b.L_V[:, q], a.bank(), ACT.Copy).then_inc(a.sem["free_a"], a.up("free_a"))
    act_head_norms(a, diff_heads(b, l), HD, gates=G_DIFF[0])
    act_attention(a, columns(units_diff(b, None), b), LAG_DIFF, gates=G_DIFF[1])
    a.eng.wait_ge(a.sem["out_squares"], a.due("out_squares"))
    a.eng.wait_ge(a.sem[a.last], a.own())
    a.eng.activation(b.col[:, 100:116], b.col[:, 100:116], ACT.Sqrt, bias=b.eps, scale=1.0 / DV)\
        .then_inc(a.sem["act_step"], a.up("act_step"))
    a.eng.wait_ge(a.sem[a.last], a.own())
    a.eng.sem_inc(a.sem["out_std"], a.up("out_std"))
    act_gate(a, G_DIFF[2])
    act_turned(a, b.col[:, 143:144])
    act_gate(a, G_DIFF[3])
    act_sigmoids(a)
    for dst, n in ((b.L_Q, 4), (b.L_K, 2)):
        for t in range(n):
            a.eng.wait_ge(a.sem["full_a"], a.due("full_a"))
            a.eng.wait_ge(a.sem[a.last], a.own())
            a.eng.activation(dst[:, t], a.bank(), ACT.Copy).then_inc(a.sem["free_a"], a.up("free_a"))
    for q in range(NQ):
        a.eng.wait_ge(a.sem["full_a"], a.due("full_a"))
        a.eng.wait_ge(a.sem[a.last], a.own())
        a.eng.activation(b.L_V[:, q, 0:P], a.bank()[:, 0:P], ACT.Copy).then_inc(a.sem["free_a"], a.up("free_a"))
    act_head_norms(a, win_heads(b, l), HD, gates=G_WIN[0])
    act_attention(a, columns(units_win(b, l), b), LAG_WIN, gates=G_WIN[1])
    act_gate(a, G_WIN[2])
    act_turned(a)
    act_gate(a, G_WIN[3])
    act_sigmoids(a)
    a.eng.wait_ge(a.sem["merged"], a.value("merged", a.counts["merged"]))
    for n in range(KD):
        a.eng.wait_ge(a.sem[a.last], a.own())
        a.eng.activation(b.h_hi[:, n], b.L_M[:, n], ACT.Copy).then_inc(a.sem["act_hi"], a.up("act_hi"))
    act_norm(a, N, KD, lambda t: b.x[:, t], D, h, src_ready="x_ready")
    a.eng.wait_ge(a.sem["mlp_clear"], a.due("mlp_clear"))
    for n in range(FF2 // P):
        a.eng.wait_ge(a.sem["full_a"], a.due("full_a"))
        a.eng.wait_ge(a.sem[a.last], a.own())
        a.eng.activation(b.F_G[:, n % 2, 1:T + 1], a.bank(), ACT.Copy).then_inc(a.sem["free_a"], a.up("free_a"))
        a.eng.wait_ge(a.sem["full_a"], a.due("full_a"))
        a.eng.wait_ge(a.sem[a.last], a.own())
        a.eng.activation(b.F_U[:, n % 2], a.bank(), ACT.Copy).then_inc(a.sem["free_a"], a.up("free_a"))
        a.eng.wait_ge(a.sem[a.last], a.own())
        a.eng.sem_inc(a.sem["gu_ready"], a.up("gu_ready"))
        a.eng.wait_ge(a.sem["conv"], a.due("conv"))
        a.eng.wait_ge(a.sem[a.last], a.own())
        a.eng.activation(b.F_A, b.F_C, ACT.Gelu_apprx_tanh, bias=b.pc("conv_b_2", n, l))\
            .then_inc(a.sem["gelu"], a.up("gelu"))
        a.eng.wait_ge(a.sem["f_ready"], a.due("f_ready"))
        a.eng.wait_ge(a.sem[a.last], a.own())
        a.eng.activation(b.o_hi[:, n % 4], b.F_F, ACT.Copy).then_inc(a.sem["act_hi"], a.up("act_hi"))
    if 16 * (l + 1) > 0:
        a.eng.wait_ge(a.sem["pe_loaded"], a.value("pe_loaded", 16 * (l + 1)))
    for t in range(2):
        a.eng.wait_ge(a.sem[a.last], a.own())
        a.eng.activation(b.s_hi[:, t], b.L_PE[:, t], ACT.Copy).then_inc(a.sem["act_hi"], a.up("act_hi"))
    act_norm(a, N, KD, lambda t: b.Y8[:, t], D, src_ready="y_ready")
    act_norm(a, N, KD, lambda t: b.x[:, t], D, h, src_ready="x_ready")
    act_gates(a, b.F_SG)


def act_program(eng, sig, b, ins):
    a = Act(eng, sig, b)
    eng.sem_inc(sig["free_a"], BANKS)
    a.raised["free_a"] = BANKS
    for dst, src in ((b.par[:, :], ins["params"]), (b.posrow_i, ins["pos_rows"]), (b.posi[:, :], ins["pos_cols"]),
                     (b.const[:, :], ins["const"]), (b.MASKS, ins["masks"][:, 0:M_BAND]),
                     (b.x[:, :, :], ins["x"].rearrange("(k p) t -> p k t", p=P))):
        eng.dma_start(dst, src).then_inc(sig["loaded"], 16)
    a.eng.wait_ge(a.sem["loaded"], a.due("loaded", NLOAD * 16))
    a.eng.activation(b.col[:, 0:8], b.pcs("c", KD), ACT.Sigmoid).then_inc(a.sem["sigmoid_c"], a.up("sigmoid_c"))
    for dst in (b.A_SN, b.A_C):
        a.eng.wait_ge(a.sem["angle"], a.due("angle"))
        a.eng.wait_ge(a.sem[a.last], a.own())
        a.eng.activation(dst, b.A_T[:, 3], ACT.Sin).then_inc(a.sem["sine"], a.up("sine"))
    h, hl = of(b.h_hi, b.h_lo)
    act_norm(a, b.N0, KD, lambda t: b.x[:, t], D, h, bias=lambda t: b.mod[:, t:t + 1])
    for n in range(12):
        a.eng.wait_ge(a.sem["full_a"], a.due("full_a"))
        a.eng.wait_ge(a.sem[a.last], a.own())
        a.eng.activation((b.A_Q if n < 6 else b.A_K)[:, n % 6], a.bank(), ACT.Copy, scale=HD ** -0.5 if n < 6 else 1.0)\
            .then_inc(a.sem["free_a"], a.up("free_a"))
    for w0, w in ((0, 512), (512, 256)):
        for q in range(NQ):
            a.eng.wait_ge(a.sem["full_a"], a.due("full_a"))
            a.eng.wait_ge(a.sem[a.last], a.own())
            a.eng.activation(b.A_V[:, q, w0:w0 + w], a.bank()[:, 0:w], ACT.Copy)\
                .then_inc(a.sem["free_a"], a.up("free_a"))
    us = columns(units_1(b), b)
    act_attention(a, us)
    for f in range(2):
        a.eng.wait_ge(a.sem["full_a"], a.due("full_a"))
        a.eng.wait_ge(a.sem[a.last], a.own())
        a.eng.activation(b.A_T[:, f], a.bank(), ACT.Copy).then_inc(a.sem["free_a"], a.up("free_a"))
        a.eng.wait_ge(a.sem[a.last], a.own())
        a.eng.sem_inc(a.sem["o_plain"], a.up("o_plain"))
        a.eng.wait_ge(a.sem[a.last], a.own())
        a.eng.activation(b.s_hi[:, 2 + f], b.A_T[:, f], ACT.Copy).then_inc(a.sem["act_hi"], a.up("act_hi"))
    for n in range(2):
        if n == 0:
            a.eng.wait_ge(a.sem["rwkv_clear"], a.due("rwkv_clear"))
        a.eng.wait_ge(a.sem["full_a"], a.due("full_a"))
        a.eng.wait_ge(a.sem[a.last], a.own())
        a.eng.activation(b.R_U[:, n, 1:], a.bank(), ACT.Copy).then_inc(a.sem["free_a"], a.up("free_a"))
        a.eng.wait_ge(a.sem[a.last], a.own())
        a.eng.sem_inc(a.sem["u_ready"], a.up("u_ready"))
    if 1 > 0:
        a.eng.wait_ge(a.sem["shifted"], a.value("shifted", 1))
    a.eng.wait_ge(a.sem[a.last], a.own())
    a.eng.activation(b.R_K[0:LORA], b.R_K[0:LORA], ACT.Tanh).then_inc(a.sem["act_step"], a.up("act_step"))
    a.eng.wait_ge(a.sem[a.last], a.own())
    a.eng.sem_inc(a.sem["lora_act"], a.up("lora_act"))
    a.eng.wait_ge(a.sem[a.last], a.own())
    a.eng.activation(b.s_hi[:, 0], b.R_K, ACT.Copy).then_inc(a.sem["act_hi"], a.up("act_hi"))
    if 2 > 0:
        a.eng.wait_ge(a.sem["shifted"], a.value("shifted", 2))
    a.eng.wait_ge(a.sem[a.last], a.own())
    a.eng.activation(b.R_V, b.R_V, ACT.Sigmoid).then_inc(a.sem["act_step"], a.up("act_step"))
    a.eng.wait_ge(a.sem[a.last], a.own())
    a.eng.sem_inc(a.sem["lora_act"], a.up("lora_act"))
    a.eng.wait_ge(a.sem[a.last], a.own())
    a.eng.activation(b.s_hi[:, 1], b.R_V, ACT.Copy).then_inc(a.sem["act_hi"], a.up("act_hi"))
    act_rwkv_keys(a, 0)
    act_rwkv_squares(a, 0)
    act_rwkv_length(a, 0)
    for j in range(KD):
        act_rwkv(a, j)
    act_rwkv_centered(a)
    act_rwkv_deviation(a)
    act_rwkv_high(a, KD - 1)
    a.eng.wait_ge(a.sem["mix_clear"], a.due("mix_clear"))
    for n in range(KD):
        if n - 1 > 0:
            a.eng.wait_ge(a.sem["merged"], a.value("merged", n - 1))
        for part in range(2):
            a.eng.wait_ge(a.sem["full_a"], a.due("full_a"))
            a.eng.wait_ge(a.sem[a.last], a.own())
            a.eng.activation(b.G_SG[:, 2 * (n % 2) + part], a.bank(), ACT.Sigmoid)\
                .then_inc(a.sem["free_a"], a.up("free_a"))
        a.eng.wait_ge(a.sem[a.last], a.own())
        a.eng.sem_inc(a.sem["gate_ready"], a.up("gate_ready"))
    for n in range(KD):
        if n == 0:
            a.eng.wait_ge(a.sem["merged"], a.due("merged", KD))
        a.eng.wait_ge(a.sem[a.last], a.own())
        a.eng.activation(b.h_hi[:, n], b.G_M[:, n], ACT.Copy).then_inc(a.sem["act_hi"], a.up("act_hi"))
    act_norm(a, b.N1, KD, lambda t: b.Y8[:, t], D, src_ready="y_ready")
    act_norm(a, b.N1, KD, lambda t: b.x[:, t], D, h, bias=lambda t: b.mod[:, 24 + t:25 + t], src_ready="x_ready")
    a.eng.dma_start(b.L_KR.bitcast(I32), ins["pos_rows_2"]).then_inc(a.sem["positions"], 16)
    for n in range(FF1 // P):
        if n - 3 > 0:
            a.eng.wait_ge(a.sem["hid_lo"], a.value("hid_lo", n - 3))
        a.eng.wait_ge(a.sem["full_a"], a.due("full_a"))
        a.eng.wait_ge(a.sem[a.last], a.own())
        a.eng.activation(b.F_R[:, n % 4], a.bank(), ACT.Relu).then_inc(a.sem["free_a"], a.up("free_a"))
        a.eng.wait_ge(a.sem[a.last], a.own())
        a.eng.activation(b.o_hi[:, n % 8], b.F_R[:, n % 4], ACT.Square).then_inc(a.sem["hid_hi"], a.up("hid_hi"))
        if n in (11, 15):
            a.eng.wait_ge(a.sem["angle"], a.due("angle"))
            a.eng.wait_ge(a.sem[a.last], a.own())
            a.eng.activation(b.L_SIN if n == 11 else b.L_COS, b.L_DW_TMP[:, 3], ACT.Sin)\
                .then_inc(a.sem["sine"], a.up("sine"))
    a.counts["hid_lo"] = FF1 // P
    act_norm(a, b.N1, KD, lambda t: b.Y8[:, t], D, src_ready="y_ready")
    a.counts["x_seen"] = 0
    a.counts["merged"] = KD
    for l in range(LAYERS):
        act_layer(a, l, ins)


def columns(units, b):
    for n, u in enumerate(units):
        c = 32 + 2 * (n % 32)
        u.top, u.neg, u.sum = b.col[:, 120 + n % 4:121 + n % 4], b.col[:, c:c + 1], b.col[:, c + 1:c + 2]
        u.inv, u.sunk = b.col[:, 124 + n % 4:125 + n % 4], b.col[:, 128 + n % 8:129 + n % 8]
    return units


class Dve(Counts):
    def __init__(self, eng, sem, b):
        super().__init__(eng, sem, "dve_step")
        self.b, self.n, self.counts = b, 0, {}

    def bank(self):
        self.n += 1
        return self.b.psum["d"][:, (self.n - 1) % BANKS]

    def each(self, mask, n):
        return mask.unsqueeze(1).to_broadcast([P, n, mask.shape[1]])


def dve_norm(v, N, k):
    for t in range(k):
        v.eng.wait_ge(v.sem["sq"], v.due("sq"))
        name = "sum_ready" if t == k - 1 else "sq_used"
        if k == 1:
            v.eng.tensor_copy(N.acc, N.sq[:, 0]).then_inc(v.sem[name], v.up(name))
        elif t:
            v.eng.wait_ge(v.sem[v.last], v.own())
            v.eng.tensor_tensor(N.acc, N.sq[:, 0] if t == 1 else N.acc, N.sq[:, t % 2], ALU.add)\
                .then_inc(v.sem[name], v.up(name))
    v.eng.wait_ge(v.sem["std"], v.due("std"))
    v.eng.reciprocal(v.b.col[:, 188:192], v.b.col[:, 176:180]).then_inc(v.sem["norm_inv"], v.up("norm_inv"))
    v.eng.wait_ge(v.sem["full_d"], v.due("full_d"))
    v.eng.wait_ge(v.sem[v.last], v.own())
    v.eng.tensor_copy(N.inv, v.bank()).then_inc(v.sem["free_d"], v.up("free_d"))


def dve_norm_split(v, N, k, src, gain, hi, lo, bias=None):
    dve_norm(v, N, k)
    for t in range(k + 1):
        v.eng.wait_ge(v.sem[v.last], v.own())
        if t < k:
            v.eng.scalar_tensor_tensor(N.tmp[:, t % 4], src(t), gain(t), N.inv, ALU.mult, ALU.mult)\
                .then_inc(v.sem["scaled"], v.up("scaled"))
        if t:
            v.eng.wait_ge(v.sem["act_hi"], v.due("act_hi"))
            y, high = N.tmp[:, (t - 1) % 4], hi(t - 1).bitcast(F32)
            if bias:
                v.eng.scalar_tensor_tensor(lo(t - 1), y, bias(t - 1), high, ALU.add, ALU.subtract)\
                    .then_inc(v.sem["act_lo"], v.up("act_lo"))
            else:
                v.eng.tensor_tensor(lo(t - 1), y, high, ALU.subtract).then_inc(v.sem["act_lo"], v.up("act_lo"))


def dve_norm_add(v, N, gain, last=None):
    b = v.b
    dve_norm(v, N, KD)
    for t in range(KD):
        v.eng.wait_ge(v.sem[v.last], v.own())
        v.eng.scalar_tensor_tensor(N.tmp[:, t % 4], b.Y8[:, t], gain(t), N.inv, ALU.mult, ALU.mult)\
            .then_inc(v.sem["dve_step"], v.up("dve_step"))
        v.eng.wait_ge(v.sem[v.last], v.own())
        name = last if last and t == KD - 1 else "x_ready"
        v.eng.tensor_tensor(b.x[:, t], b.x[:, t], N.tmp[:, t % 4], ALU.add).then_inc(v.sem[name], v.up(name))


def dve_angles(v, pos, inv, quarter, tmp):
    two_pi = 2 * np.pi
    c1 = 6.28125
    c2 = float(np.float32(np.floor((two_pi - c1) * 2 ** 21) / 2 ** 21))
    c3 = float(np.float32(two_pi - c1 - c2))
    ang, n, r = tmp[:, 0], tmp[:, 1], tmp[:, 2]
    v.eng.wait_ge(v.sem[v.last], v.own())
    v.eng.tensor_scalar(ang, pos, inv, None, ALU.mult).then_inc(v.sem["dve_step"], v.up("dve_step"))
    v.eng.wait_ge(v.sem[v.last], v.own())
    v.eng.tensor_scalar(n, ang, float(1 / two_pi), 0.25 * quarter, ALU.mult, ALU.add)\
        .then_inc(v.sem["dve_step"], v.up("dve_step"))
    v.eng.wait_ge(v.sem[v.last], v.own())
    v.eng.tensor_scalar(n, n, 12582912.0, None, ALU.add).then_inc(v.sem["dve_step"], v.up("dve_step"))
    v.eng.wait_ge(v.sem[v.last], v.own())
    v.eng.tensor_scalar(n, n, 12582912.0, None, ALU.subtract).then_inc(v.sem["dve_step"], v.up("dve_step"))
    v.eng.wait_ge(v.sem[v.last], v.own())
    v.eng.scalar_tensor_tensor(r, n, -c1, ang, ALU.mult, ALU.add).then_inc(v.sem["dve_step"], v.up("dve_step"))
    v.eng.wait_ge(v.sem[v.last], v.own())
    v.eng.scalar_tensor_tensor(r, n, -c2, r, ALU.mult, ALU.add).then_inc(v.sem["dve_step"], v.up("dve_step"))
    v.eng.wait_ge(v.sem[v.last], v.own())
    v.eng.scalar_tensor_tensor(r, n, -c3, r, ALU.mult, ALU.add).then_inc(v.sem["dve_step"], v.up("dve_step"))
    if quarter:
        v.eng.wait_ge(v.sem[v.last], v.own())
        v.eng.tensor_scalar(r, r, float(np.pi / 2), None, ALU.add).then_inc(v.sem["dve_step"], v.up("dve_step"))
    v.eng.wait_ge(v.sem[v.last], v.own())
    v.eng.tensor_scalar(tmp[:, 3], r, 3.1415925, -3.1415925, ALU.min, ALU.max).then_inc(v.sem["angle"], v.up("angle"))


def dve_ada(v, first, last):
    b = v.b
    v.eng.wait_ge(v.sem["full_d"], v.due("full_d"))
    v.eng.wait_ge(v.sem[v.last], v.own())
    if first:
        v.eng.tensor_copy(b.ADA, v.bank()[0:2]).then_inc(v.sem["free_d"], v.up("free_d"))
    else:
        v.eng.tensor_tensor(b.ADA, b.ADA, v.bank()[0:2], ALU.add).then_inc(v.sem["free_d"], v.up("free_d"))
    if last:
        v.eng.wait_ge(v.sem[v.last], v.own())
        v.eng.sem_inc(v.sem["ada_rows"], v.up("ada_rows"))


def dve_ada_turn(v, g):
    b, at, c0 = v.b, 4 * g, v.b.cols["ada_b"] + 4 * g
    v.eng.wait_ge(v.sem["full_d"], v.due("full_d"))
    v.eng.wait_ge(v.sem[v.last], v.own())
    v.eng.tensor_tensor(b.mod[:, at:at + 4], v.bank()[:, 0:4], b.par[:, c0:c0 + 4], ALU.add)\
        .then_inc(v.sem["free_d"], v.up("free_d"))


def dve_rwkv_input(v, j, step):
    b, n = v.b, 2 + 3 * j
    if step == 1:
        v.eng.wait_ge(v.sem["wa_ready"], v.due("wa_ready"))
        for c in range(NQ):
            s = slice(c * P, (c + 1) * P)
            v.eng.wait_ge(v.sem[v.last], v.own())
            v.eng.tensor_tensor_scan(b.R_CUM[:, s], b.ones, b.R_SW[:, s], 0.0, ALU.mult, ALU.add)\
                .then_inc(v.sem["dve_step"], v.up("dve_step"))
        mids = b.R_CUM.rearrange("p (c n) -> p c n", c=NQ)[:, :, P // 2 - 1]
        v.eng.wait_ge(v.sem[v.last], v.own())
        v.eng.tensor_scalar(b.col[:, 164:168], mids, -DECAY, None, ALU.mult)\
            .then_inc(v.sem["dve_step"], v.up("dve_step"))
        v.eng.wait_ge(v.sem[v.last], v.own())
        v.eng.tensor_scalar(b.col[:, 160:164], mids, DECAY, None, ALU.mult)\
            .then_inc(v.sem["cum_ready"], v.up("cum_ready"))
    if step == 2:
        dve_shift(v, n, b.R_K, 8 + j)
    if step == 3:
        v.eng.wait_ge(v.sem[v.last], v.own())
        v.eng.tensor_scalar(b.R_KP, b.R_AA, -1.0, b.pc("k_a", j), ALU.add, ALU.mult)\
            .then_inc(v.sem["dve_step"], v.up("dve_step"))
        v.eng.wait_ge(v.sem[v.last], v.own())
        v.eng.scalar_tensor_tensor(b.R_KP, b.R_KP, 1.0, b.R_K, ALU.add, ALU.mult)\
            .then_inc(v.sem["dve_step"], v.up("dve_step"))
    if step == 4:
        dve_shift(v, n + 1, b.R_R, j)
    if step == 8:
        v.eng.wait_ge(v.sem["kk_std"], v.due("kk_std"))
        v.eng.wait_ge(v.sem[v.last], v.own())
        v.eng.tensor_scalar(b.R_SW, b.R_SW, 1e-12, None, ALU.max).then_inc(v.sem["dve_step"], v.up("dve_step"))
        v.eng.wait_ge(v.sem[v.last], v.own())
        v.eng.reciprocal(b.R_SW, b.R_SW).then_inc(v.sem["dve_step"], v.up("dve_step"))
        v.eng.wait_ge(v.sem[v.last], v.own())
        v.eng.scalar_tensor_tensor(b.R_KK, b.R_K, b.pc("k_k", j), b.R_SW, ALU.mult, ALU.mult)\
            .then_inc(v.sem["dve_step"], v.up("dve_step"))
    if step == 9:
        v.eng.wait_ge(v.sem[v.last], v.own())
        v.eng.tensor_tensor(b.R_AA, b.R_KK, b.R_AA, ALU.mult).then_inc(v.sem["dve_step"], v.up("dve_step"))
    if step == 7:
        dve_shift(v, n + 2, b.R_V, 16 + j)


def dve_rwkv(v, j):
    b = v.b
    v.eng.wait_ge(v.sem["full_d"], v.due("full_d"))
    v.eng.wait_ge(v.sem[v.last], v.own())
    v.eng.tensor_copy(b.R_G[j % 2], v.bank()).then_inc(v.sem["free_d"], v.up("free_d"))
    v.eng.wait_ge(v.sem["decays"], v.due("decays"))
    chunks = lambda t: t.rearrange("p (c n) -> p c n", c=NQ)
    v.eng.wait_ge(v.sem[v.last], v.own())
    v.eng.scalar_tensor_tensor(b.R_AR[:, :, 0], chunks(b.R_KK), -1.0, b.R_PB[:, :, 0:P], ALU.mult, ALU.mult)\
        .then_inc(v.sem["dve_step"], v.up("dve_step"))
    v.eng.wait_ge(v.sem[v.last], v.own())
    v.eng.tensor_tensor(b.R_AR[:, :, 1], chunks(b.R_R), b.R_PB[:, :, 1:], ALU.mult)\
        .then_inc(v.sem["dve_step"], v.up("dve_step"))
    v.eng.wait_ge(v.sem[v.last], v.own())
    v.eng.tensor_tensor(b.R_BH, b.R_AA, b.R_CUM, ALU.mult).then_inc(v.sem["dve_step"], v.up("dve_step"))
    v.eng.wait_ge(v.sem[v.last], v.own())
    v.eng.tensor_tensor(b.R_KH, b.R_KP, b.R_CUM, ALU.mult).then_inc(v.sem["dve_step"], v.up("dve_step"))
    v.eng.wait_ge(v.sem[v.last], v.own())
    v.eng.tensor_tensor(b.col[:, 172:175], b.R_PB[:, 0:3, P], b.col[:, 169:172], ALU.mult)\
        .then_inc(v.sem["dve_step"], v.up("dve_step"))
    v.eng.wait_ge(v.sem[v.last], v.own())
    v.eng.scalar_tensor_tensor(b.R_T, b.R_R, b.pc("r_k", j), b.R_KP, ALU.mult, ALU.mult)\
        .then_inc(v.sem["rk_ready"], v.up("rk_ready"))
    v.eng.wait_ge(v.sem["full_d"], v.due("full_d"))
    v.eng.wait_ge(v.sem[v.last], v.own())
    v.eng.tensor_tensor(b.R_BV[j % 2], v.bank(), b.R_V, ALU.mult).then_inc(v.sem["free_d"], v.up("free_d"))
    mask4 = b.const[:, C_MASK4:C_MASK4 + T]
    for u in range(8):
        v.eng.wait_ge(v.sem["full_d"], v.due("full_d"))
        v.eng.wait_ge(v.sem[v.last], v.own())
        v.eng.tensor_tensor(b.R_LM[:, u].rearrange("p m t -> p (m t)"), v.bank(), mask4, ALU.mult)\
            .then_inc(v.sem["free_d"], v.up("free_d"))
    low1, low1t = b.const[:, C_LOW1:C_LOW1 + P], b.const[:, C_LOW1T:C_LOW1T + P]
    eye = v.each(b.ident, 4)
    four = lambda ps: ps.rearrange("p (u t) -> p u t", u=4)
    for g in range(2):
        us = slice(4 * g, 4 * g + 4)
        v.eng.wait_ge(v.sem["full_d"], v.due("full_d"))
        v.eng.wait_ge(v.sem[v.last], v.own())
        v.eng.tensor_tensor(b.R_TN[:, us], four(v.bank()), v.each(low1, 4), ALU.mult)\
            .then_inc(v.sem["free_d"], v.up("free_d"))
        v.eng.wait_ge(v.sem[v.last], v.own())
        v.eng.tensor_tensor(b.R_TN[:, us], b.R_TN[:, us], eye, ALU.add).then_inc(v.sem["dve_step"], v.up("dve_step"))
        v.eng.wait_ge(v.sem[v.last], v.own())
        v.eng.tensor_tensor(b.R_TT[:, us], b.R_LM[:, us, 0], v.each(low1t, 4), ALU.mult)\
            .then_inc(v.sem["dve_step"], v.up("dve_step"))
        v.eng.wait_ge(v.sem[v.last], v.own())
        v.eng.tensor_tensor(b.R_TT[:, us], b.R_TT[:, us], eye, ALU.add)\
            .then_inc(v.sem["t_ready" if g else "dve_step"], v.up("t_ready" if g else "dve_step"))
    for k in range(1, 7):
        level = b.const[:, C_LEVEL + (k - 1) * P:C_LEVEL + k * P]
        for g in range(2):
            us = slice(4 * g, 4 * g + 4)
            v.eng.wait_ge(v.sem["full_d"], v.due("full_d"))
            v.eng.wait_ge(v.sem[v.last], v.own())
            v.eng.tensor_tensor(b.R_Z[:, us], four(v.bank()), v.each(level, 4), ALU.mult)\
                .then_inc(v.sem["free_d"], v.up("free_d"))
        for g in range(2):
            us = slice(4 * g, 4 * g + 4)
            for dst in ((b.R_TN, b.R_TT) if k < 6 else (b.R_TT,)):
                v.eng.wait_ge(v.sem["full_d"], v.due("full_d"))
                v.eng.wait_ge(v.sem[v.last], v.own())
                v.eng.tensor_tensor(dst[:, us], dst[:, us], four(v.bank()), ALU.add)\
                    .then_inc(v.sem["free_d"], v.up("free_d"))
        if j + 1 < KD:
            dve_rwkv_input(v, j + 1, k)
        if j and k == 1:
            dve_rwkv_centered(v)
    pre, own = b.R_WU[:, 4], b.R_WU[:, 5]
    for c in range(NQ):
        new, old = b.R_WU[:, 2 + (c + 1) % 2], b.R_WU[:, 2 + c % 2]
        if c < NQ - 1:
            e = b.col[:, 172 + c:173 + c]
            if c:
                v.eng.wait_ge(v.sem[v.last], v.own())
                v.eng.tensor_scalar(pre, old, e, None, ALU.mult).then_inc(v.sem["dve_step"], v.up("dve_step"))
                v.eng.wait_ge(v.sem["full_d"], v.due("full_d"))
                v.eng.wait_ge(v.sem[v.last], v.own())
                v.eng.scalar_tensor_tensor(own, v.bank()[:, 0:P], e, b.pair, ALU.mult, ALU.mult)\
                    .then_inc(v.sem["dve_step"], v.up("dve_step"))
                v.eng.wait_ge(v.sem[v.last], v.own())
                v.eng.tensor_tensor(new, own, pre, ALU.add).then_inc(v.sem["free_d"], v.up("free_d"))
            else:
                v.eng.wait_ge(v.sem["full_d"], v.due("full_d"))
                v.eng.wait_ge(v.sem[v.last], v.own())
                v.eng.scalar_tensor_tensor(new, v.bank()[:, 0:P], e, b.pair, ALU.mult, ALU.mult)\
                    .then_inc(v.sem["free_d"], v.up("free_d"))
        v.eng.wait_ge(v.sem["full_d"], v.due("full_d"))
        v.eng.wait_ge(v.sem[v.last], v.own())
        v.eng.tensor_copy(b.R_Y[:, c * P:(c + 1) * P], v.bank()[:, 0:P]).then_inc(v.sem["free_d"], v.up("free_d"))
        if c == 0 and j + 1 < KD:
            dve_rwkv_input(v, j + 1, 7)
        if j and c == 0:
            dve_rwkv_normed(v, j - 1)
        if c >= 2 and j + 1 < KD:
            dve_rwkv_input(v, j + 1, 6 + c)
        if j and c == 1:
            dve_rwkv_mixed(v, j - 1)
        if j and c == 2:
            dve_rwkv_low(v, j - 1)


def dve_rwkv_centered(v):
    b = v.b
    v.eng.wait_ge(v.sem["full_d"], v.due("full_d"))
    v.eng.wait_ge(v.sem[v.last], v.own())
    v.eng.scalar_tensor_tensor(b.R_YC, v.bank(), -1.0 / HD, b.R_Y, ALU.mult, ALU.add)\
        .then_inc(v.sem["free_d"], v.up("free_d"))
    v.eng.wait_ge(v.sem[v.last], v.own())
    v.eng.sem_inc(v.sem["centered"], v.up("centered"))


def dve_rwkv_normed(v, j):
    b = v.b
    v.eng.wait_ge(v.sem["gn_std"], v.due("gn_std"))
    v.eng.wait_ge(v.sem[v.last], v.own())
    v.eng.reciprocal(b.R_STD, b.R_STD).then_inc(v.sem["dve_step"], v.up("dve_step"))
    v.eng.wait_ge(v.sem[v.last], v.own())
    v.eng.scalar_tensor_tensor(b.R_YC, b.R_YC, b.pc("gn_w", j), b.R_STD, ALU.mult, ALU.mult)\
        .then_inc(v.sem["dve_step"], v.up("dve_step"))


def dve_rwkv_mixed(v, j):
    b = v.b
    v.eng.wait_ge(v.sem[v.last], v.own())
    v.eng.scalar_tensor_tensor(b.R_YC, b.R_YC, b.pc("gn_b", j), b.R_BV[j % 2], ALU.add, ALU.add)\
        .then_inc(v.sem["dve_step"], v.up("dve_step"))
    v.eng.wait_ge(v.sem[v.last], v.own())
    v.eng.tensor_tensor(b.R_O, b.R_YC, b.R_G[j % 2], ALU.mult).then_inc(v.sem["mixed"], v.up("mixed"))


def dve_rwkv_low(v, j):
    b = v.b
    v.eng.wait_ge(v.sem["act_hi"], v.due("act_hi"))
    v.eng.wait_ge(v.sem[v.last], v.own())
    v.eng.tensor_tensor(b.o_lo[:, j], b.R_O, b.o_hi[:, j].bitcast(F32), ALU.subtract)\
        .then_inc(v.sem["act_lo"], v.up("act_lo"))


def dve_attention(v, us, lag=2, extra=None, late=None):
    b, eng = v.b, v.eng
    base = v.counts.get("e_done", 0)
    for s in range(len(us) + lag + 1):
        if s < len(us):
            u = us[s]
            if base + s - 1 > 0:
                v.eng.wait_ge(v.sem["e_done"], v.value("e_done", base + s - 1))
            parts = u.masks
            if u.dist is not None:
                bias = b.L_BIAS[:, (base + s) // 2 % 2, 0:u.s.shape[1]]
                if s == 0 or us[s - 1].dist is not u.dist:
                    v.eng.tensor_scalar(bias, u.dist, -u.slope, None, ALU.mult)\
                        .then_inc(v.sem["dve_step"], v.up("dve_step"))
                parts = [bias]
            elif not parts:
                parts = [b.zero.to_broadcast([P, T])]
            at, least = 0, FLOOR if u.sink is None else u.sink
            for m in parts:
                w = m.shape[1]
                v.eng.wait_ge(v.sem["full_d"], v.due("full_d"))
                v.eng.wait_ge(v.sem[v.last], v.own())
                v.eng.tensor_tensor_reduce(out=u.s[:, at:at + w], in0=v.bank()[:, 0:w], in1=m, scale=1.0, scalar=least, op0=ALU.add, op1=ALU.max, accum_out=u.top)\
                    .then_inc(v.sem["free_d"], v.up("free_d"))
                at, least = at + w, u.top
            v.eng.wait_ge(v.sem[v.last], v.own())
            v.eng.tensor_scalar(u.neg, u.top, -1.0, None, ALU.mult).then_inc(v.sem["s_ready"], v.up("s_ready"))
            if extra:
                extra(s)
        if 0 <= s - 2 < len(us) and us[s - 2].ready == "p_ready" and us[s - 2].v:
            u0, u1 = us[s - 3], us[s - 2]
            if base + s - 1 > 0:
                v.eng.wait_ge(v.sem["e_done"], v.value("e_done", base + s - 1))
            v.eng.wait_ge(v.sem[v.last], v.own())
            v.eng.reciprocal(u0.inv, u0.sum).then_inc(v.sem["dve_step"], v.up("dve_step"))
            v.eng.wait_ge(v.sem[v.last], v.own())
            v.eng.reciprocal(u1.inv, u1.sum).then_inc(v.sem["dve_step"], v.up("dve_step"))
            v.eng.wait_ge(v.sem[v.last], v.own())
            v.eng.tensor_tensor(u1.inv, u1.inv, u1.neg_lam, ALU.mult).then_inc(v.sem["dve_step"], v.up("dve_step"))
            v.eng.wait_ge(v.sem[v.last], v.own())
            v.eng.tensor_scalar(u1.e, u1.e, u1.inv, None, ALU.mult).then_inc(v.sem["dve_step"], v.up("dve_step"))
            v.eng.wait_ge(v.sem[v.last], v.own())
            v.eng.scalar_tensor_tensor(u1.e, u0.e, u0.inv, u1.e, ALU.mult, ALU.add)\
                .then_inc(v.sem["p_ready"], v.up("p_ready"))
        if 0 <= s - lag - 1 < len(us) and us[s - lag - 1].v:
            u = us[s - lag - 1]
            if u.ready == "p_ready":
                v.eng.wait_ge(v.sem["full_d"], v.due("full_d"))
                v.eng.wait_ge(v.sem[v.last], v.own())
                v.eng.tensor_copy(u.o, v.bank()[:, 0:u.width]).then_inc(v.sem["free_d"], v.up("free_d"))
            else:
                if u.sink is not None:
                    v.eng.wait_ge(v.sem[v.last], v.own())
                    v.eng.tensor_tensor(u.sum, u.sum, u.sunk, ALU.add).then_inc(v.sem["dve_step"], v.up("dve_step"))
                v.eng.wait_ge(v.sem[v.last], v.own())
                v.eng.reciprocal(u.inv, u.sum).then_inc(v.sem["dve_step"], v.up("dve_step"))
                v.eng.wait_ge(v.sem["full_d"], v.due("full_d"))
                v.eng.wait_ge(v.sem[v.last], v.own())
                v.eng.tensor_scalar(u.o, v.bank()[:, 0:u.width], u.inv, None, ALU.mult)\
                    .then_inc(v.sem["free_d"], v.up("free_d"))
        if late and s < len(us):
            late(s)
    v.counts["e_done"] = base + len(us)


def dve_shift(v, n, dst, mu):
    b = v.b
    u = b.R_U[:, n % 2]
    v.eng.wait_ge(v.sem["u_ready"], v.due("u_ready"))
    v.eng.wait_ge(v.sem[v.last], v.own())
    v.eng.tensor_tensor(b.R_T, u[:, 0:T], u[:, 1:T + 1], ALU.subtract).then_inc(v.sem["dve_step"], v.up("dve_step"))
    v.eng.wait_ge(v.sem[v.last], v.own())
    v.eng.scalar_tensor_tensor(dst, b.R_T, b.pc("shift_mu", mu), u[:, 1:T + 1], ALU.mult, ALU.add)\
        .then_inc(v.sem["shifted"], v.up("shifted"))


def dve_head_norms(v, heads, w=2, rope=False):
    b, N = v.b, v.b.NH
    for n, (t, gain, rows) in enumerate(heads):
        c = slice(n % 4 * 8, n % 4 * 8 + w * NQ)
        v.eng.wait_ge(v.sem["head_std"], v.due("head_std"))
        v.eng.wait_ge(v.sem[v.last], v.own())
        v.eng.reciprocal(N.inv[:, c], N.std[:, c]).then_inc(v.sem["head_inv"], v.up("head_inv"))
        v.eng.wait_ge(v.sem["full_d"], v.due("full_d"))
        v.eng.wait_ge(v.sem[v.last], v.own())
        v.eng.scalar_tensor_tensor(t[rows], t[rows], gain[rows], v.bank()[rows], ALU.mult, ALU.mult)\
            .then_inc(v.sem["free_d"], v.up("free_d"))
        v.eng.wait_ge(v.sem[v.last], v.own())
        v.eng.sem_inc(v.sem["head_normed"], v.up("head_normed"))
    if rope:
        for n, (t, gain, rows) in enumerate(heads):
            v.eng.wait_ge(v.sem["full_d"], v.due("full_d"))
            v.eng.wait_ge(v.sem[v.last], v.own())
            v.eng.tensor_tensor(N.tmp[rows, 0], v.bank()[rows], b.L_SIN[rows], ALU.mult)\
                .then_inc(v.sem["free_d"], v.up("free_d"))
            v.eng.wait_ge(v.sem[v.last], v.own())
            v.eng.tensor_tensor(t[rows], t[rows], b.L_COS[rows], ALU.mult)\
                .then_inc(v.sem["dve_step"], v.up("dve_step"))
            v.eng.wait_ge(v.sem[v.last], v.own())
            v.eng.tensor_tensor(t[rows], t[rows], N.tmp[rows, 0], ALU.add)\
                .then_inc(v.sem["dve_step"], v.up("dve_step"))
    v.eng.wait_ge(v.sem[v.last], v.own())
    v.eng.sem_inc(v.sem["heads_ready"], v.up("heads_ready"))


def dve_branch(v, first):
    b = v.b
    for n in range(KD):
        v.eng.wait_ge(v.sem["gate_ready"], v.due("gate_ready"))
        sg = b.L_GATE[n]
        if first:
            v.eng.wait_ge(v.sem["full_d"], v.due("full_d"))
            v.eng.wait_ge(v.sem[v.last], v.own())
            v.eng.tensor_tensor(b.L_M[:, n], v.bank(), sg, ALU.mult).then_inc(v.sem["free_d"], v.up("free_d"))
            v.eng.wait_ge(v.sem[v.last], v.own())
            v.eng.sem_inc(v.sem["merged"], v.up("merged"))
        else:
            v.eng.wait_ge(v.sem["full_d"], v.due("full_d"))
            v.eng.wait_ge(v.sem[v.last], v.own())
            v.eng.tensor_tensor(b.NH.tmp[:, 0], v.bank(), sg, ALU.mult).then_inc(v.sem["free_d"], v.up("free_d"))
            v.eng.wait_ge(v.sem[v.last], v.own())
            v.eng.tensor_tensor(b.L_M[:, n], b.L_M[:, n], b.NH.tmp[:, 0], ALU.add)\
                .then_inc(v.sem["merged"], v.up("merged"))


def dve_splits(v, n, lo, src, hi):
    for f in range(n):
        v.eng.wait_ge(v.sem["o_plain"], v.due("o_plain"))
        v.eng.wait_ge(v.sem["act_hi"], v.due("act_hi"))
        v.eng.wait_ge(v.sem[v.last], v.own())
        v.eng.tensor_tensor(lo[:, f], src(f), hi[:, f].bitcast(F32), ALU.subtract)\
            .then_inc(v.sem["act_lo"], v.up("act_lo"))


def dve_setup(v, step):
    b = v.b
    if step == 0:
        v.eng.wait_ge(v.sem["positions"], v.due("positions", 16))
        v.eng.wait_ge(v.sem[v.last], v.own())
        v.eng.tensor_copy(b.L_POS, b.L_KR.bitcast(I32)).then_inc(v.sem["dve_step"], v.up("dve_step"))
    if step in (1, 2):
        v.eng.wait_ge(v.sem["sine"], v.due("sine"))
    if step in (0, 1):
        dve_angles(v, b.L_POS, b.const[:, C_INV + 1:C_INV + 2], step, b.L_DW_TMP)
    for i in range(NQ):
        if i // 2 == step - 2:
            v.eng.wait_ge(v.sem[v.last], v.own())
            v.eng.tensor_scalar(b.L_D[:, i], b.L_POS, b.col[:, 180 + i:181 + i], None, ALU.subtract)\
                .then_inc(v.sem["dve_step"], v.up("dve_step"))
            v.eng.wait_ge(v.sem[v.last], v.own())
            v.eng.scalar_tensor_tensor(b.L_D[:, i], b.L_D[:, i], -1.0, b.L_D[:, i], ALU.mult, ALU.max)\
                .then_inc(v.sem["dve_step"], v.up("dve_step"))
    inc, strict = b.const[:, C_MASK4 + P:C_MASK4 + 2 * P], b.const[:, C_MASK4:C_MASK4 + P]
    for i in range(NQ):
        if i // 2 == step - 4:
            v.eng.wait_ge(v.sem[v.last], v.own())
            v.eng.tensor_copy(b.L_DW[:, i, P:2 * P], b.L_D[:, i, i * P:(i + 1) * P])\
                .then_inc(v.sem["dve_step"], v.up("dve_step"))
            if i:
                v.eng.wait_ge(v.sem[v.last], v.own())
                v.eng.tensor_scalar(b.L_DW[:, i, 0:P], inc, NEG, -NEG, ALU.mult, ALU.add)\
                    .then_inc(v.sem["dve_step"], v.up("dve_step"))
                v.eng.wait_ge(v.sem[v.last], v.own())
                v.eng.tensor_tensor(b.L_DW[:, i, 0:P], b.L_DW[:, i, 0:P], b.L_D[:, i, (i - 1) * P:i * P], ALU.add)\
                    .then_inc(v.sem["dve_step"], v.up("dve_step"))
            if i < NQ - 1:
                v.eng.wait_ge(v.sem[v.last], v.own())
                v.eng.scalar_tensor_tensor(b.L_DW[:, i, 2 * P:], strict, -NEG, b.L_D[:, i, (i + 1) * P:(i + 2) * P], ALU.mult, ALU.add)\
                    .then_inc(v.sem["dve_step"], v.up("dve_step"))


def dve_layer(v, l):
    b, N = v.b, v.b.N1
    h, hl = of(b.h_hi, b.h_lo)
    o = of(b.o_hi, b.o_lo)
    g = lambda name: (lambda t: b.pc(name, t, l))
    gq, nlam = b.col[:, 140:146], b.col[:, 150:151]
    for k, (name, scale) in enumerate((("g_mla_q_2", MQ ** -0.5), ("g_diff_q_2", HD ** -0.5),
                                       ("g_win_q_2", HD ** -0.5), ("g_diff_out_2", 1 - LAM0[l]))):
        v.eng.wait_ge(v.sem[v.last], v.own())
        v.eng.tensor_scalar(gq[:, k:k + 1], b.pc(name, 0, l), scale, None, ALU.mult)\
            .then_inc(v.sem["dve_step"], v.up("dve_step"))
    for k in range(2):
        v.eng.wait_ge(v.sem[v.last], v.own())
        v.eng.tensor_tensor(b.col[0:HD, 152 + k:153 + k], b.pc(f"lam_q{k + 1}_2", 0, l)[0:HD], b.pc(f"lam_k{k + 1}_2", 0, l)[0:HD], ALU.mult)\
            .then_inc(v.sem["lam_parts" if k else "dve_step"], v.up("lam_parts" if k else "dve_step"))
    v.eng.wait_ge(v.sem["lam_exp"], v.due("lam_exp"))
    v.eng.wait_ge(v.sem[v.last], v.own())
    v.eng.scalar_tensor_tensor(nlam, b.col[:, 155:156], -LAM0[l], b.col[:, 154:155], ALU.add, ALU.subtract)\
        .then_inc(v.sem["dve_step"], v.up("dve_step"))
    dve_norm_split(v, N, KD, lambda t: b.x[:, t], g("g_mix_2"), h, hl)
    s_hi, s_lo = of(b.s_hi, b.s_lo)
    dve_norm_split(v, N, 2, lambda t: b.L_C[:, t], g("g_q_lora_2"), s_hi, s_lo)
    kv = of(b.s_hi, b.s_lo, 2)
    dve_norm_split(v, N, 1, lambda t: b.L_C[:, 2], g("g_kv_lora_2"), *kv)
    for half in range(2):
        dve_head_norms(v, mla_heads(b, l), 1, rope=True)
        dve_attention(v, columns(units_mla(b, half), b), LAG_MLA)
    v.eng.wait_ge(v.sem[v.last], v.own())
    v.eng.sem_inc(v.sem["o_done"], v.up("o_done"))
    dve_splits(v, 4, b.o_lo, lambda f: b.L_E[:, f], b.o_hi)
    dve_branch(v, True)
    dve_head_norms(v, diff_heads(b, l))
    dve_attention(v, columns(units_diff(b, nlam), b), LAG_DIFF)
    ss = b.col[:, 100:116]
    for i in range(NQ):
        for k in range(DH):
            u = b.L_O[:, i, k * DV:(k + 1) * DV]
            v.eng.wait_ge(v.sem[v.last], v.own())
            v.eng.tensor_tensor_reduce(out=b.NH.tmp[:, 0, 0:DV], in0=u, in1=u, scale=1.0, scalar=0.0, op0=ALU.mult, op1=ALU.add, accum_out=ss[:, NQ * i + k:NQ * i + k + 1])\
                .then_inc(v.sem["dve_step"], v.up("dve_step"))
    v.eng.wait_ge(v.sem[v.last], v.own())
    v.eng.sem_inc(v.sem["out_squares"], v.up("out_squares"))
    v.eng.wait_ge(v.sem["out_std"], v.due("out_std"))
    v.eng.wait_ge(v.sem[v.last], v.own())
    v.eng.reciprocal(ss, ss).then_inc(v.sem["dve_step"], v.up("dve_step"))
    v.eng.wait_ge(v.sem[v.last], v.own())
    v.eng.tensor_tensor(b.L_O.rearrange("p q (h n) -> p (q h) n", h=DH), b.L_O.rearrange("p q (h n) -> p (q h) n", h=DH), ss.unsqueeze(2).to_broadcast([P, NQ * DH, DV]), ALU.mult)\
        .then_inc(v.sem["dve_step"], v.up("dve_step"))
    v.eng.wait_ge(v.sem[v.last], v.own())
    v.eng.sem_inc(v.sem["o_done"], v.up("o_done"))
    dve_splits(v, 4, b.o_lo, lambda f: b.L_E[:, f], b.o_hi)
    dve_branch(v, False)
    dve_head_norms(v, win_heads(b, l))
    dve_attention(v, columns(units_win(b, l), b), LAG_WIN)
    v.eng.wait_ge(v.sem[v.last], v.own())
    v.eng.sem_inc(v.sem["o_done"], v.up("o_done"))
    dve_splits(v, 4, b.o_lo, lambda f: b.L_E[:, f], b.o_hi)
    dve_branch(v, False)
    for n in range(KD):
        v.eng.wait_ge(v.sem["act_hi"], v.due("act_hi"))
        v.eng.wait_ge(v.sem[v.last], v.own())
        v.eng.tensor_tensor(b.h_lo[:, n], b.L_M[:, n], b.h_hi[:, n].bitcast(F32), ALU.subtract)\
            .then_inc(v.sem["act_lo"], v.up("act_lo"))
    for n in range(KD):
        v.eng.wait_ge(v.sem["full_d"], v.due("full_d"))
        v.eng.wait_ge(v.sem[v.last], v.own())
        v.eng.tensor_tensor(b.x[:, n], b.x[:, n], v.bank(), ALU.add).then_inc(v.sem["free_d"], v.up("free_d"))
        v.eng.wait_ge(v.sem[v.last], v.own())
        v.eng.sem_inc(v.sem["x_ready"], v.up("x_ready"))
    v.eng.wait_ge(v.sem[v.last], v.own())
    v.eng.memset(b.F_G[:, :, 0:1], 0.0).then_inc(v.sem["dve_step"], v.up("dve_step"))
    v.eng.wait_ge(v.sem[v.last], v.own())
    v.eng.memset(b.F_G[:, :, T + 1:T + 2], 0.0).then_inc(v.sem["mlp_clear"], v.up("mlp_clear"))
    dve_norm_split(v, N, KD, lambda t: b.x[:, t], g("g_ffn_2"), h, hl)

    def hidden(n):
        G = b.F_G[:, n % 2]
        v.eng.wait_ge(v.sem["gu_ready"], v.due("gu_ready"))
        v.eng.wait_ge(v.sem[v.last], v.own())
        v.eng.tensor_scalar(b.F_C, G[:, 0:T], b.pc("conv_w_2", n, l), None, ALU.mult)\
            .then_inc(v.sem["dve_step"], v.up("dve_step"))
        v.eng.wait_ge(v.sem[v.last], v.own())
        v.eng.scalar_tensor_tensor(b.F_C, G[:, 1:T + 1], b.pc("conv_w_2", 22 + n, l), b.F_C, ALU.mult, ALU.add)\
            .then_inc(v.sem["dve_step"], v.up("dve_step"))
        v.eng.wait_ge(v.sem[v.last], v.own())
        v.eng.scalar_tensor_tensor(b.F_C, G[:, 2:T + 2], b.pc("conv_w_2", 44 + n, l), b.F_C, ALU.mult, ALU.add)\
            .then_inc(v.sem["conv"], v.up("conv"))
        v.eng.wait_ge(v.sem["gelu"], v.due("gelu"))
        v.eng.wait_ge(v.sem[v.last], v.own())
        v.eng.tensor_tensor(b.F_F, b.F_A, b.F_U[:, n % 2], ALU.mult).then_inc(v.sem["f_ready"], v.up("f_ready"))
        v.eng.wait_ge(v.sem["act_hi"], v.due("act_hi"))
        v.eng.wait_ge(v.sem[v.last], v.own())
        v.eng.tensor_tensor(b.o_lo[:, n % 4], b.F_F, b.o_hi[:, n % 4].bitcast(F32), ALU.subtract)\
            .then_inc(v.sem["hid_lo"], v.up("hid_lo"))

    groups = FF2 // P // 2
    for grp in range(groups + 1):
        if grp < groups:
            hidden(2 * grp)
            hidden(2 * grp + 1)
        if grp:
            for n in range(KD):
                v.eng.wait_ge(v.sem["full_d"], v.due("full_d"))
                v.eng.wait_ge(v.sem[v.last], v.own())
                v.eng.tensor_tensor(b.x[:, n], b.x[:, n], v.bank(), ALU.add).then_inc(v.sem["free_d"], v.up("free_d"))
                if grp == groups:
                    v.eng.wait_ge(v.sem[v.last], v.own())
                    v.eng.sem_inc(v.sem["x_ready"], v.up("x_ready"))
    for t in range(2):
        v.eng.wait_ge(v.sem["act_hi"], v.due("act_hi"))
        v.eng.wait_ge(v.sem[v.last], v.own())
        v.eng.tensor_tensor(b.s_lo[:, t], b.L_PE[:, t], b.s_hi[:, t].bitcast(F32), ALU.subtract)\
            .then_inc(v.sem["act_lo"], v.up("act_lo"))
    for n in range(KD):
        v.eng.wait_ge(v.sem["full_d"], v.due("full_d"))
        v.eng.wait_ge(v.sem[v.last], v.own())
        v.eng.tensor_copy(b.Y8[:, n], v.bank()).then_inc(v.sem["free_d"], v.up("free_d"))
        v.eng.wait_ge(v.sem[v.last], v.own())
        v.eng.sem_inc(v.sem["y_ready"], v.up("y_ready"))
    dve_norm(v, N, KD)
    for t in range(KD):
        v.eng.wait_ge(v.sem[v.last], v.own())
        v.eng.scalar_tensor_tensor(b.Y8[:, t], b.Y8[:, t], b.pc("g_ple_2", t, l), N.inv, ALU.mult, ALU.mult)\
            .then_inc(v.sem["dve_step"], v.up("dve_step"))
    dve_norm_split(v, N, KD, lambda t: b.x[:, t], g("g_ple_in_2"), h, hl)
    for n in range(KD):
        v.eng.wait_ge(v.sem["gate_ready"], v.due("gate_ready"))
        v.eng.wait_ge(v.sem[v.last], v.own())
        v.eng.tensor_tensor(N.tmp[:, 0], b.F_SG[:, n % 2], b.Y8[:, n], ALU.mult)\
            .then_inc(v.sem["merged"], v.up("merged"))
        v.eng.wait_ge(v.sem[v.last], v.own())
        v.eng.tensor_tensor(b.x[:, n], b.x[:, n], N.tmp[:, 0], ALU.add)\
            .then_inc(v.sem["x_final" if l == LAYERS - 1 and n == KD - 1 else "x_ready"], v.up("x_final" if l == LAYERS - 1 and n == KD - 1 else "x_ready"))


def dve_program(eng, sig, b):
    v = Dve(eng, sig, b)
    eng.sem_inc(sig["free_d"], BANKS)
    v.raised["free_d"] = BANKS
    gain = lambda at: (lambda t: b.col[:, at + t:at + t + 1])
    v.eng.wait_ge(v.sem["loaded"], v.due("loaded", NLOAD * 16))
    v.eng.wait_ge(v.sem["sigmoid_c"], v.due("sigmoid_c"))
    v.eng.tensor_tensor(b.col[:, 0:8], b.col[:, 0:8], b.pcs("c", KD), ALU.mult)\
        .then_inc(v.sem["dve_step"], v.up("dve_step"))
    v.eng.wait_ge(v.sem[v.last], v.own())
    v.eng.tensor_copy(b.c_pair[:, :, 0], b.col[:, 0:8]).then_inc(v.sem["dve_step"], v.up("dve_step"))
    v.eng.wait_ge(v.sem[v.last], v.own())
    v.eng.tensor_tensor(b.c_pair[:, :, 1], b.col[:, 0:8], b.c_pair[:, :, 0].bitcast(F32), ALU.subtract)\
        .then_inc(v.sem["c_ready"], v.up("c_ready"))
    pos = b.Y8[:, 7]
    v.eng.wait_ge(v.sem[v.last], v.own())
    v.eng.tensor_copy(pos, b.posrow_i).then_inc(v.sem["dve_step"], v.up("dve_step"))
    v.eng.wait_ge(v.sem[v.last], v.own())
    v.eng.tensor_copy(b.col[:, 180:184], b.posi[:, :]).then_inc(v.sem["dve_step"], v.up("dve_step"))
    v.eng.wait_ge(v.sem[v.last], v.own())
    v.eng.tensor_copy(b.col[:, 184:188], b.col[:, 180:184]).then_inc(v.sem["dve_step"], v.up("dve_step"))
    for quarter in (0, 1):
        dve_angles(v, pos, b.const[:, C_INV:C_INV + 1], quarter, b.A_T)
        v.eng.wait_ge(v.sem["sine"], v.due("sine"))
    for g in range(ADA_FIRST):
        dve_ada(v, True, True)
        dve_ada_turn(v, g)
    v.eng.wait_ge(v.sem[v.last], v.own())
    v.eng.scalar_tensor_tensor(b.col[:, 16:24], b.mod[:, 8:16], 1.0, b.pcs("norm_mix_pre", KD), ALU.add, ALU.mult)\
        .then_inc(v.sem["dve_step"], v.up("dve_step"))
    h, hl = of(b.h_hi, b.h_lo)
    dve_norm_split(v, b.N0, KD, lambda t: b.x[:, t], gain(16), h, hl, bias=lambda t: b.mod[:, t:t + 1])
    for n in range(12):
        t = (b.A_Q if n < 6 else b.A_K)[:, n % 6]
        v.eng.wait_ge(v.sem["full_d"], v.due("full_d"))
        v.eng.wait_ge(v.sem[v.last], v.own())
        v.eng.tensor_tensor(b.A_T[:, n % 4], v.bank(), b.A_SN, ALU.mult).then_inc(v.sem["free_d"], v.up("free_d"))
        v.eng.wait_ge(v.sem[v.last], v.own())
        v.eng.tensor_tensor(t, t, b.A_C, ALU.mult).then_inc(v.sem["dve_step"], v.up("dve_step"))
        v.eng.wait_ge(v.sem[v.last], v.own())
        v.eng.tensor_tensor(t, t, b.A_T[:, n % 4], ALU.add)\
            .then_inc(v.sem["qk_ready" if n == 11 else "dve_step"], v.up("qk_ready" if n == 11 else "dve_step"))

    def ada(s):
        if s and s % 2 == 0:
            dve_ada_turn(v, ADA_FIRST + s // 2 - 1)
        dve_ada(v, s % 2 == 0, False)

    dve_attention(v, columns(units_1(b), b), extra=ada, late=lambda s: dve_ada(v, False, s % 2 == 1))
    dve_ada_turn(v, ADA_FIRST + 7)
    v.eng.wait_ge(v.sem[v.last], v.own())
    v.eng.scalar_tensor_tensor(b.col[:, 24:32], b.mod[:, 32:40], 1.0, b.pcs("norm_ffn_pre", KD), ALU.add, ALU.mult)\
        .then_inc(v.sem["dve_step"], v.up("dve_step"))
    v.eng.wait_ge(v.sem[v.last], v.own())
    v.eng.tensor_tensor(b.mod[:, 16:24], b.mod[:, 16:24], b.pcs("norm_mix_post", KD), ALU.mult)\
        .then_inc(v.sem["dve_step"], v.up("dve_step"))
    v.eng.wait_ge(v.sem[v.last], v.own())
    v.eng.tensor_tensor(b.mod[:, 40:48], b.mod[:, 40:48], b.pcs("norm_ffn_post", KD), ALU.mult)\
        .then_inc(v.sem["dve_step"], v.up("dve_step"))
    for f in range(2):
        v.eng.wait_ge(v.sem["o_plain"], v.due("o_plain"))
        v.eng.wait_ge(v.sem["act_hi"], v.due("act_hi"))
        v.eng.wait_ge(v.sem[v.last], v.own())
        v.eng.tensor_tensor(b.s_lo[:, 2 + f], b.A_T[:, f], b.s_hi[:, 2 + f].bitcast(F32), ALU.subtract)\
            .then_inc(v.sem["act_lo"], v.up("act_lo"))
    v.eng.wait_ge(v.sem[v.last], v.own())
    eng.memset(b.R_U[:, :, 0:1], 0.0).then_inc(v.sem["rwkv_clear"], v.up("rwkv_clear"))
    dve_shift(v, 0, b.R_K, 24)
    dve_shift(v, 1, b.R_V, 25)
    for n, src in enumerate((b.R_K, b.R_V)):
        v.eng.wait_ge(v.sem["lora_act"], v.due("lora_act"))
        v.eng.wait_ge(v.sem["act_hi"], v.due("act_hi"))
        v.eng.wait_ge(v.sem[v.last], v.own())
        v.eng.tensor_tensor(b.s_lo[:, n], src, b.s_hi[:, n].bitcast(F32), ALU.subtract)\
            .then_inc(v.sem["act_lo"], v.up("act_lo"))
    for step in range(1, 10):
        dve_rwkv_input(v, 0, step)
    for j in range(KD):
        dve_rwkv(v, j)
    dve_rwkv_centered(v)
    dve_rwkv_normed(v, KD - 1)
    dve_rwkv_mixed(v, KD - 1)
    dve_rwkv_low(v, KD - 1)
    v.eng.wait_ge(v.sem[v.last], v.own())
    v.eng.sem_inc(v.sem["mix_clear"], v.up("mix_clear"))
    for n in range(KD):
        v.eng.wait_ge(v.sem["gate_ready"], v.due("gate_ready"))
        sg = [b.G_SG[:, 2 * (n % 2) + part] for part in range(2)]
        v.eng.wait_ge(v.sem["full_d"], v.due("full_d"))
        v.eng.wait_ge(v.sem[v.last], v.own())
        v.eng.tensor_tensor(b.F_T, v.bank(), sg[0], ALU.mult).then_inc(v.sem["free_d"], v.up("free_d"))
        v.eng.wait_ge(v.sem["full_d"], v.due("full_d"))
        v.eng.wait_ge(v.sem[v.last], v.own())
        v.eng.tensor_tensor(b.G_M[:, n], v.bank(), sg[1], ALU.mult).then_inc(v.sem["free_d"], v.up("free_d"))
        v.eng.wait_ge(v.sem[v.last], v.own())
        v.eng.tensor_tensor(b.G_M[:, n], b.G_M[:, n], b.F_T, ALU.add).then_inc(v.sem["merged"], v.up("merged"))
    for n in range(KD):
        v.eng.wait_ge(v.sem["act_hi"], v.due("act_hi"))
        v.eng.wait_ge(v.sem[v.last], v.own())
        v.eng.tensor_tensor(b.h_lo[:, n], b.G_M[:, n], b.h_hi[:, n].bitcast(F32), ALU.subtract)\
            .then_inc(v.sem["act_lo"], v.up("act_lo"))
    for n in range(KD):
        v.eng.wait_ge(v.sem["full_d"], v.due("full_d"))
        v.eng.wait_ge(v.sem[v.last], v.own())
        v.eng.tensor_copy(b.Y8[:, n], v.bank()).then_inc(v.sem["free_d"], v.up("free_d"))
        v.eng.wait_ge(v.sem[v.last], v.own())
        v.eng.sem_inc(v.sem["y_ready"], v.up("y_ready"))
    dve_norm_add(v, b.N1, lambda t: b.mod[:, 16 + t:17 + t])
    dve_norm_split(v, b.N1, KD, lambda t: b.x[:, t], gain(24), h, hl, bias=lambda t: b.mod[:, 24 + t:25 + t])

    def lows(g):
        for n in range(4):
            at = (4 * g + n) % 8
            v.eng.wait_ge(v.sem["hid_hi"], v.due("hid_hi"))
            v.eng.wait_ge(v.sem[v.last], v.own())
            v.eng.tensor_tensor(b.F_T, b.F_R[:, n], b.F_R[:, n], ALU.mult)\
                .then_inc(v.sem["dve_step"], v.up("dve_step"))
            v.eng.wait_ge(v.sem[v.last], v.own())
            v.eng.tensor_tensor(b.o_lo[:, at], b.F_T, b.o_hi[:, at].bitcast(F32), ALU.subtract)\
                .then_inc(v.sem["hid_lo"], v.up("hid_lo"))

    def downs(g):
        for n in range(KD):
            if g:
                v.eng.wait_ge(v.sem["full_d"], v.due("full_d"))
                v.eng.wait_ge(v.sem[v.last], v.own())
                v.eng.tensor_tensor(b.Y8[:, n], b.Y8[:, n], v.bank(), ALU.add)\
                    .then_inc(v.sem["free_d"], v.up("free_d"))
            else:
                v.eng.wait_ge(v.sem["full_d"], v.due("full_d"))
                v.eng.wait_ge(v.sem[v.last], v.own())
                v.eng.tensor_copy(b.Y8[:, n], v.bank()).then_inc(v.sem["free_d"], v.up("free_d"))
            if g == FF1 // P // 4 - 1:
                v.eng.wait_ge(v.sem[v.last], v.own())
                v.eng.sem_inc(v.sem["y_ready"], v.up("y_ready"))

    lows(0)
    for g in range(FF1 // P // 4 - 1):
        lows(g + 1)
        downs(g)
        if g < 6:
            dve_setup(v, g)
    downs(FF1 // P // 4 - 1)
    dve_norm_add(v, b.N1, lambda t: b.mod[:, 40 + t:41 + t])
    for l in range(LAYERS):
        dve_layer(v, l)


NLOAD = 6


def build(nc, ins, out, plan):
    blocks = len(plan) // TILES
    cols, ncols = param_columns()
    with ExitStack() as ctx:
        b = Buffers(nc, ctx, ncols, cols)
        sig = Signals(nc, ctx)
        for name in ([f"raw_loaded{s}" for s in range(RAW)]
                     + ["w_ready", "w_used", "w_high", "x_final", "stored", "loaded", "c_ready", "free_a", "free_d",
                        "full_a", "full_d"]):
            sig[name]
        block = ctx.enter_context(nc.Block())

        @block.sync
        def _(eng):
            w = ins["weights"]
            for s in range(RAW):
                eng.dma_start(b.raw[:, s], w[s]).then_inc(sig[f"raw_loaded{s}"], 16)
            with eng.Fori(1, blocks // RAW) as i:
                for s in range(RAW):
                    eng.wait_ge(sig["w_ready"], i * RAW + (s + 1 - RAW))
                    eng.dma_start(b.raw[:, s], w[i * RAW + s]).then_inc(sig[f"raw_loaded{s}"], 16)
            eng.wait_ge(sig["x_final"], 1)
            eng.dma_start(out.rearrange("(k p) t -> p k t", p=P), b.x[:, :, :]).then_inc(sig["stored"], 16)
            eng.wait_ge(sig["stored"], 16)

        @block.gpsimd
        def _(eng):
            def split(i, s, used):
                eng.wait_ge(sig[f"raw_loaded{s}"], i * 16 + 16)
                if used is not None:
                    eng.wait_ge(sig["w_used"], used)
                hi, lo = b.w_hi[:, s % SPLIT], b.w_lo[:, s % SPLIT]
                if used is not None:
                    eng.tensor_tensor(b.mark[:, 1:2], b.mark[:, 0:1], b.mark[:, 0:1], ALU.add)
                eng.tensor_scalar(hi, b.raw[:, s], 1.0, 0.0, ALU.mult, ALU.add).then_inc(sig["w_high"], 1)
                eng.wait_ge(sig["w_high"], i * RAW + s + 2)
                eng.tensor_tensor(lo, b.raw[:, s], hi.bitcast(F32), ALU.subtract).then_inc(sig["w_ready"], 1)

            eng.memset(b.mark[:, :], 0.0).then_inc(sig["w_high"], 1)
            eng.wait_ge(sig["w_high"], 1)
            for s in range(RAW):
                split(0, s, s - SPLIT + 1 if s >= SPLIT else None)
            with eng.Fori(1, blocks // RAW) as i:
                for s in range(RAW):
                    split(i, s, i * RAW + (s - SPLIT + 1))

        @block.tensor
        def _(eng):
            pe_program(eng, sig, b, plan)

        @block.scalar
        def _(eng):
            act_program(eng, sig, b, ins)

        @block.vector
        def _(eng):
            dve_program(eng, sig, b)


def pack_weights(inputs, plan):
    w = np.zeros((len(plan) // TILES, P, TILES, P), np.float32)
    for t, (_, pieces) in enumerate(plan):
        for name, layer, row, rows, col, cols, at_row, at_col in pieces:
            w[t // TILES, at_row:at_row + rows, t % TILES, at_col:at_col + cols] = \
                inputs[name][layer][row:row + rows, col:col + cols]
    return w.reshape(len(plan) // TILES, P, TILES * P)


def pack_params(inputs):
    cols, n = param_columns()
    p = np.zeros((P, n), np.float32)

    def put(at, v):
        v = np.asarray(v).reshape(-1)
        if v.size == HD:
            v = np.concatenate([v, v])
        if v.size < P:
            p[:v.size, at] = v
        else:
            p[:, at:at + v.size // P] = v.reshape(-1, P).T

    for key, at in cols.items():
        if isinstance(key, str):
            put(at, inputs[key] if key == "c" else inputs[key][0])
        elif key[0] == "win_sink_2":
            p[:, at:at + WH] = inputs[key[0]][key[1]][None, :]
        else:
            put(at, inputs[key[0]][key[1]])
    return p


def kernel(**inputs):
    import concourse.bacc as bacc
    from concourse.bass_utils import run_bass_kernel_spmd

    plan = weight_plan()
    inputs = {k: np.asarray(v) for k, v in inputs.items()}
    const, masks = constants()
    positions = inputs["positions"][0], inputs["positions_2"][0]
    arrays = {
        "weights": pack_weights(inputs, plan),
        "params": pack_params(inputs),
        "const": const,
        "masks": masks,
        "x": np.ascontiguousarray(inputs["x"][0].T),
        "pe": np.ascontiguousarray(inputs["p_2"][:, 0].transpose(0, 2, 1)),
        "pos_rows": np.ascontiguousarray(np.broadcast_to(positions[0], (P, T))),
        "pos_rows_2": np.ascontiguousarray(np.broadcast_to(positions[1], (P, T))),
        "pos_cols": np.ascontiguousarray(positions[1].reshape(NQ, P).T),
    }
    nc = bacc.Bacc("TRN2", target_bir_lowering=False, num_devices=1, dynamic_dma_scratch_size=1024)
    ins = {k: nc.dram_tensor(f"in_{k}", a.shape, mybir.dt.from_np(a.dtype), kind="ExternalInput").ap()
           for k, a in arrays.items()}
    out = nc.dram_tensor("out", (D, T), F32, kind="ExternalOutput").ap()
    build(nc, ins, out, plan)
    r = run_bass_kernel_spmd(nc, [{f"in_{k}": a for k, a in arrays.items()}], core_ids=[0])
    return np.ascontiguousarray(r.results[0]["out"].T)[None]
```
